# Optimizing a Trainium2 kernel written in Bass

```python
import math
import jax
import jax.numpy as jnp
from jax import lax
import numpy as np

D_MODEL = 1024
BATCH = 1
SEQ = 256
DEPTH = 1
DEC_BATCH = 8
DEC_SEQ = 8
PAST_LEN = 1024
PAGE_SIZE = 128

HEAD_DIM = 64
NSA_HEADS = D_MODEL // 128
NSA_KV_GROUPS = 2
NSA_REP = NSA_HEADS // NSA_KV_GROUPS
CMP_BLOCK = 32
CMP_STRIDE = 16
CMP_HIDDEN = 2 * HEAD_DIM
SEL_BLOCK = 64
N_SEL = 16
WINDOW = 512
DIFF_HEADS = D_MODEL // 256
DIFF_DV = 2 * HEAD_DIM
ROT_DIM = HEAD_DIM // 4
ROPE_THETA = 500000.0
N_EXPERTS = 32
TOP_K = 4
D_FF = D_MODEL
SWIGLU_LIMIT = 7.0
SWIGLU_ALPHA = 1.702
RMS_EPS = 1e-5
Q_BLOCK = 128
SEL_Q_BLOCK = 32
EXPERT_BLOCK = 128
FORCE_BONUS = 1e4
SCALE = HEAD_DIM ** -0.5
Q_NSA_W = NSA_HEADS * HEAD_DIM
KV_NSA_W = 2 * NSA_KV_GROUPS * HEAD_DIM
GATE_NSA_W = 3 * NSA_HEADS
Q_DIFF_W = DIFF_HEADS * 2 * HEAD_DIM
V_DIFF_W = DIFF_HEADS * DIFF_DV
IN_COLS = Q_NSA_W + 3 * KV_NSA_W + GATE_NSA_W + 2 * Q_DIFF_W + V_DIFF_W + 2 * D_MODEL

kernel_name = 'nsa_diffattn_gated_moe_step'

def rmsnorm(x, g):
    xf = x.astype(jnp.float32)
    y = xf * lax.rsqrt(jnp.mean(xf * xf, axis=-1, keepdims=True) + RMS_EPS)
    return (y * g.astype(jnp.float32)).astype(x.dtype)

def partial_rope(x, pos):
    half = ROT_DIM // 2
    inv = ROPE_THETA ** (-jnp.arange(half, dtype=jnp.float32) / half)
    ang = pos.astype(jnp.float32)[:, None] * inv[None, :]
    shape = (1, pos.shape[0]) + (1,) * (x.ndim - 3) + (half,)
    cos = jnp.cos(ang).reshape(shape)
    sin = jnp.sin(ang).reshape(shape)
    xf = x.astype(jnp.float32)
    x1 = xf[..., :half]
    x2 = xf[..., half:ROT_DIM]
    out = jnp.concatenate([x1 * cos - x2 * sin, x1 * sin + x2 * cos, xf[..., ROT_DIM:]], axis=-1)
    return out.astype(x.dtype)

def rope_kv(kv, pos):
    return jnp.stack([partial_rope(kv[:, :, 0], pos), kv[:, :, 1]], axis=2)

def masked_softmax(s, mask):
    s = jnp.where(mask, s.astype(jnp.float32), -jnp.inf)
    m = jnp.max(s, axis=-1, keepdims=True)
    m = jnp.where(jnp.isfinite(m), m, 0.0)
    e = jnp.exp(s - m)
    d = jnp.sum(e, axis=-1, keepdims=True)
    return e / jnp.where(d > 0, d, 1.0)

def gather_pages(pool, page_table):
    g = pool[page_table]
    return g.reshape((page_table.shape[0], page_table.shape[1] * pool.shape[1]) + pool.shape[2:])

def split_projection(xn, w_in):
    b, t, _ = xn.shape
    proj = jnp.einsum('btd,dc->btc', xn, w_in)
    sizes = (Q_NSA_W, KV_NSA_W, KV_NSA_W, KV_NSA_W, GATE_NSA_W, Q_DIFF_W, Q_DIFF_W, V_DIFF_W, D_MODEL, D_MODEL)
    cuts = [int(c) for c in np.cumsum(sizes)[:-1]]
    p = jnp.split(proj, cuts, axis=-1)
    q_nsa = p[0].reshape(b, t, NSA_KV_GROUPS, NSA_REP, HEAD_DIM)
    kv_cmp = p[1].reshape(b, t, 2, NSA_KV_GROUPS, HEAD_DIM)
    kv_sel = p[2].reshape(b, t, 2, NSA_KV_GROUPS, HEAD_DIM)
    kv_win = p[3].reshape(b, t, 2, NSA_KV_GROUPS, HEAD_DIM)
    g_nsa = jax.nn.sigmoid(p[4]).reshape(b, t, NSA_KV_GROUPS, NSA_REP, 3)
    q_diff = p[5].reshape(b, t, DIFF_HEADS, 2, HEAD_DIM)
    k_diff = p[6].reshape(b, t, DIFF_HEADS, 2, HEAD_DIM)
    v_diff = p[7].reshape(b, t, DIFF_HEADS, DIFF_DV)
    gate_nsa = jax.nn.sigmoid(p[8])
    gate_diff = jax.nn.sigmoid(p[9])
    return (q_nsa, kv_cmp, kv_sel, kv_win, g_nsa, q_diff, k_diff, v_diff, gate_nsa, gate_diff)

def compressed_attend(q, kv_all, pos, pe, w1, w2):
    b, tk = kv_all.shape[:2]
    n_cmp = (tk - CMP_BLOCK) // CMP_STRIDE + 1
    starts = jnp.arange(n_cmp) * CMP_STRIDE
    idx = starts[:, None] + jnp.arange(CMP_BLOCK)[None, :]
    blocks = kv_all[:, idx] + jnp.transpose(pe, (1, 0, 2))[:, :, None, :]
    flat = jnp.transpose(blocks, (0, 1, 3, 4, 2, 5)).reshape(b, n_cmp, 2, NSA_KV_GROUPS, CMP_BLOCK * HEAD_DIM)
    hid = jax.nn.gelu(jnp.einsum('bncgf,cfh->bncgh', flat, w1))
    comp = jnp.einsum('bncgh,chd->bncgd', hid, w2)
    k_c = comp[:, :, 0]
    v_c = comp[:, :, 1]
    ends = starts + CMP_BLOCK - 1
    s = jnp.einsum('btgrd,bngd->btgrn', q, k_c) * SCALE
    mask = (ends[None, :] <= pos[:, None])[None, :, None, None, :]
    p = masked_softmax(s, mask)
    o = jnp.einsum('btgrn,bngd->btgrd', p.astype(v_c.dtype), v_c)
    return o, p

def select_blocks(p_cmp, pos, tk):
    b, t, g, _, n_cmp = p_cmp.shape
    nb = (tk + SEL_BLOCK - 1) // SEL_BLOCK
    sub = SEL_BLOCK // CMP_STRIDE
    n_sub = nb * sub
    pg = jnp.pad(jnp.sum(p_cmp, axis=3), ((0, 0), (0, 0), (0, 0), (0, n_sub - n_cmp)))
    mass = pg
    for shift in range(1, CMP_BLOCK // CMP_STRIDE):
        mass = mass + jnp.pad(pg[..., :-shift], ((0, 0), (0, 0), (0, 0), (shift, 0)))
    imp = mass.reshape(b, t, g, nb, sub).sum(-1)
    j = jnp.arange(nb)[None, :]
    cur = (pos // SEL_BLOCK)[:, None]
    forced = ((j == 0) | (j == cur) | (j == cur - 1))[None, :, None, :]
    valid = (j * SEL_BLOCK <= pos[:, None])[None, :, None, :]
    score = jnp.where(valid, jnp.where(forced, imp + FORCE_BONUS, imp), -jnp.inf)
    _, idx = lax.top_k(score, min(N_SEL, nb))
    return idx

def selected_attend(q, kv_all, idx, pos):
    b, tk = kv_all.shape[:2]
    t = q.shape[1]
    nb = (tk + SEL_BLOCK - 1) // SEL_BLOCK
    n_top = idx.shape[-1]
    kv = jnp.pad(kv_all, ((0, 0), (0, nb * SEL_BLOCK - tk), (0, 0), (0, 0), (0, 0)))
    kv_blocks = jnp.transpose(kv.reshape(b, nb, SEL_BLOCK, 2, NSA_KV_GROUPS, HEAD_DIM), (0, 4, 1, 2, 3, 5))
    bi = jnp.arange(b)[:, None, None, None]
    gi = jnp.arange(NSA_KV_GROUPS)[None, None, :, None]
    qc = math.gcd(t, SEL_Q_BLOCK)
    nc = t // qc

    def chunk(args):
        q_c, idx_c, pos_c = args
        kvg = kv_blocks[bi, gi, idx_c]
        kpos = idx_c[..., None] * SEL_BLOCK + jnp.arange(SEL_BLOCK)
        s = jnp.einsum('bqgrd,bqgnld->bqgrnl', q_c, kvg[..., 0, :]) * SCALE
        s = s.reshape(b, qc, NSA_KV_GROUPS, NSA_REP, n_top * SEL_BLOCK)
        mask = (kpos <= pos_c[None, :, None, None, None]).reshape(b, qc, NSA_KV_GROUPS, 1, n_top * SEL_BLOCK)
        p = masked_softmax(s, mask).reshape(b, qc, NSA_KV_GROUPS, NSA_REP, n_top, SEL_BLOCK)
        return jnp.einsum('bqgrnl,bqgnld->bqgrd', p.astype(kvg.dtype), kvg[..., 1, :])

    q_c = q.reshape(b, nc, qc, NSA_KV_GROUPS, NSA_REP, HEAD_DIM).swapaxes(0, 1)
    idx_c = idx.reshape(b, nc, qc, NSA_KV_GROUPS, n_top).swapaxes(0, 1)
    pos_c = pos.reshape(nc, qc)
    o = lax.map(chunk, (q_c, idx_c, pos_c))
    return o.swapaxes(0, 1).reshape(b, t, NSA_KV_GROUPS, NSA_REP, HEAD_DIM)

def local_attend(q, kv, qp, kp):
    s = jnp.einsum('bqgrd,bkgd->bgrqk', q, kv[:, :, 0]) * SCALE
    kpr = kp[None, :]
    qpc = qp[:, None]
    mask = (kpr <= qpc) & (kpr > qpc - WINDOW) & (kpr >= 0)
    p = masked_softmax(s, mask)
    return jnp.einsum('bgrqk,bkgd->bqgrd', p.astype(kv.dtype), kv[:, :, 1])

def window_banded(q, kv, pos):
    b, t = q.shape[:2]
    qb = math.gcd(t, Q_BLOCK)
    nb = t // qb
    span = WINDOW + qb
    kv_pad = jnp.pad(kv, ((0, 0), (WINDOW, 0), (0, 0), (0, 0), (0, 0)))
    kpos = pos[0] - WINDOW + jnp.arange(WINDOW + t)
    idx = jnp.arange(nb)[:, None] * qb + jnp.arange(span)[None, :]
    out = jax.vmap(local_attend, in_axes=(1, 1, 0, 0), out_axes=1)(
        q.reshape(b, nb, qb, NSA_KV_GROUPS, NSA_REP, HEAD_DIM), kv_pad[:, idx], pos.reshape(nb, qb), kpos[idx])
    return out.reshape(b, t, NSA_KV_GROUPS, NSA_REP, HEAD_DIM)

def diff_attention(q, k, v, qp, kp, lam):
    b, t = q.shape[:2]
    qb = math.gcd(t, Q_BLOCK)
    nb = t // qb

    def block(args):
        q_b, qp_b = args
        s = jnp.einsum('bqhcd,bkhcd->bhcqk', q_b, k) * SCALE
        p = masked_softmax(s, kp[None, :] <= qp_b[:, None])
        p_diff = p[:, :, 0] - lam * p[:, :, 1]
        return jnp.einsum('bhqk,bkhe->bqhe', p_diff.astype(v.dtype), v)

    o = lax.map(block, (q.reshape(b, nb, qb, DIFF_HEADS, 2, HEAD_DIM).swapaxes(0, 1), qp.reshape(nb, qb)))
    return o.swapaxes(0, 1).reshape(b, t, DIFF_HEADS, DIFF_DV)

def moe_ffn(h, w_router, b_router, w_gate_up, b_gate_up, w_down, b_down):
    n, d = h.shape
    logits = (h @ w_router + b_router).astype(jnp.float32)
    top_val, top_idx = lax.top_k(logits, TOP_K)
    gates = jax.nn.softmax(top_val, axis=-1)
    n_assign = n * TOP_K
    flat_e = top_idx.reshape(-1)
    order = jnp.argsort(flat_e)
    sorted_e = flat_e[order]
    counts = jnp.bincount(flat_e, length=N_EXPERTS)
    padded = (counts + EXPERT_BLOCK - 1) // EXPERT_BLOCK * EXPERT_BLOCK
    pad_end = jnp.cumsum(padded)
    pad_start = pad_end - padded
    start = jnp.cumsum(counts) - counts
    dest = pad_start[sorted_e] + jnp.arange(n_assign) - start[sorted_e]
    n_blocks = (n_assign + N_EXPERTS * (EXPERT_BLOCK - 1) + EXPERT_BLOCK - 1) // EXPERT_BLOCK
    n_rows = n_blocks * EXPERT_BLOCK
    row_token = jnp.full((n_rows,), n, jnp.int32).at[dest].set((order // TOP_K).astype(jnp.int32))
    block_expert = jnp.minimum(jnp.searchsorted(pad_end, jnp.arange(n_blocks) * EXPERT_BLOCK, side='right'), N_EXPERTS - 1)
    h_ext = jnp.concatenate([h, jnp.zeros((1, d), h.dtype)], axis=0)
    xb = h_ext[row_token].reshape(n_blocks, EXPERT_BLOCK, d)

    def expert_block(args):
        x_e, e = args
        gu = x_e @ w_gate_up[e] + b_gate_up[e]
        gate = jnp.minimum(gu[:, :D_FF], SWIGLU_LIMIT)
        up = jnp.clip(gu[:, D_FF:], -SWIGLU_LIMIT, SWIGLU_LIMIT)
        act = (up + 1.0) * gate * jax.nn.sigmoid(SWIGLU_ALPHA * gate)
        return act @ w_down[e] + b_down[e]

    yb = lax.map(expert_block, (xb, block_expert)).reshape(n_rows, d)
    y_assign = jnp.zeros((n_assign, d), yb.dtype).at[order].set(yb[dest])
    return jnp.einsum('nk,nkd->nd', gates.astype(yb.dtype), y_assign.reshape(n, TOP_K, d))

def trunk_layer(x, pos, past, lambda_init, norm_mix, w_in, cmp_pe, w_cmp1, w_cmp2, diff_lambda, diff_subln,
                w_br_nsa, w_br_diff, w_out, norm_ffn, w_router, b_router, w_gate_up, b_gate_up, w_down, b_down):
    b, t, _ = x.shape
    xn = rmsnorm(x, norm_mix)
    (q_nsa, kv_cmp, kv_sel, kv_win, g_nsa, q_diff, k_diff, v_diff, gate_nsa, gate_diff) = split_projection(xn, w_in)
    q_rot = partial_rope(q_nsa, pos)
    kv_sel = rope_kv(kv_sel, pos)
    kv_win = rope_kv(kv_win, pos)
    q_diff = partial_rope(q_diff, pos)
    k_diff = partial_rope(k_diff, pos)
    win_buf = min(WINDOW, PAST_LEN)
    if past is None:
        cmp_all, sel_all, k_all, v_all = kv_cmp, kv_sel, k_diff, v_diff
        o_win = window_banded(q_rot, kv_win, pos)
        win_state = jnp.pad(kv_win, ((0, 0), (max(win_buf - t, 0), 0), (0, 0), (0, 0), (0, 0)))[:, -win_buf:]
    else:
        past_cmp, past_sel, past_win, past_k, past_v = past
        cmp_all = jnp.concatenate([past_cmp, kv_cmp], axis=1)
        sel_all = jnp.concatenate([past_sel, kv_sel], axis=1)
        k_all = jnp.concatenate([past_k, k_diff], axis=1)
        v_all = jnp.concatenate([past_v, v_diff], axis=1)
        win_all = jnp.concatenate([past_win, kv_win], axis=1)
        wpos = pos[0] - past_win.shape[1] + jnp.arange(win_all.shape[1])
        o_win = local_attend(q_rot, win_all, pos, wpos)
        win_state = win_all[:, -past_win.shape[1]:]
    kpos = jnp.arange(k_all.shape[1])
    o_cmp, p_cmp = compressed_attend(q_nsa, cmp_all, pos, cmp_pe, w_cmp1, w_cmp2)
    sel_idx = select_blocks(p_cmp, pos, sel_all.shape[1])
    o_sel = selected_attend(q_rot, sel_all, sel_idx, pos)
    o_nsa = g_nsa[..., 0:1] * o_cmp + g_nsa[..., 1:2] * o_sel + g_nsa[..., 2:3] * o_win
    lf = diff_lambda.astype(jnp.float32)
    lam = jnp.exp(jnp.sum(lf[0] * lf[1])) - jnp.exp(jnp.sum(lf[2] * lf[3])) + lambda_init
    o_diff = diff_attention(q_diff, k_all, v_all, pos, kpos, lam)
    o_diff = rmsnorm(o_diff, diff_subln) * (1.0 - lambda_init)
    y_nsa = jnp.einsum('btf,fd->btd', o_nsa.reshape(b, t, Q_NSA_W), w_br_nsa)
    y_diff = jnp.einsum('btf,fd->btd', o_diff.reshape(b, t, V_DIFF_W), w_br_diff)
    x = x + jnp.einsum('btd,de->bte', gate_nsa * y_nsa + gate_diff * y_diff, w_out)
    h = rmsnorm(x, norm_ffn).reshape(b * t, D_MODEL)
    x = x + moe_ffn(h, w_router, b_router, w_gate_up, b_gate_up, w_down, b_down).reshape(b, t, D_MODEL)
    return x, (kv_cmp, kv_sel, win_state, k_diff, v_diff)

def setup_inputs(seed: int = 0) -> dict:
    key = jax.random.key(seed)
    ks = jax.random.split(key, 26)
    n_pages = PAST_LEN // PAGE_SIZE
    n_pool = (5 * DEC_BATCH * n_pages + 3) // 4
    win_buf = min(WINDOW, PAST_LEN)

    def nrm(k, shape, scale=1.0):
        return jax.random.normal(k, shape, jnp.float32) * scale

    page_table = jax.random.permutation(ks[7], n_pool)[:DEC_BATCH * n_pages].reshape(DEC_BATCH, n_pages).astype(jnp.int32)
    return {
        'x_prompt': nrm(ks[0], (BATCH, SEQ, D_MODEL)),
        'x_sample': nrm(ks[1], (DEC_BATCH, DEC_SEQ, D_MODEL)),
        'cache_cmp_kv': nrm(ks[2], (DEPTH, n_pool, PAGE_SIZE, 2, NSA_KV_GROUPS, HEAD_DIM)),
        'cache_sel_kv': nrm(ks[3], (DEPTH, n_pool, PAGE_SIZE, 2, NSA_KV_GROUPS, HEAD_DIM)),
        'state_win_kv': nrm(ks[4], (DEPTH, DEC_BATCH, win_buf, 2, NSA_KV_GROUPS, HEAD_DIM)),
        'cache_diff_k': nrm(ks[5], (DEPTH, n_pool, PAGE_SIZE, DIFF_HEADS, 2, HEAD_DIM)),
        'cache_diff_v': nrm(ks[6], (DEPTH, n_pool, PAGE_SIZE, DIFF_HEADS, DIFF_DV)),
        'page_table': page_table,
        'norm_mix': 1.0 + nrm(ks[8], (DEPTH, D_MODEL), 0.02),
        'w_in': nrm(ks[9], (DEPTH, D_MODEL, IN_COLS), D_MODEL ** -0.5),
        'cmp_pe': nrm(ks[10], (DEPTH, 2, CMP_BLOCK, HEAD_DIM), 0.1),
        'w_cmp1': nrm(ks[11], (DEPTH, 2, CMP_BLOCK * HEAD_DIM, CMP_HIDDEN), (CMP_BLOCK * HEAD_DIM) ** -0.5),
        'w_cmp2': nrm(ks[12], (DEPTH, 2, CMP_HIDDEN, HEAD_DIM), CMP_HIDDEN ** -0.5),
        'diff_lambda': nrm(ks[13], (DEPTH, 4, HEAD_DIM), 0.1),
        'diff_subln': 1.0 + nrm(ks[14], (DEPTH, DIFF_DV), 0.02),
        'w_br_nsa': nrm(ks[15], (DEPTH, Q_NSA_W, D_MODEL), Q_NSA_W ** -0.5),
        'w_br_diff': nrm(ks[16], (DEPTH, V_DIFF_W, D_MODEL), V_DIFF_W ** -0.5),
        'w_out': nrm(ks[17], (DEPTH, D_MODEL, D_MODEL), D_MODEL ** -0.5),
        'norm_ffn': 1.0 + nrm(ks[18], (DEPTH, D_MODEL), 0.02),
        'w_router': nrm(ks[19], (DEPTH, D_MODEL, N_EXPERTS), D_MODEL ** -0.5),
        'b_router': nrm(ks[20], (DEPTH, N_EXPERTS), 0.01),
        'w_gate_up': nrm(ks[21], (DEPTH, N_EXPERTS, D_MODEL, 2 * D_FF), D_MODEL ** -0.5),
        'b_gate_up': nrm(ks[22], (DEPTH, N_EXPERTS, 2 * D_FF), 0.01),
        'w_down': nrm(ks[23], (DEPTH, N_EXPERTS, D_FF, D_MODEL), D_FF ** -0.5),
        'b_down': nrm(ks[24], (DEPTH, N_EXPERTS, D_MODEL), 0.01),
        'norm_final': 1.0 + nrm(ks[25], (D_MODEL,), 0.02),
    }

def reference(x_prompt, x_sample, cache_cmp_kv, cache_sel_kv, state_win_kv, cache_diff_k, cache_diff_v, page_table,
              norm_mix, w_in, cmp_pe, w_cmp1, w_cmp2, diff_lambda, diff_subln, w_br_nsa, w_br_diff, w_out,
              norm_ffn, w_router, b_router, w_gate_up, b_gate_up, w_down, b_down, norm_final):
    past_len = page_table.shape[1] * cache_cmp_kv.shape[2]
    pos_p = jnp.arange(x_prompt.shape[1], dtype=jnp.int32)
    pos_s = past_len + jnp.arange(x_sample.shape[1], dtype=jnp.int32)
    xp, xs = x_prompt, x_sample
    st_p, st_s = [], []
    for l in range(DEPTH):
        lambda_init = 0.8 - 0.6 * math.exp(-0.3 * l)
        weights = (norm_mix[l], w_in[l], cmp_pe[l], w_cmp1[l], w_cmp2[l], diff_lambda[l], diff_subln[l],
                   w_br_nsa[l], w_br_diff[l], w_out[l], norm_ffn[l], w_router[l], b_router[l],
                   w_gate_up[l], b_gate_up[l], w_down[l], b_down[l])
        past = (gather_pages(cache_cmp_kv[l], page_table), gather_pages(cache_sel_kv[l], page_table), state_win_kv[l],
                gather_pages(cache_diff_k[l], page_table), gather_pages(cache_diff_v[l], page_table))
        xp, sp = trunk_layer(xp, pos_p, None, lambda_init, *weights)
        xs, ss = trunk_layer(xs, pos_s, past, lambda_init, *weights)
        st_p.append(sp)
        st_s.append(ss)
    y_prompt = rmsnorm(xp, norm_final)
    y_sample = rmsnorm(xs, norm_final)
    new_cmp_kv_prompt = jnp.stack([s[0] for s in st_p])
    new_cmp_kv_sample = jnp.stack([s[0] for s in st_s])
    new_sel_kv_prompt = jnp.stack([s[1] for s in st_p])
    new_sel_kv_sample = jnp.stack([s[1] for s in st_s])
    new_win_kv_prompt = jnp.stack([s[2] for s in st_p])
    new_win_kv_sample = jnp.stack([s[2] for s in st_s])
    new_diff_k_prompt = jnp.stack([s[3] for s in st_p])
    new_diff_k_sample = jnp.stack([s[3] for s in st_s])
    new_diff_v_prompt = jnp.stack([s[4] for s in st_p])
    new_diff_v_sample = jnp.stack([s[4] for s in st_s])
    return (y_prompt, y_sample, new_cmp_kv_prompt, new_cmp_kv_sample, new_sel_kv_prompt, new_sel_kv_sample,
            new_win_kv_prompt, new_win_kv_sample, new_diff_k_prompt, new_diff_k_sample, new_diff_v_prompt, new_diff_v_sample)


_drawn_inputs = setup_inputs


def setup_inputs(seed=0):
    import zlib

    import numpy as np

    out = dict(_drawn_inputs(seed))
    spreads = {}
    factors = {'b_gate_up': 8.0, 'b_down': 8.0, 'norm_final': 2.789}
    for name, (base, spread) in spreads.items():
        noise = np.random.default_rng([zlib.crc32(name.encode()), seed]).standard_normal(out[name].shape)
        drawn = base * np.exp(spread * noise) if base else spread * noise
        out[name] = jnp.asarray(drawn.astype(out[name].dtype))
    for name, factor in factors.items():
        out[name] = (out[name] * factor).astype(out[name].dtype)
    return out
```

```python
import numpy as np
import concourse.bass as bass
from concourse import mybir
from contextlib import ExitStack

F32 = mybir.dt.float32
BF16 = mybir.dt.bfloat16
I32 = mybir.dt.int32
U32 = mybir.dt.uint32
ALU = mybir.AluOpType
ACT = mybir.ActivationFunctionType
AX = mybir.AxisListType.X

D = 1024
KD = D // 128
SEQ = 256
NB, NT = 8, 8
NS = NB * NT
NTOK = SEQ + NS
ROWS = (128, 128, NS)
PAST, PAGE = 1024, 128
NPAGE = PAST // PAGE
NPOOL = (5 * NB * NPAGE + 3) // 4
WIN = 512
HD = 64
SCALE = HD ** -0.5
EPS = 1e-5
CB, CS = 32, 16
NCP = (SEQ - CB) // CS + 1
NCC = (PAST + NT - CB) // CS + 1
SB = 64
NE, TOPK, DFF = 32, 4, 1024
LIM, ALPHA = 7.0, 1.702
LAMBDA0 = 0.8 - 0.6 * 1.0
NEG = -1e30
THETA = 500000.0

CHUNKS = ((0, 512), (512, 512), (1024, 280), (1304, 512), (1816, 512), (2328, 512),
          (2840, 512), (3352, 512), (3864, 512), (4376, 512))
P_CMP, P_SEL, P_WIN, P_GN, P_KD, P_VD, PW = 0, 256, 512, 768, 792, 1304, 1816

BS = 64
NBLK_OVER = 20
NBLK = NE + NBLK_OVER


def shape_constants():
    f = np.float32
    p = np.arange(128)
    tok = np.stack([p, 128 + p, PAST + p % NT])
    half = HD // 8
    inv = (f(THETA) ** (-np.arange(half, dtype=f) / f(half))).astype(f)
    ang = tok.astype(f)[:, :, None] * inv
    cos, sin = np.cos(ang).astype(f), np.sin(ang).astype(f)
    a = {}
    a["ident"] = np.eye(128)
    k = np.arange(SEQ)
    a["causal"] = np.where(k[None, None] <= tok[:2, :, None], 0, NEG).transpose(1, 0, 2).reshape(128, -1)
    ends = np.arange(NCP) * CS + CB - 1
    a["cmpm"] = np.where(ends[None, None] <= tok[:2, :, None], 0, NEG).transpose(1, 0, 2).reshape(128, -1)
    a["cmpv"] = (tok[:2] >= CB - 1).T
    a["cos"] = cos.transpose(1, 0, 2).reshape(128, -1)
    a["sin"] = sin.transpose(1, 0, 2).reshape(128, -1)
    kb, kt = np.arange(NS) // NT, np.arange(NS) % NT
    t = p % NT
    nsa = np.full((128, NB // 2, NS), NEG)
    for i in range(NB // 2):
        b = 2 * i + p // 64
        nsa[:, i] = np.where((kb[None] == b[:, None]) & (kt[None] <= t[:, None]), 0, NEG)
    a["newn"] = nsa.reshape(128, -1)
    dif = np.full((128, NB, NS), NEG)
    for b in range(NB):
        dif[:, b] = np.where((kb[None] == b) & (kt[None] <= t[:, None]), 0, NEG)
    a["newd"] = dif.reshape(128, -1)
    a["oldw"] = np.where(np.arange(NT)[None] > t[:, None], 0, NEG)
    a["rsum"] = (p[:, None] // 32 == p[None] // 32) & (t[:, None] == t[None])
    row, col = p[:, None], p[None]
    own = (row // 32 == col // 32) & (col % 32 < NT)
    a["c0"] = own & (row % 32 == col % 32)
    a["c1"] = own & (row % 32 == col % 32 + NT)
    a["blk"] = np.tile(np.arange(1, PAST // SB - 1), (128, 1))
    d = {}
    d["lower"] = row < col
    d["ones"] = np.ones((128, 128))
    d["before"] = np.where((row < col) & (row < NE), 1, 0)[:, :NE]
    d["expert"] = np.tile(np.arange(NE), (128, 1))
    d["over"] = np.tile(np.arange(NBLK_OVER), (128, 1))
    d["pairs"] = np.tile(2 * np.arange(NBLK_OVER // 2), (128, 1))
    d["pmod"] = (p % NE)[:, None]
    d["tokid"] = np.stack([p, 128 + p, SEQ + p], 1)
    out = []
    for group in (a, d):
        at, where = 0, {}
        for name, v in group.items():
            where[name] = (at, v.shape[1])
            at += v.shape[1]
        out += [np.ascontiguousarray(np.concatenate([np.asarray(v, f) for v in group.values()], 1)), where]
    return out


class Steps:

    def __init__(self, eng, own):
        self.eng, self.default, self.n, self.base, self.last = eng, own, {}, {}, None

    def __call__(self, ins, sem=None):
        sem = sem or self.default
        self.n[sem.name] = self.n.get(sem.name, 0) + 1
        ins.then_inc(sem, 1)
        self.last = (sem, self.n[sem.name])

    def own(self):
        sem, n = self.last
        self.eng.wait_ge(sem, self.base.get(sem.name, 0) + n)

    def enter(self, i, per):
        self.start, self.per = dict(self.n), per
        self.base = {s: i * k for s, k in per.items()}

    def leave(self, trips):
        for s in set(self.n) | set(self.per):
            k = self.per.get(s, 0)
            got = self.n.get(s, 0) - self.start.get(s, 0)
            assert got == k, (s, got, k, {q: self.n[q] - self.start.get(q, 0) for q in self.n})
            self.n[s] = self.start.get(s, 0) + (trips * k if trips else 0)
        self.base, self.last = {}, None


def build(nc, io, const_a, at_a, const_b, at_b):
    ctx = ExitStack()
    with ctx:
        sem = lambda name: ctx.enter_context(nc.semaphore(name))
        arena = ctx.enter_context(nc.sbuf_tensor("arena", [128, 53200], F32))
        PS = ctx.enter_context(nc.psum_tensor("PS", [128, 8 * 512], F32))

        def at(off, *dims):
            n = int(np.prod(dims))
            v = arena[:, off:off + n]
            if len(dims) == 2:
                return v.rearrange("p (a b) -> p a b", b=dims[1])
            if len(dims) == 3:
                return v.rearrange("p (a b c) -> p a b c", b=dims[1], c=dims[2])
            if len(dims) == 4:
                return v.rearrange("p (a b c d) -> p a b c d", b=dims[1], c=dims[2], d=dims[3])
            return v

        def bank(k, n=512, off=0):
            return PS[:, 512 * k + off:512 * k + off + n]

        RING = 24576
        wslot = [at(4096 * s, KD, 512) for s in range(4)]
        sel_raw = at(0, 2, NPAGE, 256)
        win_raw = at(4096, 2, WIN // PAGE, 256)
        dv_raw = at(6144, NPAGE, 512)
        w1 = at(10240, 2, CB, 128)
        xin = at(18432, 3, D)
        cmpT = at(18432, 2, 2, PAST)
        kdT = at(18432, 4, PAST)
        xnT = at(22528, KD, NTOK)
        ropet = [at(25088 + 384 * k, 384) for k in range(4)]
        ebuf = at(22528, 2048)
        ptb = at(24576, 2048)
        qraw, qrot, qdif = (at(26624 + 1536 * k, 3, 512) for k in range(3))
        ons, ods = at(26624, 2, 512), at(27648, 2, 4, 128)
        pvt = at(28672, 512)
        cmp_raw = at(26624, NPAGE, 256)
        dk_raw = at(28672, 4, 512)
        qTraw, qTrot, qTd = (at(31232 + 1024 * k, 4, SEQ) for k in range(3))
        winT, selT = at(31232, 2, WIN), at(32256, 2, PAST)
        proj = at(34304, 3, PW)
        onT, odT = at(39752, 4, NTOK), at(41032, 4, NTOK)
        cst = at(42312, const_a.shape[1])
        o = 42312 + const_a.shape[1]

        def alloc(*dims):
            nonlocal o
            o += int(np.prod(dims))
            assert o <= 53200, o
            return at(o - int(np.prod(dims)), *dims)

        cmat = alloc(128)
        bd_raw, bd_rot, bd_dif = alloc(NB, 64), alloc(NB, 64), alloc(NB, 128)
        cur_raw, cur_rot, cur_dif = alloc(2, 64), alloc(2, 64), alloc(2, 128)
        ksT, kwT, kdnT = alloc(NTOK), alloc(NTOK), alloc(4, NTOK)
        hid = alloc(2, 2, 126)
        kcT, vc = alloc(2, NCC), alloc(2, 128)
        pcT, w2 = alloc(2, SEQ), alloc(2, 64)
        gmix, sg, hb, peT = alloc(KD), alloc(1), alloc(2), alloc(64)
        ssq, lam, lv = alloc(8), alloc(8), alloc(4)
        gates, gS = alloc(3, 24), alloc(NB // 2, 3)
        mx, nmx, sm, cf = alloc(2, 4), alloc(2, 4), alloc(4, 4), alloc(2, 4)
        dl, peraw = alloc(256), alloc(64)
        osm, onrm, odn = alloc(128), alloc(128), alloc(2, 128)
        pgs, mass, imp, dropm = alloc(NCC + 1), alloc(14, 4), alloc(14), alloc(14)
        smx = alloc(8)
        zero = alloc(256)
        ptab = alloc(NB * NPAGE)[0:1, :].bitcast(I32)

        def C(name, *dims):
            off, n = at_a[name]
            return at(42312 + off, *(dims or (n,)))

        ident = C("ident")

        xn_dram = nc.dram_tensor("xn_scratch", [128, KD * NTOK], F32, kind="Internal").ap()
        gate_dram = nc.dram_tensor("gate_scratch", [NS, 24], F32, kind="Internal").ap()
        h_dram = nc.dram_tensor("h_scratch", [NTOK, D], F32, kind="Internal").ap()
        tab_dram = nc.dram_tensor("slot_scratch", [NBLK * BS, 1], F32, kind="Internal").ap()
        y_dram = nc.dram_tensor("y_scratch", [NBLK * BS, D], F32, kind="Internal").ap()

        w_in = io["w_in"][0].rearrange("(k p) n -> p k n", p=128)
        x_rows = [io["x_prompt"][0, 0:128], io["x_prompt"][0, 128:256],
                  io["x_sample"].rearrange("b t d -> (b t) d")]

        loaded = {}

        def load(eng, name, dst, src, **kw):
            if name not in loaded:
                loaded[name] = [sem("load_" + name), 0]
            loaded[name][1] += 16
            eng.dma_start(dst, src, **kw).then_inc(loaded[name][0], 16)

        def arrived(eng, name):
            eng.wait_ge(loaded[name][0], loaded[name][1])

        stored = sem("stored")
        n_stored = 0
        w_arrived = [sem(f"w_arrived{s}") for s in range(4)]
        tp_full = sem("tp_full")
        tp_out = [sem("tp_out_act"), sem("tp_out_dve")]
        pj_full = sem("pj_full")
        pj_out = [sem("pj_out_act"), sem("pj_out_dve")]
        var_ready, root_ready = sem("var_ready"), sem("root_ready")
        act_own, dve_own, pool_own = sem("act_own"), sem("dve_own"), sem("pool_own")
        squares = sem("squares")
        xn_stored = sem("xn_stored")
        xn_ready = sem("xn_ready")
        zeroed = sem("zeroed")
        roped = sem("roped")
        gates_ready = sem("gates_ready")
        lam_sums, lam_exp, lam_done = sem("lam_sums"), sem("lam_exp"), sem("lam_done")
        hb_full, hb_out = sem("hb_full"), sem("hb_out")
        ph_full, ph_out, pkv_full, pkv_out = (sem(n) for n in ("ph_full", "ph_out", "pkv_full", "pkv_out"))
        s_full, s_read, nmx_ready, e_ready = (sem(n) for n in ("s_full", "s_read", "nmx_ready", "e_ready"))
        pv_full, pv_read = sem("pv_full"), sem("pv_read")
        od_ready = sem("od_ready")

        CHUNK_SLOT = (0, 1, 2, 3, 0, 1, 0, 1, 2, 3)
        CHUNK_USE = (1, 1, 1, 1, 2, 2, 3, 3, 2, 2)
        PAIRS = tuple((2 * q, 2 * q + 1) for q in range(5))

        def proj_bank(q, slot):
            return (2, 3, 5, 6, 4 if q % 2 == 0 else 7)[slot]

        UNITS = [(kind, t, g) for t in range(2) for kind in ("sel", "win", "cmp", "dif") for g in range(2)]

        def unit_keys(u):
            kind, t, _ = UNITS[u]
            return NCP if kind == "cmp" else 128 * (t + 1)

        def unit_groups(u):
            kind, t, _ = UNITS[u]
            return 1 if kind == "cmp" else t + 1

        G_XN = 0
        G_PE = 6
        G_QK = 7
        G_UNIT = [G_QK + 14 + sum(unit_groups(v) for v in range(u)) for u in range(len(UNITS) + 1)]
        G_OUT = G_UNIT[-1]
        G_END = G_OUT + 4
        qk_groups = [(t, what) for t in range(3) for what in ("raw", "rot", "dif", "kd", "kc")]
        qk_groups.remove((2, "kc"))
        qk_groups.append((2, "kc"))
        assert len(qk_groups) == 15
        G_UNIT = [g + 1 for g in G_UNIT]
        G_OUT += 1
        G_END += 1

        def out_done(eng, n, sems=tp_out):
            eng.wait_ge(sems[0], n // 2 + 1)
            if n >= 1:
                eng.wait_ge(sems[1], (n + 1) // 2)

        def pe_projection(pe, pairs, first, xnT=xnT):
            for n, (j0, j1) in enumerate(pairs):
                q = first + n
                for s, j in enumerate((j0, j1)):
                    w, slot = CHUNKS[j][1], CHUNK_SLOT[j]
                    pe.wait_ge(w_arrived[slot], 16 * CHUNK_USE[j])
                    for t in range(2):
                        if n >= 1:
                            pe.wait_ge(pj_out[t], 3 * (q - 1) + s + 1)
                        for k in range(KD):
                            last = nc.tensor.matmul(bank(proj_bank(q, 2 * s + t))[:, 0:w], xnT[:, k, 128 * t:128 * t + 128],
                                                    wslot[slot][:, k, 0:w], start=(k == 0), stop=(k == KD - 1))
                        last.then_inc(pj_full, 1)
                if n >= 2:
                    for e in range(2):
                        pe.wait_ge(pj_out[e], 3 * (q - 1))
                for k in range(KD):
                    for s, j in enumerate((j0, j1)):
                        w = CHUNKS[j][1]
                        last = nc.tensor.matmul(bank(proj_bank(q, 4))[64 * s:64 * s + 64, 0:w], xnT[:, k, 256:NTOK],
                                                wslot[CHUNK_SLOT[j]][:, k, 0:w], start=(k == 0), stop=(k == KD - 1))
                last.then_inc(pj_full, 1)

        PAIRS_OF_SEQ = NB // 2
        L_TP = 42
        place_in = [sem(f"place_in{k}") for k in range(8)]
        cmp_in = place_in[0:4]
        sel_in = place_in[4:8]
        dk_in = [sem(f"dk_in{k}") for k in range(4)]
        win_in = [sem(f"win_in{k}") for k in range(2)]
        dv_in = [sem(f"dv_in{k}") for k in range(2)]
        l_tp, l_out = sem("l_tp"), [sem("l_out_act"), sem("l_out_dve")]
        l_hid, l_gelu, l_kv, l_kv_out = sem("l_hid"), sem("l_gelu"), sem("l_kv"), sem("l_kv_out")
        l_cur = sem("l_cur")
        l_sc = sem("l_sc")
        l_nmx, l_exp = sem("l_nmx"), sem("l_exp")
        l_pn, l_grp = sem("l_pn"), sem("l_grp")
        l_pv, l_pv_out = sem("l_pv"), sem("l_pv_out")
        l_on, l_join, l_osq, l_sq, l_var, l_root, l_odn = (sem(n) for n in ("l_on", "l_join", "l_osq", "l_sq", "l_var", "l_root", "l_odn"))
        l_act, l_dve = sem("l_act"), sem("l_dve")

        SELW, WINW = PAST + NS, WIN + NS
        E_SEL, E_WIN, E_CMP = 0, SELW, SELW + WINW
        e_sel, e_win, e_cmp = ebuf[:, 0:SELW], ebuf[:, E_WIN:E_WIN + WINW], ebuf[:, E_CMP:E_CMP + NCC]
        s_sel, s_win = PS[:, 5 * 512:5 * 512 + SELW], PS[:, 3 * 512:3 * 512 + WINW]
        s_cmp = bank(7)[:, 128:128 + NCC]
        s_new = PS[:, 5 * 512 + PAST:5 * 512 + SELW]
        pv_nsa = bank(4)[:, 128:320].rearrange("p (b d) -> p b d", b=3)
        pv_dif = bank(4)[:, 320:448]
        joined = bank(2)[:, 0:128]
        ptl = ptb[:, 0:1920].rearrange("p (j r) -> p j r", r=128)
        J_WIN, J_NEW = 8, 12
        G_CMP, G_SEL, G_WIN, G_KD, G_P, G_O, G_PD, G_OD = 0, 8, 12, (14, 26), 22, 34, (35, 38), 41

        def l_out_done(eng, i, n):
            eng.wait_ge(l_out[0], i * (L_TP // 2) + n // 2 + 1)
            if n >= 1:
                eng.wait_ge(l_out[1], i * (L_TP // 2) + (n + 1) // 2)

        def page_of(eng, i, b, pg):
            return eng.value_load(ptab[0:1, bass.ds(i * (2 * NPAGE) + (b * NPAGE + pg), 1)], min_val=0, max_val=NPOOL - 1)

        def sync_attention(sp):
            flat = lambda name: io[name][0].rearrange("n p c g d -> n p (c g d)")
            cmp_d, sel_d, win_d = flat("cache_cmp_kv"), flat("cache_sel_kv"), flat("state_win_kv")
            arrived(sp, "small")
            sp.wait_ge(tp_full, G_END)
            with sp.Fori(0, PAIRS_OF_SEQ) as i:
                for b in range(2):
                    for k in range(4):
                        for h in range(2):
                            pg = page_of(sp, i, b, 2 * k + h)
                            if h == 0:
                                sp.wait_ge(l_tp, i * L_TP + (k + 1 if b else 0))
                            sp.dma_start(cmp_raw[:, 2 * k + h], cmp_d[bass.ds(pg, 1)].rearrange("a p n -> (a p) n")).then_inc(cmp_in[k], 16)
                    if b == 1:
                        for bb in range(2):
                            for k in range(2):
                                for h in range(4):
                                    pg = page_of(sp, i, bb, 4 * k + h)
                                    if bb + k + h == 0:
                                        sp.wait_ge(l_pv, i * 3)
                                    sp.dma_start(sel_raw[:, bb, 4 * k + h], sel_d[bass.ds(pg, 1)].rearrange("a p n -> (a p) n")).then_inc(sel_in[2 * bb + k], 16)
                        for bb in range(2):
                            sp.dma_start(win_raw[:, bb], win_d[bass.ds(2 * i + bb, 1)].rearrange("a (s p) n -> p (a s) n", p=128)).then_inc(win_in[bb], 16)
            sync_merge(sp)

        def pool_attention(pool, st):
            kd_d = io["cache_diff_k"][0].rearrange("n p h c d -> n p (h c d)")
            vd_d = io["cache_diff_v"][0].rearrange("n p h e -> n p (h e)")
            out_done(pool, G_QK + 14)
            arrived(pool, "small")
            pool.wait_ge(tp_full, G_END)
            with pool.Fori(0, PAIRS_OF_SEQ) as i:
                pool.wait_ge(l_sc, i * 3)
                for src, dst in ((bd_raw, cur_raw), (bd_rot, cur_rot), (bd_dif, cur_dif)):
                    nc.gpsimd.tensor_copy(dst, src[:, bass.ds(2 * i, 2), :]).then_inc(l_cur, 1)
                def values_in(b):
                    for p2 in range(NPAGE):
                        page = page_of(pool, i, b, p2)
                        if p2 == 0:
                            pool.wait_ge(l_pv, i * 3 + (2 if b else 0))
                        pool.dma_start(dv_raw[:, p2], vd_d[bass.ds(page, 1)].rearrange("a p n -> (a p) n")).then_inc(dv_in[p2 // 4], 16)

                for b in range(2):
                    for pg in range(NPAGE):
                        page = page_of(pool, i, b, pg)
                        before = (G_KD[b] + pg - 3) if pg >= 4 else (G_KD[0] + pg + 5 if b else 0)
                        pool.wait_ge(l_tp, i * L_TP + before)
                        pool.dma_start(dk_raw[:, pg % 4], kd_d[bass.ds(page, 1)].rearrange("a p n -> (a p) n")).then_inc(dk_in[pg % 4], 16)
                        if b == 0 and pg == 3:
                            values_in(0)
                values_in(1)
            pool_moe(pool, st)

        def pe_attention(pe):
            out_done(pe, G_END - 1)
            with pe.Fori(0, PAIRS_OF_SEQ) as i:
                def tp(n, items):
                    if n >= 2:
                        pe.wait_ge(l_out[n % 2], i * (L_TP // 2) + n // 2)
                    else:
                        pe.wait_ge(l_out[n % 2], i * (L_TP // 2))
                    for src, col in items:
                        r, c = src.shape[0], src.free_size()
                        last = nc.tensor.transpose(bank(n % 2)[0:c, col:col + r], src, ident[0:r, 0:r])
                    last.then_inc(l_tp, 1)

                for b in range(2):
                    for k in range(4):
                        pe.wait_ge(cmp_in[k], i * 64 + 32 * (b + 1))
                        tp(G_CMP + 4 * b + k, [(cmp_raw[:, 2 * k + h, 128 * c:128 * c + 128], 256 * h + 128 * c) for h in range(2) for c in range(2)])
                l_out_done(pe, i, 7)
                for c in range(2):
                    for l in range(CB):
                        for g in range(2):
                            last = nc.tensor.matmul(bank(2 + g)[:, 126 * c:126 * c + 126], w1[64 * g:64 * g + 64, c, l, :],
                                                    cmpT[64 * g:64 * g + 64, c, :, l:l + CS * (NCC - 1) + 1:CS],
                                                    start=(l == 0), stop=(l == CB - 1))
                last.then_inc(l_hid, 1)
                for b in range(2):
                    for k in range(2):
                        pe.wait_ge(sel_in[2 * b + k], (i + 1) * 64)
                        tp(G_SEL + 2 * b + k, [(sel_raw[:, b, 4 * k + h, 0:128], 128 * h) for h in range(4)])
                for b in range(2):
                    pe.wait_ge(win_in[b], (i + 1) * 16)
                    tp(G_WIN + b, [(win_raw[:, b, h, 0:128], 128 * h) for h in range(4)])
                pe.wait_ge(l_gelu, i + 1)
                for g in range(2):
                    nc.tensor.matmul(bank(2)[64 * g:64 * g + 64, 256:382], w2[:, 0, :], hid[:, 0, g, :], start=True, stop=True)
                for b in range(2):
                    for g in range(2):
                        last = nc.tensor.matmul(bank(3)[0:NCC, 256 + 128 * b + 64 * g:320 + 128 * b + 64 * g],
                                                hid[:, 1, g, NCC * b:NCC * b + NCC], w2[:, 1, :], start=True, stop=True)
                last.then_inc(l_kv, 1)
                pe.wait_ge(l_cur, (i + 1) * 3)
                l_out_done(pe, i, 13)
                pe.wait_ge(l_exp, i * 5)
                for k0, w in ((0, 512), (512, 512)):
                    for b in range(2):
                        nc.tensor.matmul(s_sel[64 * b:64 * b + 64, k0:k0 + w], cur_rot[:, b, :], selT[:, b, k0:k0 + w], start=True, stop=True)
                for b in range(2):
                    nc.tensor.matmul(s_sel[64 * b:64 * b + 64, PAST:SELW], cur_rot[:, b, :], ksT[:, SEQ:NTOK], start=True, stop=True)
                pe.wait_ge(l_kv_out, i + 1)
                for b in range(2):
                    nc.tensor.matmul(s_win[64 * b:64 * b + 64, 0:WIN], cur_rot[:, b, :], winT[:, b, :], start=True, stop=True)
                for b in range(2):
                    nc.tensor.matmul(s_win[64 * b:64 * b + 64, WIN:WINW], cur_rot[:, b, :], kwT[:, SEQ:NTOK], start=True, stop=True)
                for b in range(2):
                    last = nc.tensor.matmul(s_cmp[64 * b:64 * b + 64], cur_raw[:, b, :], kcT[:, b, :], start=True, stop=True)
                last.then_inc(l_sc, 1)

                def keys_t(b):
                    for pg in range(NPAGE):
                        pe.wait_ge(dk_in[pg % 4], i * 64 + 16 * (2 * b + pg // 4 + 1))
                        tp(G_KD[b] + pg, [(dk_raw[:, pg % 4, 128 * h:128 * h + 128], 128 * h) for h in range(4)])
                        if b == 0 and pg == 5:
                            pe.wait_ge(l_pn, i + 1)
                            nc.tensor.matmul(bank(2)[:, 0:NCC], C("rsum"), pn, start=True, stop=True).then_inc(l_grp, 1)

                keys_t(0)
                pe.wait_ge(l_exp, i * 5 + 3)
                for k in range(2):
                    tp(G_P + k, [(e_sel[:, 512 * k + 128 * j:512 * k + 128 * j + 128], 128 * j) for j in range(4)])
                tp(G_P + 2, [(e_win[:, 128 * j:128 * j + 128], 128 * j) for j in range(4)])
                tp(G_P + 3, [(ebuf[:, PAST:PAST + 128], 0), (e_win[:, WIN:WINW], 128), (pn, 256)])
                l_out_done(pe, i, G_P + 3)
                for br, n, j0 in ((1, NPAGE, 0), (2, WIN // PAGE, J_WIN), (0, 0, 0)):
                    raw = sel_raw if br == 1 else win_raw
                    for j in range(n + 1):
                        for b in range(2):
                            for g in range(2):
                                r0 = 64 * b + 32 * g
                                out = pv_nsa[r0:r0 + 32, br]
                                if j < n:
                                    last = nc.tensor.matmul(out, ptl[:, j0 + j, r0:r0 + 32], raw[:, b, j, 128 + 64 * g:192 + 64 * g],
                                                            start=(j == 0), stop=False)
                                elif br:
                                    base = (P_SEL if br == 1 else P_WIN) + 128 + 64 * g
                                    last = nc.tensor.matmul(out, ptl[0:NS, J_NEW + br - 1, r0:r0 + 32], proj[0:NS, 2, base:base + 64],
                                                            start=False, stop=True)
                                else:
                                    last = nc.tensor.matmul(out, ptl[0:NCC, J_NEW + 2, r0:r0 + 32], vc[0:NCC, b, 64 * g:64 * g + 64],
                                                            start=True, stop=True)
                last.then_inc(l_pv, 1)

                def dif_scores(b):
                    l_out_done(pe, i, G_KD[b] + 7)
                    pe.wait_ge(l_exp, i * 5 + 3 + b)
                    for k0 in (0, 512):
                        for h in range(4):
                            nc.tensor.matmul(s_sel[32 * h:32 * h + 32, k0:k0 + 512], cur_dif[:, b, 32 * h:32 * h + 32], kdT[:, h, k0:k0 + 512], start=True, stop=True)
                    for h in range(4):
                        last = nc.tensor.matmul(s_new[32 * h:32 * h + 32], cur_dif[:, b, 32 * h:32 * h + 32], kdnT[:, h, SEQ:NTOK], start=True, stop=True)
                    last.then_inc(l_sc, 1)

                def dif_values(b):
                    pe.wait_ge(l_exp, i * 5 + 4 + b)
                    for k in range(2):
                        tp(G_PD[b] + k, [(e_sel[:, 512 * k + 128 * j:512 * k + 128 * j + 128], 128 * j) for j in range(4)])
                    tp(G_PD[b] + 2, [(ebuf[:, PAST:PAST + 128], 0)])
                    l_out_done(pe, i, G_PD[b] + 2)
                    for k in range(2):
                        pe.wait_ge(dv_in[k], i * 128 + 64 * (b + 1))
                    if b == 1:
                        pe.wait_ge(l_pv_out, i * 3 + 2)
                    for j in range(NPAGE + 1):
                        for h in range(4):
                            out = pv_dif[32 * h:32 * h + 32]
                            if j < NPAGE:
                                nc.tensor.matmul(out, ptl[:, j, 32 * h:32 * h + 32], dv_raw[:, j, 128 * h:128 * h + 128], start=(j == 0), stop=False)
                            else:
                                last = nc.tensor.matmul(out, ptl[0:NS, J_NEW, 32 * h:32 * h + 32], proj[0:NS, 2, P_VD + 128 * h:P_VD + 128 * h + 128], start=False, stop=True)
                    last.then_inc(l_pv, 1)
                    pe.wait_ge(l_on, i * 2 + b + 1)
                    nc.tensor.matmul(joined, cmat, onrm, start=True, stop=True).then_inc(l_join, 1)

                dif_scores(0)
                keys_t(1)
                pe.wait_ge(l_pv_out, i * 3 + 1)
                tp(G_O, [(osm, 0)])
                dif_values(0)
                dif_scores(1)
                dif_values(1)
                pe.wait_ge(l_odn, i + 1)
                tp(G_OD, [(odn[:, b, :], 128 * b) for b in range(2)])
            pe_merge(pe)

        def l_evac(eng, st, i, n, which, copy):
            assert n % 2 == which
            eng.wait_ge(l_tp, i * L_TP + n + 1)
            src = bank(n % 2)
            s4 = src.rearrange("p (k n) -> p k n", k=4)
            if n < G_SEL:
                b, k = n // 4, n % 4
                st(copy(cmpT[:, :, b, 256 * k:256 * k + 256].rearrange("p c (h n) -> p h c n", h=2),
                        src.rearrange("p (h c n) -> p h c n", h=2, c=2)), l_out[which])
            elif n < G_WIN:
                st(copy(selT[:, (n - G_SEL) // 2, 512 * (n % 2):512 * (n % 2) + 512], src), l_out[which])
            elif n < G_KD[0]:
                st(copy(winT[:, n - G_WIN, :], src), l_out[which])
            elif n < G_P or G_KD[1] <= n < G_O:
                b = 0 if n < G_P else 1
                pg = n - G_KD[b]
                if pg < 2:
                    if b == 0:
                        eng.wait_ge(l_hid, i + 1)
                    else:
                        eng.wait_ge(l_sc, i * 3 + 2)
                st(copy(kdT[:, :, 128 * pg:128 * pg + 128], s4), l_out[which])
            elif n < G_P + 3:
                j = {0: 0, 1: 4, 2: J_WIN}[n - G_P]
                st(copy(ptl[:, j:j + 4, :], s4), l_out[which])
            elif n == G_P + 3:
                st(copy(ptl[0:NS, J_NEW:J_NEW + 2, :], s4[0:NS, 0:2]))
                st(copy(ptl[0:NCC, J_NEW + 2, :], s4[0:NCC, 2]), l_out[which])
            elif n == G_O:
                for par in range(2):
                    for b in range(2):
                        d = onT[64 * par:64 * par + 64, :, bass.ds(i * 16 + (SEQ + NT * b), NT)]
                        s = src[64 * par:64 * par + 64, 64 * b:64 * b + 64].rearrange("p (k r t) -> p k r t", r=2, t=NT)[:, :, par]
                        st(copy(d, s), l_out[which] if par and b else None)
            elif n == G_OD:
                for b in range(2):
                    d = odT[:, :, bass.ds(i * 16 + (SEQ + NT * b), NT)]
                    s = src[:, 128 * b:128 * b + 128].rearrange("p (h x) -> p h x", h=4)[:, :, 0:NT]
                    st(nc.vector.tensor_scalar(d, s, sg, None, ALU.mult), l_out[which] if b else None)
            else:
                k = (n - G_PD[0]) % 3
                if k < 2:
                    if k == 0 and n == G_PD[0]:
                        eng.wait_ge(l_pv, i * 3 + 1)
                    if k == 1 and n == G_PD[0] + 1:
                        eng.wait_ge(l_pv, i * 3 + 1)
                    if n >= G_PD[1]:
                        eng.wait_ge(l_pv, i * 3 + 2)
                    st(copy(ptl[:, 4 * k:4 * k + 4, :], s4), l_out[which])
                else:
                    eng.wait_ge(l_pv, i * 3 + (1 if n < G_PD[1] else 2))
                    st(copy(ptl[0:NS, J_NEW, :], src[0:NS, 0:128]), l_out[which])

        pn = alloc(NCC)
        ACT_PER_TURN = {"l_act": 6, "l_out_act": 21, "l_gelu": 1, "l_exp": 5, "l_sq": 2, "l_root": 1}
        DVE_PER_TURN = {"l_out_dve": 21, "l_dve": 33, "l_osq": 2, "l_kv_out": 1, "l_nmx": 5, "l_pn": 1, "l_pv_out": 3, "l_on": 2, "l_var": 1,
                        "l_odn": 1}

        def act_attention(act, st):
            copy = lambda d, s: nc.scalar.activation(d, s, ACT.Copy)
            before, st = st, Steps(act, l_act)
            with act.Fori(0, PAIRS_OF_SEQ) as i:
                st.enter(i, ACT_PER_TURN)
                ev = lambda *ns: [l_evac(act, st, i, n, 0, copy) for n in ns]

                def exp(k, out, src, sums):
                    act.wait_ge(l_nmx, i * 5 + k + 1)
                    st(nc.scalar.activation(out, src, ACT.Exp, bias=smx[:, k:k + 1], scale=SCALE, accum_out=sums), l_exp)

                ev(0, 2, 4, 6)
                act.wait_ge(l_hid, i + 1)
                for c in range(2):
                    for g in range(2):
                        ins = nc.scalar.activation(hid[:, c, g, :], bank(2 + g)[:, 126 * c:126 * c + 126], ACT.Gelu_apprx_tanh, bias=hb[:, c:c + 1])
                        st(ins, l_gelu if c and g else None)
                    if c == 0:
                        ev(8)
                ev(10, 12, 14, 16)
                exp(0, e_win, s_win, lsum[:, 0:1])
                exp(1, pn, s_cmp, lsum[:, 1:2])
                ev(18, 20)
                exp(2, e_sel, s_sel, lsum[:, 2:3])
                ev(22, 24, 26, 28)
                exp(3, e_sel, s_sel, lsum[:, 3:4])
                ev(30, 32, 34, 36)
                def square(b):
                    act.wait_ge(l_osq, i * 2 + b + 1)
                    st(nc.scalar.activation(sqj, osq[:, b], ACT.Square, accum_out=lsum[:, 5 + b:6 + b]), l_sq)
                square(0)
                exp(4, e_sel, s_sel, lsum[:, 4:5])
                ev(38, 40)
                st.own()
                square(1)
                act.wait_ge(l_var, i + 1)
                st(nc.scalar.activation(lvar, lvar, ACT.Sqrt), l_root)
            st.leave(PAIRS_OF_SEQ)
            act_merge(act, before)

        lsum, lvar, lcf, sqj, osq = alloc(8), alloc(2), alloc(8), alloc(128), alloc(2, 128)

        def dve_attention(dve, st):
            V = nc.vector
            before, st = st, Steps(dve, l_dve)
            arrived(dve, "gS")
            with dve.Fori(0, PAIRS_OF_SEQ) as i:
                st.enter(i, DVE_PER_TURN)
                ev = lambda *ns: [l_evac(dve, st, i, n, 1, V.tensor_copy) for n in ns]

                def negmax(k, s):
                    st.own()
                    st(V.reduce_max(lcf[:, k:k + 1], s, AX))
                    st.own()
                    st(V.tensor_scalar(smx[:, k:k + 1], lcf[:, k:k + 1], -SCALE, None, ALU.mult), l_nmx)

                if True:
                    dve.wait_ge(l_exp, i * 5)
                ev(1, 3, 5, 7, 9, 11, 13)
                dve.wait_ge(l_kv, i + 1)
                st(V.tensor_copy(kcT.rearrange("p b n -> p (b n)"), bank(2)[:, 256:382]))
                st(V.tensor_copy(vc[0:NCC].rearrange("p b n -> p (b n)"), bank(3)[0:NCC, 256:512]), l_kv_out)
                dve.wait_ge(l_sc, i * 3 + 1)
                st(V.tensor_tensor(s_win[:, 0:NT], s_win[:, 0:NT], C("oldw"), ALU.add))
                newn = C("newn", NB // 2, NS)[:, bass.ds(i, 1), :].rearrange("p a n -> p (a n)")
                st(V.tensor_tensor(s_win[:, WIN:WINW], s_win[:, WIN:WINW], newn, ALU.add))
                st(V.tensor_tensor(s_new, s_new, newn, ALU.add))
                negmax(0, s_win)
                negmax(1, s_cmp)
                ev(15, 17)
                dve.wait_ge(l_exp, i * 5 + 2)
                st(V.reciprocal(lcf[:, 1:2], lsum[:, 1:2]))
                st.own()
                st(V.tensor_scalar(pn, pn, lcf[:, 1:2], None, ALU.mult), l_pn)
                ev(19)
                dve.wait_ge(l_grp, i + 1)
                st(V.tensor_copy(pgs[:, 0:NCC], bank(2)[:, 0:NCC]))
                st.own()
                n14 = PAST // SB - 2
                st(V.tensor_tensor(mass, pgs[:, 4:4 + 4 * n14].rearrange("p (a b) -> p a b", b=4),
                                   pgs[:, 3:3 + 4 * n14].rearrange("p (a b) -> p a b", b=4), ALU.add))
                st.own()
                st(V.reduce_sum(imp, mass, AX))
                st.own()
                st(V.tensor_reduce(lcf[:, 5:6], imp, AX, ALU.min))
                st.own()
                st(V.scalar_tensor_tensor(imp, imp, lcf[:, 5:6], C("blk"), ALU.is_equal, ALU.mult))
                st.own()
                st(V.reduce_max(lcf[:, 6:7], imp, AX))
                st.own()
                st(V.tensor_scalar(dropm, C("blk"), lcf[:, 6:7], NEG, ALU.is_equal, ALU.mult))
                st.own()
                mid = s_sel[:, SB:SB + n14 * SB].rearrange("p (a b) -> p a b", b=SB)
                st(V.tensor_tensor(mid, mid, dropm.unsqueeze(2).to_broadcast([128, n14, SB]), ALU.add))
                negmax(2, s_sel)
                ev(21, 23, 25)
                dve.wait_ge(l_exp, i * 5 + 3)
                gi = gS[:, bass.ds(i, 1), :].rearrange("p a b -> p (a b)")
                st(V.reciprocal(lcf[:, 0:1], lsum[:, 0:1]))
                st(V.reciprocal(lcf[:, 2:3], lsum[:, 2:3]))
                st.own()
                st(V.tensor_copy(lgt, gi))
                st.own()
                st(V.tensor_tensor(lcf[:, 0:1], lcf[:, 0:1], lgt[:, 2:3], ALU.mult))
                st(V.tensor_tensor(lcf[:, 2:3], lcf[:, 2:3], lgt[:, 1:2], ALU.mult))
                dve.wait_ge(l_pv, i * 3 + 1)
                st.own()
                st(V.tensor_scalar(osm[:, 0:64], pv_nsa[:, 0], lgt[:, 0:1], None, ALU.mult))
                st.own()
                st(V.scalar_tensor_tensor(osm[:, 0:64], pv_nsa[:, 1], lcf[:, 2:3], osm[:, 0:64], ALU.mult, ALU.add))
                st.own()
                st(V.scalar_tensor_tensor(osm[:, 0:64], pv_nsa[:, 2], lcf[:, 0:1], osm[:, 0:64], ALU.mult, ALU.add))
                st.own()
                st(V.tensor_copy(osm[:, 64:128], osm[:, 0:64]), l_pv_out)

                def dif_mask(b):
                    dve.wait_ge(l_sc, i * 3 + 2 + b)
                    newd = C("newd", NB, NS)[:, bass.ds(2 * i + b, 1), :].rearrange("p a n -> p (a n)")
                    st(V.tensor_tensor(s_new, s_new, newd, ALU.add))
                    negmax(3 + b, s_sel)

                def dif_norm(b):
                    st(V.reciprocal(lcf[:, 3 + b:4 + b], lsum[:, 3 + b:4 + b]))
                    dve.wait_ge(l_pv, i * 3 + 2 + b)
                    st.own()
                    st(V.tensor_scalar(onrm, pv_dif, lcf[:, 3 + b:4 + b], None, ALU.mult), l_pv_out)
                    st(V.memset(lcf[:, 7:8], 0.0), l_on)
                    dve.wait_ge(l_join, i * 2 + b + 1)
                    st(V.tensor_copy(osq[:, b], joined), l_osq)

                dif_mask(0)
                ev(27, 29, 31, 33)
                dve.wait_ge(l_exp, i * 5 + 4)
                ev(35, 37)
                dif_norm(0)
                dif_mask(1)
                dve.wait_ge(l_exp, i * 5 + 5)
                ev(39)
                dif_norm(1)
                dve.wait_ge(l_sq, i * 2 + 2)
                st(V.tensor_scalar(lvar, lsum[:, 5:7], 1.0 / 128, EPS, ALU.mult, ALU.add), l_var)
                dve.wait_ge(l_root, i + 1)
                st(V.reciprocal(lvar, lvar))
                st.own()
                st(V.tensor_tensor(odn, osq, lvar.unsqueeze(2).to_broadcast([128, 2, 128]), ALU.mult), l_odn)
                ev(41)
            st.leave(PAIRS_OF_SEQ)
            dve_merge(dve, before)

        lgt = alloc(3)

        xnT5 = at(24576, KD, NTOK)
        gsig = at(27136, 3, 2 * D)
        x5 = at(33280, 3, D)
        mT = at(36352, KD, NTOK)
        bias16 = at(36352, 1536).bitcast(BF16)
        cstb = at(38912, const_b.shape[1])
        br_n, br_d = at(16384, 4, D), at(20480, 4, D)
        w_out = at(0, KD, D)
        hn, hT6 = at(27136, 3, D), at(24576, KD, NTOK)
        hg, hTm = at(24576, D), at(25600, KD, 2 * BS)
        g1, sg1, u1, av = (at(27648 + 512 * k, 512) for k in range(4))
        aT = [at(29696 + 512 * u, 4, 128) for u in range(2)]
        ysb = [at(30720 + 512 * u, 512) for u in range(2)]
        yk = [at(4096 * t, 4, D) for t in range(3)]
        ROLE = (8192, 16384, 0)
        wring = [at(r, KD, D) for r in ROLE]
        zo = 42440

        def zalloc(*dims):
            nonlocal zo
            zo += int(np.prod(dims))
            assert zo <= 53200, zo
            return at(zo - int(np.prod(dims)), *dims)

        b32, r32 = zalloc(3 * D), zalloc(3 * D)
        mid16 = b32[:, 0:1536].bitcast(BF16)
        nfin = zalloc(D)
        wr, rb, gffn = zalloc(KD, NE), zalloc(NE), zalloc(KD)
        lg, v8, i8 = zalloc(3, NE), zalloc(3, 8), zalloc(3, 8)
        i8u = i8.bitcast(U32)
        i8f, gt, gts = zalloc(3, TOPK), zalloc(3, TOPK), zalloc(3)
        oh, dtmp = zalloc(3, TOPK, NE), zalloc(3, TOPK, NE)
        msk, rk, nb = zalloc(3, NE), zalloc(128), zalloc(128)
        cc, ncol, nr, ovb = zalloc(1), zalloc(1), zalloc(NE), zalloc(NE + 1)
        qq, qa, qb_ = zalloc(3, NE), zalloc(3, NE), zalloc(3, NE)
        ebf, novp, dest = zalloc(NBLK), zalloc(1), zalloc(3, TOPK)
        ebi, novi, desti = zalloc(NBLK).bitcast(I32), zalloc(1).bitcast(I32), zalloc(3 * TOPK).bitcast(U32)
        etmp = zalloc(NBLK_OVER, NE)
        tabr, slots = zalloc(2 * BS), zalloc(NBLK // 2).bitcast(U32)
        idx = zalloc(1).bitcast(U32)
        ohb = zalloc(NBLK // 2).bitcast(BF16)
        bsel = [zalloc(BS // 2).bitcast(BF16) for _ in range(2)]
        ssf, sq5 = zalloc(9), at(30208, 3, D)
        ztab = zalloc(2 * BS)

        def CB_(name, *dims):
            off, n = at_b[name]
            return at(38912 + off, *(dims or (n,)))

        br_full, m_done, z_full, x2_done = (sem(n) for n in ("br_full", "m_done", "z_full", "x2_done"))
        m_tp, m_out = sem("m_tp"), [sem("m_out_act"), sem("m_out_dve")]
        sq_done, var5, root5, hn_ready = (sem(n) for n in ("sq_done", "var5", "root5", "hn_ready"))
        lg_full, gt_in, gt_exp, msk_ready, rk_full, nb_ready, ov_full = (
            sem(n) for n in ("lg_full", "gt_in", "gt_exp", "msk_ready", "rk_full", "nb_ready", "ov_full"))
        dest_ready, blocks_ready, slots_ready = sem("dest_ready"), sem("blocks_ready"), sem("slots_ready")
        ztab_ready, ztab_stored, scattered, tab_in = sem("ztab_ready"), sem("ztab_stored"), sem("scattered"), sem("tab_in")
        h_stored, bias_ready = sem("h_stored"), sem("bias_ready")
        e_in = place_in + w_arrived
        e_base = [64 * PAIRS_OF_SEQ] * 8 + [48, 48, 32, 32]
        e_used = sem("e_used")
        hg_in = sem("hg_in")
        i_ready, x_tp, x_out, g_full, u_full, g1_ready, sg_ready, a_ready, a_tp, a_out, yb_full, y_ready = (
            sem(n) for n in ("i_ready", "x_tp", "x_out", "g_full", "u_full", "g1_ready", "sg_ready", "a_ready",
                             "a_tp", "a_out", "yb_full", "y_ready"))
        y_stored, yk_in = [sem(f"y_stored{u}") for u in range(2)], [sem(f"yk_in{t}") for t in range(3)]
        sq8, var8, root8, out_ready, out_stored = (sem(n) for n in ("sq8", "var8", "root8", "out_ready", "out_stored"))
        dx, sum_ready = sem("dve_experts_own"), sem("sum_ready")

        V3 = [(t, nh) for t in range(3) for nh in range(2)]

        def m_out_done(eng, n):
            eng.wait_ge(m_out[0], n // 2 + 1)
            if n >= 1:
                eng.wait_ge(m_out[1], (n + 1) // 2)

        wgu = io["w_gate_up"][0].rearrange("e (p k) n -> e p k n", k=KD)
        wdn = io["w_down"][0].rearrange("e (h p k) n -> e p h k n", h=2, k=4)

        def block_weights(eng, e, s):
            role, j = s // 4, s % 4
            if role < 2:
                src = wgu[e, :, 2 * j:2 * j + 2, D * role:D * role + D]
            else:
                src = wdn[e, :, j // 2, 2 * (j % 2):2 * (j % 2) + 2, :]
            if not isinstance(e, int):
                src = src.rearrange("a p k n -> (a p) k n")
            eng.dma_start(wring[role][:, 2 * j:2 * j + 2, :], src).then_inc(e_in[s], 16)

        def sync_merge(sp):
            nonlocal n_stored
            sp.wait_ge(l_tp, PAIRS_OF_SEQ * L_TP)
            sp.wait_ge(l_out[1], PAIRS_OF_SEQ * L_TP // 2)
            for j in (6, 7):
                c0, w = CHUNKS[j]
                sp.dma_start(wslot[CHUNK_SLOT[j]], w_in[:, :, c0:c0 + w]).then_inc(w_arrived[CHUNK_SLOT[j]], 16)
            load(sp, "xn5", xnT5.rearrange("p k n -> p (k n)"), xn_dram)
            for j in (8, 9):
                c0, w = CHUNKS[j]
                sp.dma_start(wslot[CHUNK_SLOT[j]], w_in[:, :, c0:c0 + w]).then_inc(w_arrived[CHUNK_SLOT[j]], 16)
            load(sp, "br", br_n, io["w_br_nsa"][0].rearrange("(k p) n -> p k n", p=128))
            load(sp, "br", br_d, io["w_br_diff"][0].rearrange("(k p) n -> p k n", p=128))
            for t in range(3):
                load(sp, "late", x5[0:ROWS[t], t, :], x_rows[t])
            load(sp, "late", cstb, io["const_b"])
            load(sp, "late", gffn, io["norm_ffn"].rearrange("a (p k) -> p (a k)", k=KD))
            load(sp, "late", wr, io["w_router"][0].rearrange("(p k) e -> p k e", k=KD))
            load(sp, "late", rb, io["b_router"].to_broadcast([128, NE]))
            load(sp, "late", nfin, io["norm_final"].rearrange("(a n) -> a n", a=1).to_broadcast([128, D]))
            for s in range(3):
                load(sp, "bias", b32[32 * s:32 * s + 32, 0:2 * D], io["b_gate_up"][0])
                load(sp, "bias", b32[32 * s:32 * s + 32, 2 * D:3 * D], io["b_down"][0])
            sp.wait_ge(pj_full, 20)
            load(sp, "wout", w_out, io["w_out"][0].rearrange("(k p) n -> p k n", p=128))
            sp.wait_ge(ztab_ready, 1)
            sp.dma_start(tab_dram.rearrange("(b s) o -> b (s o)", s=2 * BS), ztab[0:NBLK // 2]).then_inc(ztab_stored, 16)
            sp.wait_ge(pj_full, 25)
            for s in range(4):
                block_weights(sp, 0, s)
            sp.wait_ge(br_full, 6)
            for s in range(4, 8):
                block_weights(sp, 0, s)
            sp.wait_ge(z_full, 6)
            for s in range(8, 12):
                block_weights(sp, 0, s)
            for t in range(3):
                sp.wait_ge(hn_ready, t + 1)
                sp.dma_start(h_dram[128 * t:128 * t + ROWS[t]], hn[0:ROWS[t], t, :]).then_inc(h_stored, 16)
            for s in range(12):
                sp.wait_ge(e_used, s + 1)
                block_weights(sp, 1, s)
            with sp.Fori(1, NE // 2) as i:
                for u in range(2):
                    for s in range(12):
                        sp.wait_ge(e_used, i * 24 + (12 * (u - 1) + s + 1))
                        block_weights(sp, bass.ds(2 * i + u, 1), s)
            sp.wait_ge(blocks_ready, 1)
            more = sp.value_load(novi[0:1, 0:1], min_val=0, max_val=NBLK_OVER // 2)
            with sp.If(more > 0):
                with sp.Fori(NE // 2, more + NE // 2) as i:
                    for u in range(2):
                        e = sp.value_load(ebi[0:1, bass.ds(2 * i + u, 1)], min_val=0, max_val=NE - 1)
                        for s in range(12):
                            sp.wait_ge(e_used, i * 24 + (12 * (u - 1) + s + 1))
                            block_weights(sp, bass.ds(e, 1), s)
            yp, ys = io["y_prompt"][0], io["y_sample"].rearrange("b t d -> (b t) d")
            for t in range(3):
                sp.wait_ge(out_ready, t + 1)
                sp.dma_start(yp[128 * t:128 * t + 128] if t < 2 else ys, x5[0:ROWS[t], t, :]).then_inc(out_stored, 16)
            sp.wait_ge(out_stored, 48)

        def pool_moe(pool, st):
            G = nc.gpsimd
            pool.wait_ge(l_odn, PAIRS_OF_SEQ)
            G.memset(ztab, 0.0).then_inc(ztab_ready, 1)
            arrived(pool, "bias")
            pool.wait_ge(z_full, 6)
            r96 = slice(0, 96)
            st(G.tensor_copy(bias16[r96], b32[r96]))
            st.own()
            st(G.tensor_tensor(r32[r96], b32[r96], bias16[r96], ALU.subtract))
            st.own()
            st(G.tensor_copy(mid16[r96], r32[r96]))
            st.own()
            st(G.tensor_tensor(r32[64:96], r32[64:96], mid16[64:96], ALU.subtract))
            st(G.tensor_copy(bias16[32:64], mid16[32:64]))
            st.own()
            st(G.tensor_copy(bias16[64:96], r32[64:96]), bias_ready)
            pool.wait_ge(dest_ready, 1)
            pool.wait_ge(ztab_stored, 16)
            pool.wait_ge(bias_ready, 1)
            for t in range(3):
                for k in range(TOPK):
                    r = ROWS[t]
                    G.indirect_dma_start(out=tab_dram, out_offset=bass.IndirectOffsetOnAxis(ap=desti[0:r, TOPK * t + k:TOPK * t + k + 1], axis=0),
                                         in_=CB_("tokid")[0:r, t:t + 1], in_offset=None).then_inc(scattered, 16)
            pool.wait_ge(scattered, 16 * 3 * TOPK)
            pool.dma_start(tabr[0:NBLK // 2], tab_dram.rearrange("(b s) o -> b (s o)", s=2 * BS)).then_inc(tab_in, 16)
            pool.wait_ge(slots_ready, 1)
            pool.wait_ge(h_stored, 48)
            pool.wait_ge(blocks_ready, 1)
            more = pool.value_load(novi[0:1, 0:1], min_val=0, max_val=NBLK_OVER // 2)
            with pool.Fori(0, more + NE // 2) as i:
                G.tensor_copy(idx, slots[:, bass.ds(i, 1)]).then_inc(i_ready, 1)
                pool.wait_ge(x_tp, i)
                pool.wait_ge(yb_full, i * 2)
                pool.wait_ge(i_ready, i * 3 + 1)
                for u in range(2):
                    G.tensor_copy(bsel[u][0:96], ohb[0:96, bass.ds(2 * i + u, 1)].to_broadcast([96, BS])).then_inc(i_ready, 1)
                G.indirect_dma_start(out=hg, out_offset=None, in_=h_dram,
                                     in_offset=bass.IndirectOffsetOnAxis(ap=idx, axis=0)).then_inc(hg_in, 16)
                for u in range(2):
                    for h in range(2):
                        pool.wait_ge(y_ready, i * 2 + (u + 1))
                        pool.dma_start(y_dram[bass.ds(i * (2 * BS) + u * BS, BS), 512 * h:512 * h + 512], ysb[u][64 * h:64 * h + 64]).then_inc(y_stored[u], 16)
            for u in range(2):
                pool.wait_ge(y_stored[u], (more + NE // 2) * 32)
            G.tensor_tensor(ztab[:, 0:1], ztab[:, 1:2], ztab[:, 2:3], ALU.add).then_inc(ztab_ready, 1)
            pool.wait_ge(ztab_ready, 2)
            for t in range(3):
                for k in range(TOPK):
                    r = ROWS[t]
                    G.indirect_dma_start(out=yk[t][0:r, k, :], out_offset=None, in_=y_dram,
                                         in_offset=bass.IndirectOffsetOnAxis(ap=desti[0:r, TOPK * t + k:TOPK * t + k + 1], axis=0)).then_inc(yk_in[t], 16)

        def pe_merge(pe):
            def tp(n, items):
                if n >= 2:
                    pe.wait_ge(m_out[n % 2], n // 2)
                for src, col in items:
                    r, c = src.shape[0], src.free_size()
                    last = nc.tensor.transpose(bank(n % 2)[0:c, col:col + r], src, ident[0:r, 0:r])
                last.then_inc(m_tp, 1)

            l_out_done(pe, PAIRS_OF_SEQ - 1, L_TP - 1)
            arrived(pe, "xn5")
            pe_projection(pe, PAIRS[3:5], 3, xnT5)
            arrived(pe, "br")
            arrived(pe, "br")
            for e in range(2):
                pe.wait_ge(pj_out[e], 15)
            for v, (t, nh) in enumerate(V3):
                if v >= 3:
                    pe.wait_ge(m_done, v - 2)
                r, b = ROWS[t], 2 + 2 * (v % 3)
                for k in range(4):
                    nc.tensor.matmul(bank(b)[0:r], onT[:, k, 128 * t:128 * t + r], br_n[:, k, 512 * nh:512 * nh + 512], start=(k == 0), stop=(k == 3))
                for k in range(4):
                    last = nc.tensor.matmul(bank(b + 1)[0:r], odT[:, k, 128 * t:128 * t + r], br_d[:, k, 512 * nh:512 * nh + 512], start=(k == 0), stop=(k == 3))
                last.then_inc(br_full, 1)
            for v, (t, nh) in enumerate(V3):
                pe.wait_ge(m_done, v + 1)
                tp(v, [(gsig[0:ROWS[t], t, 512 * nh + 128 * k:512 * nh + 128 * k + 128], ROWS[t] * k) for k in range(4)])
            arrived(pe, "wout")
            for v, (t, nh) in enumerate(V3):
                r = ROWS[t]
                m_out_done(pe, 2 * t + 1)
                for k in range(KD):
                    last = nc.tensor.matmul(bank(2 + v)[0:r], mT[:, k, 128 * t:128 * t + r], w_out[:, k, 512 * nh:512 * nh + 512], start=(k == 0), stop=(k == KD - 1))
                last.then_inc(z_full, 1)
            for t in range(3):
                pe.wait_ge(hn_ready, t + 1)
                for half in range(2):
                    tp(6 + 2 * t + half, [(hn[0:ROWS[t], t, 4 * half + k:D:KD], ROWS[t] * k) for k in range(4)])
            arrived(pe, "late")
            pe.wait_ge(x2_done, 6)
            for t in range(3):
                m_out_done(pe, 7 + 2 * t)
                for k in range(KD):
                    last = nc.tensor.matmul(bank(2)[0:ROWS[t], NE * t:NE * t + NE], hT6[:, k, 128 * t:128 * t + ROWS[t]], wr[:, k, :], start=(k == 0), stop=(k == KD - 1))
            last.then_inc(lg_full, 1)
            pe.wait_ge(msk_ready, 1)
            ones, lower = CB_("ones"), CB_("lower")
            for t in range(4):
                terms = [(ones[0:ROWS[s]], msk[0:ROWS[s], s]) for s in range(min(t, 3))]
                if t < 3:
                    terms.append((lower[0:ROWS[t]], msk[0:ROWS[t], t]))
                for n, (l, r) in enumerate(terms):
                    nc.tensor.matmul(bank(3)[:, NE * t:NE * t + NE], l, r, start=(n == 0), stop=(n == len(terms) - 1))
            for t in range(3):
                last = nc.tensor.matmul(bank(3)[0:NE, 128:129], msk[0:ROWS[t], t], ones[0:ROWS[t], 0:1], start=(t == 0), stop=(t == 2))
            last.then_inc(rk_full, 1)
            pe.wait_ge(nb_ready, 1)
            nc.tensor.matmul(bank(4)[:, 0:NE], nb[0:NE], CB_("before")[0:NE], start=True, stop=True)
            nc.tensor.matmul(bank(4)[:, NE:NE + 1], nb[0:NE], ones[0:NE, 0:1], start=True, stop=True).then_inc(ov_full, 1)
            pe.wait_ge(tab_in, 16)
            tp(12, [(tabr[0:NBLK // 2], 0)])
            m_out_done(pe, 12)
            pe.wait_ge(blocks_ready, 1)
            pe.wait_ge(bias_ready, 1)
            more = pe.value_load(novi[0:1, 0:1], min_val=0, max_val=NBLK_OVER // 2)
            with pe.Fori(0, more + NE // 2) as i:
                pe.wait_ge(hg_in, (i + 1) * 16)
                pe.wait_ge(a_out, i * 2)
                for k in range(KD):
                    last = nc.tensor.transpose(bank(k // 4)[:, 128 * (k % 4):128 * (k % 4) + 128], hg[:, k:D:KD], ident)
                last.then_inc(x_tp, 1)
                pe.wait_ge(i_ready, (i + 1) * 3)
                pe.wait_ge(x_out, i + 1)
                for u in range(2):
                    for role, full in ((0, g_full), (1, u_full)):
                        b = 2 + 2 * role + u
                        pe.wait_ge(a_ready, i * 2)
                        for k in range(KD):
                            if k % 2 == 0:
                                pe.wait_ge(e_in[4 * role + k // 2], i * 32 + (e_base[4 * role + k // 2] + 16 * (u + 1)))
                            for h in range(2):
                                last = nc.tensor.matmul(bank(b)[64 * h:64 * h + 64], hTm[:, k, BS * u:BS * u + BS], wring[role][:, k, 512 * h:512 * h + 512],
                                                        start=(k == 0), stop=False)
                            if k % 2:
                                last.then_inc(e_used, 1)
                        for h in range(2):
                            last = nc.tensor.matmul(bank(b)[64 * h:64 * h + 64], bsel[u][0:96, 0:BS], bias16[0:96, D * role + 512 * h:D * role + 512 * h + 512],
                                                    start=False, stop=True)
                        last.then_inc(full, 1)
                    pe.wait_ge(a_ready, i * 2 + (u + 1))
                    if u:
                        pe.wait_ge(a_out, i * 2 + 1)
                    for k in range(4):
                        last = nc.tensor.transpose(bank(1)[:, 128 * k:128 * k + 128], av[:, k:512:4], ident)
                    last.then_inc(a_tp, 1)
                    pe.wait_ge(a_out, i * 2 + (u + 1))
                    pe.wait_ge(y_ready, i * 2)
                    for c in range(KD):
                        if c % 2 == 0:
                            pe.wait_ge(e_in[8 + c // 2], i * 32 + (e_base[8 + c // 2] + 16 * (u + 1)))
                        for h in range(2):
                            last = nc.tensor.matmul(bank(6 + u)[64 * h:64 * h + 64], aT[u][:, c % 4, 64 * (c // 4):64 * (c // 4) + 64],
                                                    wring[2][:, c, 512 * h:512 * h + 512], start=(c == 0), stop=False)
                        if c % 2:
                            last.then_inc(e_used, 1)
                    for h in range(2):
                        last = nc.tensor.matmul(bank(6 + u)[64 * h:64 * h + 64], bsel[u][0:96, 0:BS], bias16[0:96, 2 * D + 512 * h:2 * D + 512 * h + 512],
                                                start=False, stop=True)
                    last.then_inc(yb_full, 1)

        def act_merge(act, st):
            A = nc.scalar.activation
            for q in (3, 4):
                for s in range(4):
                    j, t = PAIRS[q][s // 2], s % 2
                    act.wait_ge(pj_full, 5 * q + s + 1)
                    st(A(gsig[:, t, 512 * (j - 6):512 * (j - 6) + 512], bank(proj_bank(q, s)), ACT.Sigmoid), pj_out[t])
                act.wait_ge(pj_full, 5 * q + 5)
                for s in range(2):
                    j = PAIRS[q][s]
                    st(A(gsig[0:NS, 2, 512 * (j - 6):512 * (j - 6) + 512], bank(proj_bank(q, 4))[64 * s:64 * s + 64], ACT.Sigmoid), pj_out[s])

            def evac(n, gain):
                act.wait_ge(m_tp, n + 1)
                t, r = (n % 6) // 2, ROWS[(n % 6) // 2]
                for k in range(4 if gain else 1):
                    if gain:
                        st(A(hT6[:, k, 128 * t:128 * t + r], bank(0)[:, r * k:r * k + r], ACT.Copy, scale=gffn[:, k:k + 1]),
                           m_out[0] if k == 3 else None)
                    else:
                        st(A(mT[:, 0:4, 128 * t:128 * t + r], bank(0)[:, 0:4 * r].rearrange("p (k n) -> p k n", k=4), ACT.Copy), m_out[0])

            for n in (0, 2, 4):
                evac(n, False)
            arrived(act, "late")
            for t in range(3):
                r = ROWS[t]
                act.wait_ge(x2_done, 2 * t + 2)
                st(A(sq5[0:r, t], x5[0:r, t], ACT.Square, accum_out=ssf[0:r, t:t + 1]), sq_done)
                act.wait_ge(var5, t + 1)
                st(A(ssf[0:r, 3 + t:4 + t], ssf[0:r, 3 + t:4 + t], ACT.Sqrt), root5)
            for n in (6, 8, 10):
                evac(n, True)
            act.wait_ge(gt_in, 1)
            st(A(gt, gt, ACT.Exp), gt_exp)
            act.wait_ge(m_tp, 13)
            st(A(slots, bank(0)[:, 0:NBLK // 2], ACT.Copy), m_out[0])
            act.wait_ge(blocks_ready, 1)
            more = act.value_load(novi[0:1, 0:1], min_val=0, max_val=NBLK_OVER // 2)
            with act.Fori(0, more + NE // 2) as i:
                for u in range(2):
                    act.wait_ge(g1_ready, i * 2 + (u + 1))
                    A(sg1, g1, ACT.Sigmoid, scale=ALPHA).then_inc(sg_ready, 1)
                    act.wait_ge(a_tp, i * 2 + (u + 1))
                    act.wait_ge(yb_full, i * 2)
                    A(aT[u], bank(1).rearrange("p (k n) -> p k n", k=4), ACT.Copy).then_inc(a_out, 1)
                    act.wait_ge(yb_full, i * 2 + (u + 1))
                    act.wait_ge(y_stored[u], i * 32)
                    A(ysb[u], bank(6 + u), ACT.Copy).then_inc(y_ready, 1)
            for t in range(3):
                r = ROWS[t]
                act.wait_ge(sum_ready, t + 1)
                st(A(yk[t][0:r, 1, :], x5[0:r, t], ACT.Square, accum_out=ssf[0:r, t:t + 1]), sq8)
                act.wait_ge(var8, t + 1)
                st(A(ssf[0:r, 3 + t:4 + t], ssf[0:r, 3 + t:4 + t], ACT.Sqrt), root8)

        def dve_merge(dve, st):
            V = nc.vector
            for v, (t, nh) in enumerate(V3):
                r, b = ROWS[t], 2 + 2 * (v % 3)
                if v == 0:
                    for e in range(2):
                        dve.wait_ge(pj_out[e], 15)
                dve.wait_ge(br_full, v + 1)
                gn = gsig[0:r, t, 512 * nh:512 * nh + 512]
                gd = gsig[0:r, t, D + 512 * nh:D + 512 * nh + 512]
                st(V.tensor_tensor(gn, gn, bank(b)[0:r], ALU.mult))
                st(V.tensor_tensor(gd, gd, bank(b + 1)[0:r], ALU.mult))
                st.own()
                st(V.tensor_tensor(gn, gn, gd, ALU.add), m_done)
            for n in (1, 3, 5):
                t, r = n // 2, ROWS[n // 2]
                dve.wait_ge(m_tp, n + 1)
                st(V.tensor_copy(mT[:, 4:8, 128 * t:128 * t + r], bank(1)[:, 0:4 * r].rearrange("p (k n) -> p k n", k=4)), m_out[1])
            arrived(dve, "late")
            for t in range(3):
                r = ROWS[t]
                for nh in range(2):
                    v = 2 * t + nh
                    dve.wait_ge(z_full, v + 1)
                    xv = x5[0:r, t, 512 * nh:512 * nh + 512]
                    st(V.tensor_tensor(xv, xv, bank(2 + v)[0:r], ALU.add), x2_done)
                dve.wait_ge(sq_done, t + 1)
                s = ssf[0:r, 3 + t:4 + t]
                st(V.tensor_scalar(s, ssf[0:r, t:t + 1], 1.0 / D, EPS, ALU.mult, ALU.add), var5)
                dve.wait_ge(root5, t + 1)
                st(V.reciprocal(s, s))
                st.own()
                if t == 0:
                    dve.wait_ge(z_full, 6)
                st(V.tensor_scalar(hn[0:r, t], x5[0:r, t], s, None, ALU.mult), hn_ready)
            arrived(dve, "late")
            for n in (7, 9, 11):
                t, r = (n - 6) // 2, ROWS[(n - 6) // 2]
                dve.wait_ge(m_tp, n + 1)
                st(V.tensor_tensor(hT6[:, 4:8, 128 * t:128 * t + r], bank(1)[:, 0:4 * r].rearrange("p (k n) -> p k n", k=4),
                                   gffn[:, 4:8].unsqueeze(2).to_broadcast([128, 4, r]), ALU.mult), m_out[1])

            def op(f, *a):
                st(f(*a))
                st.own()

            op(V.memset, lg, 0.0)
            arrived(dve, "late")
            arrived(dve, "late")
            dve.wait_ge(lg_full, 1)
            st(V.tensor_tensor(lg[:, 0:2], bank(2)[:, 0:2 * NE].rearrange("p (t e) -> p t e", t=2), rb.unsqueeze(1).to_broadcast([128, 2, NE]), ALU.add))
            op(V.tensor_tensor, lg[0:NS, 2], bank(2)[0:NS, 2 * NE:3 * NE], rb[0:NS], ALU.add)
            for t in range(3):
                op(V.max, v8[:, t], lg[:, t])
                op(V.max_index, i8u.rearrange("p (t k) -> p t k", k=8)[:, t] if len(i8u.shape) == 2 else i8u[:, t], v8[:, t], lg[:, t])
            st(V.tensor_tensor(gt, v8[:, :, 0:TOPK], v8[:, :, 0:1].to_broadcast([128, 3, TOPK]), ALU.subtract), gt_in)
            op(V.tensor_copy, i8f, i8u[:, :, 0:TOPK])
            ex12 = CB_("expert").unsqueeze(1).to_broadcast([128, 12, NE])
            oh12, dt12 = oh.rearrange("p t k e -> p (t k) e"), dtmp.rearrange("p t k e -> p (t k) e")
            op(V.tensor_tensor, oh12, ex12, i8f.rearrange("p t k -> p (t k)").unsqueeze(2).to_broadcast([128, 12, NE]), ALU.is_equal)
            st(V.reduce_sum(msk, oh.rearrange("p t k e -> p t e k"), AX), msk_ready)
            dve.wait_ge(gt_exp, 1)
            op(V.reduce_sum, gts, gt, AX)
            op(V.reciprocal, gts, gts)
            op(V.tensor_tensor, gt, gt, gts.unsqueeze(2).to_broadcast([128, 3, TOPK]), ALU.mult)
            dve.wait_ge(rk_full, 1)
            st(V.tensor_copy(rk, bank(3)[:, 0:128]))
            op(V.tensor_copy, cc[0:NE], bank(3)[0:NE, 128:129])

            def steps_over(out, src, ge):
                cmp = ALU.is_ge if ge else ALU.is_gt
                op(V.tensor_scalar, out, src, float(BS), None, cmp)
                for c in range(2, NTOK // BS if NTOK % BS == 0 else NTOK // BS + 1):
                    op(V.scalar_tensor_tensor, out, src, float(BS * c), out, cmp, ALU.add)

            steps_over(ncol[0:NE], cc[0:NE], False)
            st(V.tensor_copy(nb[0:NE], ncol[0:NE].to_broadcast([NE, 128])), nb_ready)
            steps_over(nr, rk[:, 96:128], False)
            rk3 = rk[:, 0:96].rearrange("p (t e) -> p t e", t=3)
            steps_over(qq, rk3, True)
            dve.wait_ge(ov_full, 1)
            op(V.tensor_copy, ovb, bank(4)[:, 0:NE + 1])
            ovb3 = ovb[:, 0:NE].unsqueeze(1).to_broadcast([128, 3, NE])
            ex3 = CB_("expert").unsqueeze(1).to_broadcast([128, 3, NE])
            op(V.tensor_tensor, qa, qq, ovb3, ALU.add)
            op(V.tensor_tensor, qa, qa, ex3, ALU.subtract)
            op(V.tensor_scalar, qb_, qq, 0.0, None, ALU.is_gt)
            op(V.scalar_tensor_tensor, qa, qa, float(NE - 1), qb_, ALU.add, ALU.mult)
            op(V.tensor_tensor, qa, qa, ex3, ALU.add)
            op(V.scalar_tensor_tensor, qb_, qq, -float(BS), rk3, ALU.mult, ALU.add)
            op(V.scalar_tensor_tensor, qa, qa, float(BS), qb_, ALU.mult, ALU.add)
            for t in range(3):
                op(V.tensor_tensor, dtmp[:, t], oh[:, t], qa[:, t].unsqueeze(1).to_broadcast([128, TOPK, NE]), ALU.mult)
            op(V.reduce_sum, dest.rearrange("p t k -> p (t k)"), dt12, AX)
            st(V.tensor_copy(desti, dest.rearrange("p t k -> p (t k)")), dest_ready)
            op(V.tensor_tensor, nr, nr, ovb[:, 0:NE], ALU.add)
            op(V.tensor_tensor, etmp, nr.unsqueeze(1).to_broadcast([128, NBLK_OVER, NE]), CB_("over").unsqueeze(2).to_broadcast([128, NBLK_OVER, NE]), ALU.is_le)
            op(V.reduce_sum, ebf[:, NE:NBLK], etmp, AX)
            op(V.tensor_scalar, ebf[:, NE:NBLK], ebf[:, NE:NBLK], float(NE - 1), None, ALU.min)
            op(V.tensor_copy, ebf[:, 0:NE], CB_("expert"))
            st(V.tensor_copy(ebi, ebf))
            op(V.tensor_scalar, ohb[0:96], ebf[0:96], CB_("pmod")[0:96], None, ALU.is_equal)
            op(V.tensor_scalar, etmp[:, 0, 0:NBLK_OVER // 2], CB_("pairs"), ovb[:, NE:NE + 1], None, ALU.is_lt)
            op(V.reduce_sum, novp, etmp[:, 0, 0:NBLK_OVER // 2], AX)
            st(V.tensor_copy(novi, novp), blocks_ready)
            m_out_done(dve, 12)
            st(V.memset(cc, 0.0), slots_ready)
            dve.wait_ge(blocks_ready, 1)
            more = dve.value_load(novi[0:1, 0:1], min_val=0, max_val=NBLK_OVER // 2)
            before, st = st, Steps(dve, dx)
            with dve.Fori(0, more + NE // 2) as i:
                st.enter(i, {"dve_experts_own": 4, "x_out": 1, "g1_ready": 2, "a_ready": 2})
                dve.wait_ge(x_tp, i + 1)
                st(V.tensor_tensor(hTm, PS[:, 0:1024].rearrange("p (k n) -> p k n", k=KD), gffn.unsqueeze(2).to_broadcast([128, KD, 2 * BS]), ALU.mult), x_out)
                for u in range(2):
                    dve.wait_ge(g_full, i * 2 + (u + 1))
                    st(V.tensor_scalar(g1, bank(2 + u), LIM, None, ALU.min), g1_ready)
                    dve.wait_ge(u_full, i * 2 + (u + 1))
                    st(V.tensor_scalar(u1, bank(4 + u), -LIM, LIM, ALU.max, ALU.min))
                    st.own()
                    st(V.scalar_tensor_tensor(u1, u1, 1.0, g1, ALU.add, ALU.mult))
                    dve.wait_ge(sg_ready, i * 2 + (u + 1))
                    st.own()
                    if u:
                        dve.wait_ge(a_tp, i * 2 + 1)
                    st(V.tensor_tensor(av, u1, sg1, ALU.mult), a_ready)
            st.leave(None)
            st = before
            for t in range(3):
                r = ROWS[t]
                y = yk[t]
                dve.wait_ge(yk_in[t], 64)
                op_ = lambda ins: (st(ins), st.own())
                op_(V.tensor_scalar(y[0:r, 0], y[0:r, 0], gt[0:r, t, 0:1], None, ALU.mult))
                for k in range(1, TOPK):
                    op_(V.scalar_tensor_tensor(y[0:r, 0], y[0:r, k], gt[0:r, t, k:k + 1], y[0:r, 0], ALU.mult, ALU.add))
                st(V.tensor_tensor(x5[0:r, t], x5[0:r, t], y[0:r, 0], ALU.add), sum_ready)
                s = ssf[0:r, 3 + t:4 + t]
                dve.wait_ge(sq8, t + 1)
                st(V.tensor_scalar(s, ssf[0:r, t:t + 1], 1.0 / D, EPS, ALU.mult, ALU.add), var8)
                dve.wait_ge(root8, t + 1)
                st(V.reciprocal(s, s))
                st.own()
                if t == 0:
                    arrived(dve, "late")
                st(V.scalar_tensor_tensor(x5[0:r, t], x5[0:r, t], s, nfin[0:r], ALU.mult, ALU.mult), out_ready)

        block = ctx.enter_context(nc.Block())

        @block.sync
        def _(sp):
            nonlocal n_stored

            def store(dst, src):
                nonlocal n_stored
                n_stored += 16
                sp.dma_start(dst, src).then_inc(stored, 16)

            def load_chunk(j, slot, n):
                c0, w = CHUNKS[j]
                sp.dma_start(wslot[slot][:, :, 0:w], w_in[:, :, c0:c0 + w]).then_inc(w_arrived[slot], 16)

            for t in range(3):
                load(sp, f"x{t}", xin[0:ROWS[t], t, :], x_rows[t])
            load(sp, "const", cst, io["const_a"])
            load(sp, "const", gmix, io["norm_mix"].rearrange("a (k p) -> p (a k)", p=128),
                 allow_slow_non_contiguous=True)
            for j in range(4):
                load_chunk(j, j, 0)
            load(sp, "small", peraw[0:64, :], io["cmp_pe"].rearrange("a c l d -> (a c l) d"))
            load(sp, "small", w2, io["w_cmp2"].rearrange("a c h d -> h (a c) d"))
            load(sp, "small", dl, io["diff_lambda"].rearrange("a m d -> a (m d)").to_broadcast([128, 256]))
            load(sp, "small", sg, io["diff_subln"].rearrange("a (p o) -> (a p) o", o=1))
            load(sp, "small", ptab[:, :], io["page_table"].rearrange("(a b) n -> a (b n)", a=1))
            sp.wait_ge(pj_full, 5)
            load_chunk(4, 0, 1)
            load_chunk(5, 1, 1)
            sp.wait_ge(pj_full, 10)
            for c in range(2):
                for g in range(2):
                    load(sp, "w1", w1[64 * g:64 * g + 64, c], io["w_cmp1"][0, c].rearrange("(l d) h -> d l h", d=HD))
            sp.wait_ge(xn_ready, 6)
            out_done(sp, 5)
            sp.dma_start(xn_dram, xnT.rearrange("p k n -> p (k n)")).then_inc(xn_stored, 16)
            sp.wait_ge(gates_ready, 1)
            store(gate_dram, gates[0:NS, 2, :])

            def rows(name, p0, w):
                inner = io[name]
                return inner, p0, w

            sp.wait_ge(zeroed, 1)
            wp = io["new_win_kv_prompt"].rearrange("a b s c g d -> (a b s) (c g d)")
            for k in range(2):
                store(wp[128 * k:128 * k + 128], zero)
            for b in range(NB):
                store(io["new_win_kv_sample"].rearrange("a b s c g d -> (a b) s (c g d)")[b, 0:WIN - NT],
                      io["state_win_kv"].rearrange("a b s c g d -> (a b) s (c g d)")[b, NT:WIN])
            for k in range(NE * BS // 128, NBLK * BS // 128):
                store(y_dram[128 * k:128 * k + 128].rearrange("p (c n) -> p c n", n=256), zero.unsqueeze(1).to_broadcast([128, 4, 256]))
            sp.wait_ge(pj_out[0], 9)
            sp.wait_ge(pj_out[1], 9)
            sp.wait_ge(roped, 5)
            for name, p0, w in (("cmp_kv", P_CMP, 256), ("sel_kv", P_SEL, 256), ("diff_k", P_KD, 512), ("diff_v", P_VD, 512)):
                pr, sa = io[f"new_{name}_prompt"], io[f"new_{name}_sample"]
                fl = "a b s c g d -> (a b s) (c g d)" if len(pr.shape) == 6 else "a b s h d -> (a b s) (h d)"
                for t in range(2):
                    store(pr.rearrange(fl)[128 * t:128 * t + 128], proj[:, t, p0:p0 + w])
                store(sa.rearrange(fl), proj[0:NS, 2, p0:p0 + w])
            for t in range(2):
                store(wp[256 + 128 * t:384 + 128 * t], proj[:, t, P_WIN:P_WIN + 256])
            for b in range(NB):
                store(io["new_win_kv_sample"].rearrange("a b s c g d -> (a b) s (c g d)")[b, WIN - NT:WIN],
                      proj[NT * b:NT * b + NT, 2, P_WIN:P_WIN + 256])
            sp.wait_ge(stored, n_stored)
            for b in range(NB):
                for h in range(8):
                    load(sp, "gS", gS[64 * (b % 2) + 8 * h:64 * (b % 2) + 8 * h + 8, b // 2, :],
                         gate_dram[NT * b:NT * b + NT, 3 * h:3 * h + 3])
            sync_attention(sp)

        @block.gpsimd
        def _(pool):
            st = Steps(pool, pool_own)
            for v in (bd_raw, bd_rot, bd_dif, proj[64:128, 2], qraw[64:128, 2], qrot[64:128, 2], qdif[64:128, 2]):
                st(nc.gpsimd.memset(v, 0.0))
                st.own()
            nc.gpsimd.memset(zero, 0.0).then_inc(zeroed, 1)
            pool_attention(pool, st)

        @block.tensor
        def _(pe):
            def tp(n, items):
                if n >= 2:
                    pe.wait_ge(tp_out[n % 2], n // 2)
                for src, col in items:
                    r, c = src.shape[0], src.free_size()
                    last = nc.tensor.transpose(bank(n % 2)[0:c, col:col + r], src, ident[0:r, 0:r])
                last.then_inc(tp_full, 1)

            arrived(pe, "const")
            for t in range(3):
                r = ROWS[t]
                pe.wait_ge(xn_ready, 2 * t + 2)
                for half in range(2):
                    tp(2 * t + half, [(xin[0:r, t, 128 * (4 * half + k):128 * (4 * half + k) + 128], r * k) for k in range(4)])
            arrived(pe, "small")
            tp(G_PE, [(peraw[0:64, :], 0)])
            out_done(pe, G_PE)
            pe_projection(pe, PAIRS[0:3], 0)

            for n, (t, what) in enumerate(qk_groups):
                r = ROWS[t]
                if n == 0:
                    pe.wait_ge(pj_out[0], 9)
                    pe.wait_ge(pj_out[1], 9)
                pe.wait_ge(roped, {"raw": 0, "rot": 1, "dif": 4, "kd": 5, "kc": 3}[what])
                src = {"raw": qraw[0:r, t], "rot": qrot[0:r, t], "dif": qdif[0:r, t], "kd": proj[0:r, t, P_KD:P_KD + 512]}
                if what == "kc":
                    cols = [P_SEL, P_WIN] + ([P_CMP, P_CMP + 128] if t < 2 else [])
                    tp(G_QK + n, [(proj[0:r, t, c:c + 128], r * k) for k, c in enumerate(cols)])
                else:
                    tp(G_QK + n, [(src[what][:, 128 * k:128 * k + 128], r * k) for k in range(4)])

            arrived(pe, "w1")
            out_done(pe, G_QK + 14)
            for c in range(2):
                for l in range(CB):
                    last = nc.tensor.matmul(bank(7)[:, c:c + 1], w1[0:64, c, l, :], peT[0:64, c * CB + l:c * CB + l + 1],
                                            start=(l == 0), stop=(l == CB - 1))
            last.then_inc(hb_full, 1)
            for c in range(2):
                for l in range(CB):
                    for g in range(2):
                        last = nc.tensor.matmul(bank(2 + g)[:, 16 * c:16 * c + NCP], w1[64 * g:64 * g + 64, c, l, :],
                                                pcT[64 * g:64 * g + 64, c, l:l + CS * (NCP - 1) + 1:CS],
                                                start=(l == 0), stop=(l == CB - 1))
            last.then_inc(ph_full, 1)
            arrived(pe, "small")
            pe.wait_ge(ph_out, 1)
            for g in range(2):
                nc.tensor.matmul(bank(6)[64 * g:64 * g + 64, 0:NCP], w2[:, 0, :], hid[:, 0, g, 0:NCP], start=True, stop=True)
            for g in range(2):
                last = nc.tensor.matmul(bank(6)[0:NCP, 64 + 64 * g:128 + 64 * g], hid[:, 1, g, 0:NCP], w2[:, 1, :], start=True, stop=True)
            last.then_inc(pkv_full, 1)
            pe.wait_ge(pkv_out, 1)

            def scores(u):
                kind, t, g = UNITS[u]
                if u >= 2:
                    pe.wait_ge(s_read, u - 1)
                nk = unit_keys(u)
                b0 = 512 * (2 + 2 * (u % 2))
                for m in range(4):
                    out = PS[:, b0 + 256 * m:b0 + 256 * m + nk]
                    if kind == "dif":
                        h, c = 2 * g + m % 2, m // 2
                        q, k = qTd[64 * c:64 * c + 64, h], kdnT[64 * c:64 * c + 64, h, 0:nk]
                    else:
                        q = (qTraw if kind == "cmp" else qTrot)[64 * g:64 * g + 64, m]
                        k = {"sel": ksT, "win": kwT, "cmp": kcT.rearrange("p b n -> p (b n)")}[kind][64 * g:64 * g + 64, 0:nk]
                    last = nc.tensor.matmul(out, q[:, 128 * t:128 * t + 128], k, start=True, stop=True)
                last.then_inc(s_full, 1)

            def probs_t(u):
                nk, e0 = unit_keys(u), 1024 * (u % 2)
                pe.wait_ge(e_ready, u + 1)
                for j in range(unit_groups(u)):
                    w = min(128, nk)
                    tp(G_UNIT[u] + j, [(ebuf[:, e0 + m * nk + 128 * j:e0 + m * nk + 128 * j + w], 128 * m) for m in range(4)])

            def values(u):
                kind, t, g = UNITS[u]
                out_done(pe, G_UNIT[u + 1] - 1)
                if u >= 2:
                    pe.wait_ge(pv_read, u - 1)
                ng, dv = unit_groups(u), 128 if kind == "dif" else 64
                rows = NCP if kind == "cmp" else 128
                for m in range(4):
                    for j in range(ng):
                        p0 = 1024 * (u % 2) + 512 * j + 128 * m
                        if kind == "cmp":
                            v = vc[0:NCP, 0, 64 * g:64 * g + 64]
                        elif kind == "dif":
                            h = 2 * g + m % 2
                            v = proj[:, j, P_VD + 128 * h:P_VD + 128 * h + 128]
                        else:
                            base = (P_SEL if kind == "sel" else P_WIN) + 128 + 64 * g
                            v = proj[:, j, base:base + 64]
                        last = nc.tensor.matmul(bank(6 + u % 2)[:, dv * m:dv * m + dv], ptb[0:rows, p0:p0 + 128], v,
                                                start=(j == 0), stop=(j == ng - 1))
                last.then_inc(pv_full, 1)

            n = len(UNITS)
            for s in range(n + 2):
                if s < n:
                    scores(s)
                if 1 <= s <= n:
                    probs_t(s - 1)
                if s >= 2:
                    values(s - 2)
            pe.wait_ge(od_ready, 1)
            for t in range(2):
                tp(G_OUT + 2 * t, [(ons[:, t, 128 * k:128 * k + 128], 128 * k) for k in range(4)])
                tp(G_OUT + 2 * t + 1, [(ods[:, t, k, :], 128 * k) for k in range(4)])
            pe_attention(pe)

        def projection_out(eng, st, q, which, copy):
            for s in range(2):
                j = PAIRS[q][s]
                eng.wait_ge(pj_full, 5 * (q % 3) + 2 * s + which + 1)
                place(copy, st, j, which, bank(proj_bank(q, 2 * s + which)), 128, which)
            eng.wait_ge(pj_full, 5 * (q % 3) + 5)
            place(copy, st, PAIRS[q][which], 2, bank(proj_bank(q, 4))[64 * which:64 * which + 64], 64, which)

        def place(copy, st, j, t, src, r, which):
            w = CHUNKS[j][1]
            src = src[:, 0:w]
            if j == 0:
                dst = qraw[0:r, t].rearrange("p (r g d) -> p r g d", r=4, g=2)
                src = src.rearrange("p (g r d) -> p r g d", r=4, g=2)
            elif j == 3:
                dst = qdif[0:r, t]
            else:
                off = {1: P_CMP, 2: P_WIN, 4: P_KD, 5: P_VD}[j]
                dst = proj[0:r, t, off:off + w]
            st(copy(dst, src), pj_out[which])

        def qk_out(st, n, which, copy):
            t, what = qk_groups[n]
            g, r = G_QK + n, ROWS[t]
            src = bank(g % 2)[:, 0:4 * r].rearrange("p (k n) -> p k n", k=4)
            if what == "kc":
                parts = [(ksT[:, 128 * t:128 * t + r], src[:, 0]), (kwT[:, 128 * t:128 * t + r], src[:, 1])]
                if t < 2:
                    parts.append((pcT[:, :, 128 * t:128 * t + r], src[:, 2:4]))
            elif what == "kd":
                parts = [(kdnT[:, :, 128 * t:128 * t + r], src)]
            elif t < 2:
                parts = [({"raw": qTraw, "rot": qTrot, "dif": qTd}[what][:, :, 128 * t:128 * t + r], src)]
            elif what == "dif":
                parts = []
                for c in range(2):
                    d = bd_dif[64 * c:64 * c + 64].rearrange("p b (h x) -> p h b x", h=4)[:, :, :, 8 * c:8 * c + 8]
                    parts.append((d, src[64 * c:64 * c + 64].rearrange("p h (b t) -> p h b t", b=NB)))
            else:
                parts = []
                for gg in range(2):
                    d = (bd_raw if what == "raw" else bd_rot)[64 * gg:64 * gg + 64, :, 32 * gg:32 * gg + 32]
                    parts.append((d.rearrange("p b (r t) -> p r b t", r=4),
                                  src[64 * gg:64 * gg + 64].rearrange("p r (b t) -> p r b t", b=NB)))
            for k, (d, s) in enumerate(parts):
                st(copy(d, s), tp_out[which] if k == len(parts) - 1 else None)

        def prompt_evac(eng, st, u, which, copy):
            if u >= 2:
                eng.wait_ge(pv_full, u - 1)
            for j in range(unit_groups(u)):
                g = G_UNIT[u] + j
                if g % 2 == which:
                    eng.wait_ge(tp_full, g + 1)
                    rows = min(128, unit_keys(u))
                    p0 = 1024 * (u % 2) + 512 * j
                    st(copy(ptb[0:rows, p0:p0 + 512], bank(g % 2)[0:rows, :]), tp_out[which])

        def prompt_out(st, g, t, k, which):
            src = bank(g % 2).rearrange("p (k n) -> p k n", k=4)
            dst = (onT if k == 0 else odT)[:, :, 128 * t:128 * t + 128]
            if k == 0:
                ins = nc.scalar.activation(dst, src, ACT.Copy) if which == 0 else nc.vector.tensor_copy(dst, src)
            else:
                ins = (nc.scalar.activation(dst, src, ACT.Copy, scale=sg) if which == 0
                       else nc.vector.tensor_scalar(dst, src, sg, None, ALU.mult))
            st(ins, tp_out[which])

        @block.scalar
        def _(act):
            st = Steps(act, act_own)
            copy = lambda d, s: nc.scalar.activation(d, s, ACT.Copy)
            def root(v):
                n = st.n.get("root_ready", 0) + 1
                act.wait_ge(var_ready, n)
                st(nc.scalar.activation(v, v, ACT.Sqrt), root_ready)

            for t in range(3):
                arrived(act, f"x{t}")
                st(nc.scalar.activation(at(31232 + 1024 * t, 1024)[0:ROWS[t]], xin[0:ROWS[t], t, :], ACT.Square,
                                        accum_out=ssq[0:ROWS[t], t:t + 1]), squares)
            arrived(act, "const")
            for n in (0, 2, 4):
                t, r = n // 2, ROWS[n // 2]
                root(ssq[0:r, 3 + t:4 + t])
                act.wait_ge(tp_full, n + 1)
                for k in range(4):
                    st(nc.scalar.activation(xnT[:, k, 128 * t:128 * t + r], bank(0)[:, r * k:r * k + r], ACT.Copy,
                                            scale=gmix[:, k:k + 1]), tp_out[0] if k == 3 else None)
            act.wait_ge(tp_full, G_PE + 1)
            st(copy(peT[0:64, :], bank(0)[0:64, 0:64]), tp_out[0])
            act.wait_ge(pool_own, 7)
            for q in range(3):
                projection_out(act, st, q, 0, copy)
                if q == 1:
                    act.wait_ge(pj_out[0], 6)
                    act.wait_ge(pj_out[1], 6)
                    nc.scalar.activation(gates, proj[:, :, P_GN:P_GN + 24], ACT.Sigmoid).then_inc(gates_ready, 1)
            for n in range(15):
                if (G_QK + n) % 2 == 0:
                    act.wait_ge(tp_full, G_QK + n + 1)
                    qk_out(st, n, 0, copy)
            act.wait_ge(lam_sums, 1)
            nc.scalar.activation(lam[:, 2:4], lam[:, 0:2], ACT.Exp).then_inc(lam_exp, 1)
            act.wait_ge(hb_full, 1)
            st(copy(hb, bank(7)[:, 0:2]))
            act.wait_ge(ph_full, 1)
            st.own()
            for c in range(2):
                for g in range(2):
                    last = nc.scalar.activation(hid[:, c, g, 0:NCP], bank(2 + g)[:, 16 * c:16 * c + NCP],
                                                ACT.Gelu_apprx_tanh, bias=hb[:, c:c + 1])
            st(last, ph_out)
            act.wait_ge(pkv_full, 1)
            st(copy(kcT.rearrange("p b n -> p (b n)")[:, 0:NCP], bank(6)[:, 0:NCP]))
            st(copy(vc[0:NCP, 0, :], bank(6)[0:NCP, 64:192]), pkv_out)
            n = len(UNITS)
            for s in range(n + 1):
                if s >= 1:
                    prompt_evac(act, st, s - 1, 0, copy)
                if s < n:
                    nk, e0 = unit_keys(s), 1024 * (s % 2)
                    act.wait_ge(nmx_ready, s + 1)
                    if s >= 4:
                        act.wait_ge(pv_read, s - 3)
                    for m in range(4):
                        e = ebuf[:, e0 + m * nk:e0 + (m + 1) * nk]
                        st(nc.scalar.activation(e, e, ACT.Exp, bias=nmx[:, s % 2, m:m + 1], scale=SCALE,
                                                accum_out=sm[:, s % 4, m:m + 1]), e_ready if m == 3 else None)
            root(ssq)
            for t in range(2):
                for k in range(2):
                    g = G_OUT + 2 * t + k
                    if g % 2 == 0:
                        act.wait_ge(tp_full, g + 1)
                        prompt_out(st, g, t, k, 0)
            act_attention(act, st)

        @block.vector
        def _(dve):
            st = Steps(dve, dve_own)
            V = nc.vector

            def rstd(dst, src, n):
                st(V.tensor_scalar(dst, src, 1.0 / n, EPS, ALU.mult, ALU.add), var_ready)
                dve.wait_ge(root_ready, st.n["var_ready"])
                st(V.reciprocal(dst, dst))
                st.own()

            for t in range(3):
                r = ROWS[t]
                dve.wait_ge(squares, t + 1)
                rstd(ssq[0:r, 3 + t:4 + t], ssq[0:r, t:t + 1], D)
                for half in range(2):
                    v = xin[0:r, t, 512 * half:512 * half + 512]
                    st(V.tensor_scalar(v, v, ssq[0:r, 3 + t:4 + t], None, ALU.mult), xn_ready)
                n = 2 * t + 1
                if t == 0:
                    arrived(dve, "const")
                dve.wait_ge(tp_full, n + 1)
                st(V.tensor_tensor(xnT[:, 4:8, 128 * t:128 * t + r], bank(1)[:, 0:4 * r].rearrange("p (k n) -> p k n", k=4),
                                   gmix[:, 4:8].unsqueeze(2).to_broadcast([128, 4, r]), ALU.mult), tp_out[1])
            arrived(dve, "small")
            l4 = dl.rearrange("p (a b d) -> p a b d", a=2, b=2)
            st(V.tensor_tensor(l4[:, :, 0], l4[:, :, 0], l4[:, :, 1], ALU.mult))
            st.own()
            st(V.reduce_sum(lam[:, 0:2], l4[:, :, 0], AX), lam_sums)
            arrived(dve, "small")
            st(V.tensor_scalar(sg, sg, 1.0 - LAMBDA0, None, ALU.mult))
            dve.wait_ge(pool_own, 7)
            copy = V.tensor_copy

            def rope(src, dst, nh, t0):
                x1, x2 = src[:, :, :, 0:8], src[:, :, :, 8:16]
                cos = C("cos", 3, 8).unsqueeze(2).to_broadcast([128, 3, nh, 8])
                sin = C("sin", 3, 8).unsqueeze(2).to_broadcast([128, 3, nh, 8])
                tmp = [v[:, 0:24 * nh].rearrange("p (t h d) -> p t h d", t=3, h=nh) for v in ropet]
                for d, a, b in ((tmp[0], x1, cos), (tmp[1], x2, sin), (tmp[2], x1, sin), (tmp[3], x2, cos)):
                    st(V.tensor_tensor(d, a, b, ALU.mult))
                st.own()
                st(V.tensor_tensor(dst[:, :, :, 0:8], tmp[0], tmp[1], ALU.subtract))
                st(V.tensor_tensor(dst[:, :, :, 8:16], tmp[2], tmp[3], ALU.add), roped)
                st.own()

            heads = lambda v: v.rearrange("p t (h d) -> p t h d", d=HD)
            projection_out(dve, st, 0, 1, copy)
            dve.wait_ge(pj_out[0], 3)
            st.own()
            st(copy(qrot, qraw))
            st.own()
            rope(heads(qraw), heads(qrot), 8, 0)
            rope(heads(proj[:, :, P_SEL:P_SEL + 128]), heads(proj[:, :, P_SEL:P_SEL + 128]), 2, 0)
            projection_out(dve, st, 1, 1, copy)
            dve.wait_ge(pj_out[0], 6)
            st.own()
            rope(heads(proj[:, :, P_WIN:P_WIN + 128]), heads(proj[:, :, P_WIN:P_WIN + 128]), 2, 0)
            rope(heads(qdif), heads(qdif), 8, 0)
            projection_out(dve, st, 2, 1, copy)
            dve.wait_ge(pj_out[0], 9)
            st.own()
            rope(heads(proj[:, :, P_KD:P_KD + 512]), heads(proj[:, :, P_KD:P_KD + 512]), 8, 0)
            for n in range(15):
                if (G_QK + n) % 2 == 1:
                    dve.wait_ge(tp_full, G_QK + n + 1)
                    qk_out(st, n, 1, copy)
            dve.wait_ge(lam_exp, 1)
            st(V.tensor_tensor(lam[:, 4:5], lam[:, 3:4], lam[:, 2:3], ALU.subtract))
            st.own()
            st(V.tensor_scalar(lam[:, 4:5], lam[:, 4:5], LAMBDA0, None, ALU.subtract))
            st(V.memset(lv[:, 0:2], 1.0))
            st.own()
            st(V.tensor_copy(lv[:, 2:4], lam[:, 4:5].to_broadcast([128, 2])))
            st(V.scalar_tensor_tensor(cmat, C("c1"), lam[:, 4:5], C("c0"), ALU.mult, ALU.add), lam_done)

            def masked(u):
                kind, t, g = UNITS[u]
                nk, e0, b0 = unit_keys(u), 1024 * (u % 2), 512 * (2 + 2 * (u % 2))
                dve.wait_ge(s_full, u + 1)
                if u >= 2:
                    dve.wait_ge(tp_full, G_UNIT[u - 1])
                m = (C("cmpm", 2, NCP) if kind == "cmp" else C("causal", 2, SEQ))[:, t, 0:nk]
                e = ebuf[:, e0:e0 + 4 * nk].rearrange("p (m k) -> p m k", m=4)
                s = PS[:, b0:b0 + 1024].rearrange("p (m k) -> p m k", m=4)[:, :, 0:nk]
                st(V.tensor_tensor(e, s, m.unsqueeze(1).to_broadcast([128, 4, nk]), ALU.add), s_read)
                st.own()
                st(V.reduce_max(mx[:, u % 2], e, AX))
                st.own()
                if u >= 2:
                    dve.wait_ge(e_ready, u - 1)
                st(V.tensor_scalar(nmx[:, u % 2], mx[:, u % 2], -SCALE, None, ALU.mult), nmx_ready)

            def combine(u):
                kind, t, g = UNITS[u]
                c = cf[:, u % 2]
                dve.wait_ge(pv_full, u + 1)
                st(V.reciprocal(c, sm[:, u % 4]))
                st.own()
                if kind == "dif":
                    st(V.tensor_tensor(c, c, lv, ALU.mult))
                else:
                    br = {"cmp": 0, "sel": 1, "win": 2}[kind]
                    st(V.tensor_tensor(c, c, gates[:, t, 12 * g:12 * g + 12].rearrange("p (r b) -> p r b", b=3)[:, :, br], ALU.mult))
                    if kind == "cmp":
                        st.own()
                        st(V.tensor_scalar(c, c, C("cmpv")[:, t:t + 1], None, ALU.mult))
                st.own()
                if kind == "dif":
                    pv = bank(6 + u % 2).rearrange("p (m e) -> p m e", m=4)
                    tm = pvt.rearrange("p (m e) -> p m e", m=4)
                    st(V.tensor_tensor(tm, pv, c.unsqueeze(2).to_broadcast([128, 4, 128]), ALU.mult), pv_read)
                    st.own()
                    st(V.tensor_tensor(ods[:, t, 2 * g:2 * g + 2, :], tm[:, 0:2], tm[:, 2:4], ALU.add))
                else:
                    pv = bank(6 + u % 2)[:, 0:256].rearrange("p (m e) -> p m e", m=4)
                    dst = ons[:, t, 256 * g:256 * g + 256].rearrange("p (m e) -> p m e", m=4)
                    out = dst if kind == "sel" else pvt[:, 0:256].rearrange("p (m e) -> p m e", m=4)
                    st(V.tensor_tensor(out, pv, c.unsqueeze(2).to_broadcast([128, 4, 64]), ALU.mult), pv_read)
                    if kind != "sel":
                        st.own()
                        st(V.tensor_tensor(dst, dst, out, ALU.add))
                st.own()

            dve.wait_ge(gates_ready, 1)
            dve.wait_ge(xn_stored, 16)
            n = len(UNITS)
            for s in range(n + 2):
                if s < n:
                    masked(s)
                if 1 <= s <= n:
                    prompt_evac(dve, st, s - 1, 1, copy)
                if s >= 2:
                    combine(s - 2)
            sq = at(24576, 1024)
            st(V.tensor_tensor(sq, ods.rearrange("p t h e -> p (t h e)"), ods.rearrange("p t h e -> p (t h e)"), ALU.mult))
            st.own()
            st(V.reduce_sum(ssq, sq.rearrange("p (a e) -> p a e", e=128), AX))
            st.own()
            rstd(ssq, ssq, 128)
            o8 = ods.rearrange("p t h e -> p (t h) e")
            st(V.tensor_tensor(o8, o8, ssq.unsqueeze(2).to_broadcast([128, 8, 128]), ALU.mult), od_ready)
            for t in range(2):
                for k in range(2):
                    g = G_OUT + 2 * t + k
                    if g % 2 == 1:
                        dve.wait_ge(tp_full, g + 1)
                        prompt_out(st, g, t, k, 1)
            dve_attention(dve, st)


_INS = ['x_prompt', 'x_sample', 'cache_cmp_kv', 'cache_sel_kv', 'state_win_kv', 'cache_diff_k', 'cache_diff_v',
        'page_table', 'norm_mix', 'w_in', 'cmp_pe', 'w_cmp1', 'w_cmp2', 'diff_lambda', 'diff_subln', 'w_br_nsa',
        'w_br_diff', 'w_out', 'norm_ffn', 'w_router', 'b_router', 'w_gate_up', 'b_gate_up', 'w_down', 'b_down',
        'norm_final']
_OUTS = [('y_prompt', (1, SEQ, D)), ('y_sample', (NB, NT, D)),
         ('new_cmp_kv_prompt', (1, 1, SEQ, 2, 2, HD)), ('new_cmp_kv_sample', (1, NB, NT, 2, 2, HD)),
         ('new_sel_kv_prompt', (1, 1, SEQ, 2, 2, HD)), ('new_sel_kv_sample', (1, NB, NT, 2, 2, HD)),
         ('new_win_kv_prompt', (1, 1, WIN, 2, 2, HD)), ('new_win_kv_sample', (1, NB, WIN, 2, 2, HD)),
         ('new_diff_k_prompt', (1, 1, SEQ, 4, 2, HD)), ('new_diff_k_sample', (1, NB, NT, 4, 2, HD)),
         ('new_diff_v_prompt', (1, 1, SEQ, 4, 128)), ('new_diff_v_sample', (1, NB, NT, 4, 128))]


def kernel(**inputs):
    import numpy as _np
    import concourse.bacc as _bacc
    from concourse import mybir as _mybir
    from concourse.bass_utils import run_bass_kernel_spmd as _run

    nc = _bacc.Bacc("TRN2", target_bir_lowering=False, num_devices=1)
    const_a, at_a, const_b, at_b = shape_constants()
    arrays, io = {}, {}
    for name in _INS:
        a = _np.ascontiguousarray(inputs[name])
        arrays["in_" + name] = a
        io[name] = nc.dram_tensor("in_" + name, a.shape, _mybir.dt.from_np(a.dtype), kind="ExternalInput").ap()
    for name, a in (("const_a", const_a), ("const_b", const_b)):
        arrays["in_" + name] = a
        io[name] = nc.dram_tensor("in_" + name, a.shape, _mybir.dt.from_np(a.dtype), kind="ExternalInput").ap()
    for name, shape in _OUTS:
        io[name] = nc.dram_tensor("out_" + name, shape, F32, kind="ExternalOutput").ap()
    build(nc, io, const_a, at_a, const_b, at_b)
    r = _run(nc, [arrays], core_ids=[0])
    return tuple(r.results[0]["out_" + name] for name, _ in _OUTS)
```

```python
import numpy as np
import concourse.bass as bass
from concourse import mybir
from contextlib import ExitStack

F32 = mybir.dt.float32
BF16 = mybir.dt.bfloat16
I32 = mybir.dt.int32
U32 = mybir.dt.uint32
ALU = mybir.AluOpType
ACT = mybir.ActivationFunctionType
AX = mybir.AxisListType.X

D = 1024
KD = D // 128
SEQ = 256
NB, NT = 8, 8
NS = NB * NT
NTOK = SEQ + NS
ROWS = (128, 128, NS)
PAST, PAGE = 1024, 128
NPAGE = PAST // PAGE
NPOOL = (5 * NB * NPAGE + 3) // 4
WIN = 512
HD = 64
SCALE = HD ** -0.5
EPS = 1e-5
CB, CS = 32, 16
NCP = (SEQ - CB) // CS + 1
NCC = (PAST + NT - CB) // CS + 1
SB = 64
NE, TOPK, DFF = 32, 4, 1024
LIM, ALPHA = 7.0, 1.702
LAMBDA0 = 0.8 - 0.6 * 1.0
NEG = -1e30
THETA = 500000.0

CHUNKS = ((0, 512), (512, 512), (1024, 280), (1304, 512), (1816, 512), (2328, 512),
          (2840, 512), (3352, 512), (3864, 512), (4376, 512))
P_CMP, P_SEL, P_WIN, P_GN, P_KD, P_VD, PW = 0, 256, 512, 768, 792, 1304, 1816

BS = 64
NBLK_OVER = 20
NBLK = NE + NBLK_OVER


def shape_constants():
    f = np.float32
    p = np.arange(128)
    tok = np.stack([p, 128 + p, PAST + p % NT])
    half = HD // 8
    inv = (f(THETA) ** (-np.arange(half, dtype=f) / f(half))).astype(f)
    ang = tok.astype(f)[:, :, None] * inv
    cos, sin = np.cos(ang).astype(f), np.sin(ang).astype(f)
    a = {}
    a["ident"] = np.eye(128)
    k = np.arange(SEQ)
    a["causal"] = np.where(k[None, None] <= tok[:2, :, None], 0, NEG).transpose(1, 0, 2).reshape(128, -1)
    ends = np.arange(NCP) * CS + CB - 1
    a["cmpm"] = np.where(ends[None, None] <= tok[:2, :, None], 0, NEG).transpose(1, 0, 2).reshape(128, -1)
    a["cmpv"] = (tok[:2] >= CB - 1).T
    a["cos"] = cos.transpose(1, 0, 2).reshape(128, -1)
    a["sin"] = sin.transpose(1, 0, 2).reshape(128, -1)
    kb, kt = np.arange(NS) // NT, np.arange(NS) % NT
    t = p % NT
    nsa = np.full((128, NB // 2, NS), NEG)
    for i in range(NB // 2):
        b = 2 * i + p // 64
        nsa[:, i] = np.where((kb[None] == b[:, None]) & (kt[None] <= t[:, None]), 0, NEG)
    a["newn"] = nsa.reshape(128, -1)
    dif = np.full((128, NB, NS), NEG)
    for b in range(NB):
        dif[:, b] = np.where((kb[None] == b) & (kt[None] <= t[:, None]), 0, NEG)
    a["newd"] = dif.reshape(128, -1)
    a["oldw"] = np.where(np.arange(NT)[None] > t[:, None], 0, NEG)
    a["rsum"] = (p[:, None] // 32 == p[None] // 32) & (t[:, None] == t[None])
    row, col = p[:, None], p[None]
    own = (row // 32 == col // 32) & (col % 32 < NT)
    a["c0"] = own & (row % 32 == col % 32)
    a["c1"] = own & (row % 32 == col % 32 + NT)
    a["blk"] = np.tile(np.arange(1, PAST // SB - 1), (128, 1))
    d = {}
    d["lower"] = row < col
    d["ones"] = np.ones((128, 128))
    d["before"] = np.where((row < col) & (row < NE), 1, 0)[:, :NE]
    d["expert"] = np.tile(np.arange(NE), (128, 1))
    d["over"] = np.tile(np.arange(NBLK_OVER), (128, 1))
    d["pairs"] = np.tile(2 * np.arange(NBLK_OVER // 2), (128, 1))
    d["pmod"] = (p % NE)[:, None]
    d["pair128"] = np.tile(2 * BS * np.arange(1, NBLK // 2), (128, 1))
    d["slot"] = np.tile(np.arange(2 * BS), (128, 1))
    d["pair"] = np.tile(np.arange(NBLK // 2), (128, 1))
    d["tokid"] = np.stack([p, 128 + p, SEQ + p], 1)
    out = []
    for group in (a, d):
        at, where = 0, {}
        for name, v in group.items():
            where[name] = (at, v.shape[1])
            at += v.shape[1]
        out += [np.ascontiguousarray(np.concatenate([np.asarray(v, f) for v in group.values()], 1)), where]
    return out


class Steps:

    def __init__(self, eng, own, primed=()):
        self.eng, self.default, self.base, self.last = eng, own, {}, None
        self.n = {s.name: 1 for s in primed}

    def __call__(self, ins, sem=None):
        sem = sem or self.default
        self.n[sem.name] = self.n.get(sem.name, 0) + 1
        ins.then_inc(sem, 1)
        self.last = (sem, self.n[sem.name])

    def own(self):
        sem, n = self.last
        self.eng.wait_ge(sem, self.base.get(sem.name, 0) + n)

    def enter(self, i, per):
        self.start, self.per = dict(self.n), per
        self.base = {s: i * k for s, k in per.items()}

    def leave(self, trips):
        for s in set(self.n) | set(self.per):
            k = self.per.get(s, 0)
            got = self.n.get(s, 0) - self.start.get(s, 0)
            assert got == k, (s, got, k, {q: self.n[q] - self.start.get(q, 0) for q in self.n})
            self.n[s] = self.start.get(s, 0) + (trips * k if trips else 0)
        self.base, self.last = {}, None


def build(nc, io, const_a, at_a, const_b, at_b):
    ctx = ExitStack()
    with ctx:
        sem = lambda name: ctx.enter_context(nc.semaphore(name))
        arena = ctx.enter_context(nc.sbuf_tensor("arena", [128, 53200], F32))
        PS = ctx.enter_context(nc.psum_tensor("PS", [128, 8 * 512], F32))

        def at(off, *dims):
            n = int(np.prod(dims))
            v = arena[:, off:off + n]
            if len(dims) == 2:
                return v.rearrange("p (a b) -> p a b", b=dims[1])
            if len(dims) == 3:
                return v.rearrange("p (a b c) -> p a b c", b=dims[1], c=dims[2])
            if len(dims) == 4:
                return v.rearrange("p (a b c d) -> p a b c d", b=dims[1], c=dims[2], d=dims[3])
            return v

        def bank(k, n=512, off=0):
            return PS[:, 512 * k + off:512 * k + off + n]

        RING = 24576
        wslot = [at(4096 * s, KD, 512) for s in range(4)]
        sel_raw = at(0, 2, NPAGE, 256)
        win_raw = at(4096, 2, WIN // PAGE, 256)
        dv_raw = [[at(6144 + 512 * j, 512) for j in range(NPAGE)],
                  [at(34304 + 512 * j if j < NPAGE - 1 else 30720, 512) for j in range(NPAGE)]]
        w1 = at(10240, 2, CB // 2, 128)
        xin = at(18432, 3, D)
        cmpT = at(18432, 4, 2, PAST // 2)
        kdT = at(18432, 4, PAST)
        xnT = at(22528, KD, NTOK)
        ropet = [at(25088 + 384 * k, 384) for k in range(4)]
        ebuf = at(22528, 2048)
        ptb = at(24576, 2048)
        qraw, qrot, qdif = (at(26624 + 1536 * k, 3, 512) for k in range(3))
        ons, ods = at(26624, 2, 512), at(27648, 2, 4, 128)
        pvt = at(28672, 512)
        cmp_raw = at(14336, NPAGE, 512)
        dk_raw = at(26624, NPAGE, 512)
        qTraw, qTrot, qTd = (at(31232 + 1024 * k, 4, SEQ) for k in range(3))
        winT, selT = at(31232, 2, WIN), at(32256, 2, PAST)
        proj = at(34304, 3, PW)
        onT, odT = at(39752, 4, NTOK), at(41032, 4, NTOK)
        cst = at(42312, const_a.shape[1])
        o = 42312 + const_a.shape[1]

        def alloc(*dims):
            nonlocal o
            o += int(np.prod(dims))
            assert o <= 53200, o
            return at(o - int(np.prod(dims)), *dims)

        cmat = alloc(128)
        bd_raw, bd_rot, bd_dif = alloc(NB, 64), alloc(NB, 64), alloc(NB, 128)
        cur_raw, cur_rot, cur_dif = alloc(2, 64), alloc(2, 64), alloc(2, 128)
        ksT, kwT, kdnT = alloc(NTOK), alloc(NTOK), alloc(4, NTOK)
        hid = alloc(2, 2, 126)
        kcT, vc = alloc(2, NCC), alloc(2, 128)
        pcT, w2 = alloc(2, 2, SEQ // 2), alloc(2, 64)
        gmix, sg, hb, peT = alloc(KD), alloc(1), alloc(2), alloc(CB)
        ssq, lam, lv = alloc(8), alloc(8), alloc(4)
        gates, gS = alloc(3, 24), alloc(NB // 2, 3)
        mx, nmx, sm, cf = alloc(2, 4), alloc(2, 4), alloc(4, 4), alloc(2, 4)
        dl, peraw = alloc(256), alloc(128)
        osm, onrm, odn = alloc(128), alloc(128), alloc(2, 128)
        pgs, mass, imp, dropm = alloc(NCC + 1), alloc(14, 4), alloc(14), alloc(14)
        smx, primer = alloc(8), alloc(12)
        zero = alloc(256)
        ptab = alloc(NB * NPAGE)[0:1, :].bitcast(I32)

        def C(name, *dims):
            off, n = at_a[name]
            return at(42312 + off, *(dims or (n,)))

        ident = C("ident")

        xn_dram = nc.dram_tensor("xn_scratch", [128, KD * NTOK], F32, kind="Internal").ap()
        gate_dram = nc.dram_tensor("gate_scratch", [NS, 24], F32, kind="Internal").ap()
        h_dram = nc.dram_tensor("h_scratch", [NTOK, D], F32, kind="Internal").ap()
        y_dram = nc.dram_tensor("y_scratch", [NBLK * BS, D], F32, kind="Internal").ap()

        w_in = io["w_in"][0].rearrange("(k p) n -> p k n", p=128)
        x_rows = [io["x_prompt"][0, 0:128], io["x_prompt"][0, 128:256],
                  io["x_sample"].rearrange("b t d -> (b t) d")]

        loaded = {}

        def load(eng, name, dst, src, **kw):
            if name not in loaded:
                loaded[name] = [sem("load_" + name), 0]
            loaded[name][1] += 16
            eng.dma_start(dst, src, **kw).then_inc(loaded[name][0], 16)

        def arrived(eng, name):
            eng.wait_ge(loaded[name][0], loaded[name][1])

        stored = sem("stored")
        n_stored = 0
        w_arrived = [sem(f"w_arrived{s}") for s in range(4)]
        tp_full = sem("tp_full")
        tp_out = [sem("tp_out_act"), sem("tp_out_dve")]
        pj_full = sem("pj_full")
        pj_out = [sem("pj_out_act"), sem("pj_out_dve")]
        var_ready, root_ready = sem("var_ready"), sem("root_ready")
        act_own, dve_own, pool_own = sem("act_own"), sem("dve_own"), sem("pool_own")
        squares = sem("squares")
        xn_stored = sem("xn_stored")
        xn_ready = sem("xn_ready")
        zeroed = sem("zeroed")
        roped = sem("roped")
        gates_ready = sem("gates_ready")
        lam_sums, lam_exp, lam_done = sem("lam_sums"), sem("lam_exp"), sem("lam_done")
        hb_full, hb_out = sem("hb_full"), sem("hb_out")
        ph_full, ph_out, pkv_full, pkv_out = (sem(n) for n in ("ph_full", "ph_out", "pkv_full", "pkv_out"))
        s_full, s_read, nmx_ready, e_ready = (sem(n) for n in ("s_full", "s_read", "nmx_ready", "e_ready"))
        pv_full, pv_read = sem("pv_full"), sem("pv_read")
        od_ready = sem("od_ready")

        CHUNK_SLOT = (0, 1, 2, 3, 0, 1, 2, 3, 0, 1)
        CHUNK_USE = (1, 1, 1, 1, 2, 2, 2, 2, 3, 3)

        def chunk_at(j):
            return {6: at(10240, KD, 512), 7: at(14336, KD, 512), 9: at(18432, KD, 512)}.get(j, wslot[CHUNK_SLOT[j]])

        PAIRS = tuple((2 * q, 2 * q + 1) for q in range(5))

        def proj_bank(q, slot):
            return (2, 3, 5, 6, 4 if q % 2 == 0 else 7)[slot]

        UNITS = [(kind, t, g) for t in range(2) for kind in ("sel", "win", "cmp", "dif") for g in range(2)]

        def unit_keys(u):
            kind, t, _ = UNITS[u]
            return NCP if kind == "cmp" else 128 * (t + 1)

        def unit_groups(u):
            kind, t, _ = UNITS[u]
            return 1 if kind == "cmp" else t + 1

        G_XN = 0
        G_PE = 6
        G_QK = 7
        G_UNIT = [G_QK + 14 + sum(unit_groups(v) for v in range(u)) for u in range(len(UNITS) + 1)]
        G_OUT = G_UNIT[-1]
        G_END = G_OUT + 4
        qk_groups = [(t, what) for t in range(3) for what in ("raw", "rot", "dif", "kd", "kc")]
        qk_groups.remove((2, "kc"))
        qk_groups.append((2, "kc"))
        assert len(qk_groups) == 15
        G_UNIT = [g + 1 for g in G_UNIT]
        G_OUT += 1
        G_END += 1

        def out_done(eng, n, sems=tp_out):
            eng.wait_ge(sems[0], n // 2 + 1)
            if n >= 1:
                eng.wait_ge(sems[1], (n + 1) // 2)

        def pe_projection(pe, pairs, first, xnT=xnT):
            for n, (j0, j1) in enumerate(pairs):
                q = first + n
                for s, j in enumerate((j0, j1)):
                    w, slot = CHUNKS[j][1], CHUNK_SLOT[j]
                    pe.wait_ge(w_arrived[slot], 16 * CHUNK_USE[j])
                    for t in range(2):
                        if n >= 1:
                            pe.wait_ge(pj_out[t], 3 * (q - 1) + s + 1)
                        for k in range(KD):
                            last = nc.tensor.matmul(bank(proj_bank(q, 2 * s + t))[:, 0:w], xnT[:, k, 128 * t:128 * t + 128],
                                                    chunk_at(j)[:, k, 0:w], start=(k == 0), stop=(k == KD - 1))
                        last.then_inc(pj_full, 1)
                if n >= 2:
                    for e in range(2):
                        pe.wait_ge(pj_out[e], 3 * (q - 1))
                for k in range(KD):
                    for s, j in enumerate((j0, j1)):
                        w = CHUNKS[j][1]
                        last = nc.tensor.matmul(bank(proj_bank(q, 4))[64 * s:64 * s + 64, 0:w], xnT[:, k, 256:NTOK],
                                                chunk_at(j)[:, k, 0:w], start=(k == 0), stop=(k == KD - 1))
                last.then_inc(pj_full, 1)

        PAIRS_OF_SEQ = NB // 2
        L_TP = 42
        place_in = [sem(f"place_in{k}") for k in range(8)]
        cmp_in = place_in[0:4]
        sel_in = place_in[4:8]
        dk_in = [sem(f"dk_in{k}") for k in range(2)]
        win_in = [sem(f"win_in{k}") for k in range(2)]
        dv_in = [sem(f"dv_in{k}") for k in range(4)]
        l_tp, l_out = sem("l_tp"), [sem("l_out_act"), sem("l_out_dve")]
        l_hid, l_gelu, l_kv, l_kv_out = sem("l_hid"), sem("l_gelu"), sem("l_kv"), sem("l_kv_out")
        l_cur = sem("l_cur")
        l_sc = sem("l_sc")
        l_nmx, l_exp = sem("l_nmx"), sem("l_exp")
        l_pn, l_grp = sem("l_pn"), sem("l_grp")
        l_pv, l_pv_out = sem("l_pv"), sem("l_pv_out")
        l_on, l_join, l_osq, l_sq, l_var, l_root, l_odn = (sem(n) for n in ("l_on", "l_join", "l_osq", "l_sq", "l_var", "l_root", "l_odn"))
        l_act, l_dve = sem("l_act"), sem("l_dve")
        primed = [l_tp, l_out[0], l_out[1], l_sc, l_exp, l_pv]

        def past(eng, s, n):
            eng.wait_ge(s, n + 1)


        SELW, WINW = PAST + NS, WIN + NS
        E_SEL, E_WIN, E_CMP = 0, SELW, SELW + WINW
        e_sel, e_win, e_cmp = ebuf[:, 0:SELW], ebuf[:, E_WIN:E_WIN + WINW], ebuf[:, E_CMP:E_CMP + NCC]
        s_sel, s_win = PS[:, 5 * 512:5 * 512 + SELW], PS[:, 3 * 512:3 * 512 + WINW]
        s_cmp = bank(7)[:, 128:128 + NCC]
        s_new = PS[:, 5 * 512 + PAST:5 * 512 + SELW]
        pv_nsa = bank(4)[:, 128:320].rearrange("p (b d) -> p b d", b=3)
        pv_dif = bank(4)[:, 320:448]
        joined = bank(2)[:, 0:128]
        ptl = ptb[:, 0:1920].rearrange("p (j r) -> p j r", r=128)
        J_WIN, J_NEW = 8, 12
        G_CMP, G_SEL, G_WIN, G_KD, G_P, G_O, G_PD, G_OD = 0, 8, 12, (14, 26), 22, 34, (35, 38), 41

        def l_out_done(eng, i, n):
            past(eng, l_out[0], i * (L_TP // 2) + n // 2 + 1)
            if n >= 1:
                past(eng, l_out[1], i * (L_TP // 2) + (n + 1) // 2)

        def page_of(eng, i, b, pg):
            return eng.value_load(ptab[0:1, bass.ds(i * (2 * NPAGE) + (b * NPAGE + pg), 1)], min_val=0, max_val=NPOOL - 1)

        def sync_attention(sp, early):
            flat = lambda name: io[name][0].rearrange("n p c g d -> n p (c g d)")
            cmp_d, sel_d, win_d = flat("cache_cmp_kv"), flat("cache_sel_kv"), flat("state_win_kv")
            kd_d = io["cache_diff_k"][0].rearrange("n p h c d -> n p (h c d)")
            def cmp_pages(i, first=False):
                for b in range(2):
                    for k in range(4):
                        for h in range(2):
                            pg = page_of(sp, i, b, 2 * k + h)
                            if h == 0 and not first:
                                past(sp, l_tp, i * L_TP + (4 * b + k + 1 - L_TP))
                            sp.dma_start(cmp_raw[64 * h:64 * h + 64, 4 * b + k], cmp_d[bass.ds(pg, 1)].rearrange("a (p q) n -> (a p) (q n)", q=2)).then_inc(cmp_in[2 * b + k // 2], 16)

            def sel_win_pages(i, first=False):
                for b in range(2):
                    for k in range(2):
                        for h in range(4):
                            pg = page_of(sp, i, b, 4 * k + h)
                            if b + k + h == 0 and not first:
                                past(sp, l_pv, i * 3 - 2)
                            sp.dma_start(sel_raw[:, b, 4 * k + h], sel_d[bass.ds(pg, 1)].rearrange("a p n -> (a p) n")).then_inc(sel_in[2 * b + k], 16)
                for b in range(2):
                    sp.dma_start(win_raw[:, b], win_d[bass.ds(2 * i + b, 1)].rearrange("a (s p) n -> p (a s) n", p=128)).then_inc(win_in[b], 16)

            def dk_pages(i, b, first=False):
                for pg in range(NPAGE):
                    page = page_of(sp, i, b, pg)
                    if not first:
                        past(sp, l_tp, i * L_TP + (G_KD[0] + pg + 1 if b else G_KD[1] + pg + 1 - L_TP))
                    sp.dma_start(dk_raw[:, pg], kd_d[bass.ds(page, 1)].rearrange("a p n -> (a p) n")).then_inc(dk_in[pg // 4], 16)

            if early:
                cmp_pages(0, True)
                sel_win_pages(0, True)
                return
            sp.wait_ge(tp_full, G_END)
            dk_pages(0, 0, True)
            with sp.Fori(1, PAIRS_OF_SEQ) as i:
                cmp_pages(i)
                dk_pages(i - 1, 1)
                sel_win_pages(i)
                dk_pages(i, 0)
            dk_pages(PAIRS_OF_SEQ - 1, 1)
            sync_merge(sp)

        def pool_attention(pool, st):
            vd_d = io["cache_diff_v"][0].rearrange("n p h e -> n p (h e)")
            def values_in(i, b, first=False):
                for pg in range(NPAGE):
                    page = page_of(pool, i, b, pg)
                    if pg == 0 and not first:
                        past(pool, l_pv, i * 3 + (b - 1))
                    pool.dma_start(dv_raw[b][pg], vd_d[bass.ds(page, 1)].rearrange("a p n -> (a p) n")).then_inc(dv_in[2 * b + pg // 4], 16)

            def queries_of(i, first=False):
                if not first:
                    past(pool, l_sc, i * 3)
                for src, dst in ((bd_raw, cur_raw), (bd_rot, cur_rot), (bd_dif, cur_dif)):
                    nc.gpsimd.tensor_copy(dst, src[:, bass.ds(2 * i, 2), :]).then_inc(l_cur, 1)

            arrived(pool, "small")
            pool.wait_ge(pj_full, 15)
            values_in(0, 0, True)
            out_done(pool, G_QK + 14)
            queries_of(0, True)
            pool.wait_ge(tp_full, G_END)
            pool.wait_ge(stored, n_stored)
            values_in(0, 1, True)
            with pool.Fori(1, PAIRS_OF_SEQ) as i:
                values_in(i, 0)
                queries_of(i)
                values_in(i, 1)
            pool_moe(pool, st)

        def pe_attention(pe):
            out_done(pe, G_END - 1)
            with pe.Fori(0, PAIRS_OF_SEQ) as i:
                def tp(n, items):
                    if n >= 2:
                        past(pe, l_out[n % 2], i * (L_TP // 2) + n // 2)
                    else:
                        past(pe, l_out[n % 2], i * (L_TP // 2))
                    for src, col in items:
                        r, c = src.shape[0], src.free_size()
                        last = nc.tensor.transpose(bank(n % 2)[0:c, col:col + r], src, ident[0:r, 0:r])
                    last.then_inc(l_tp, 1)

                for b in range(2):
                    for k in range(4):
                        if k % 2 == 0:
                            pe.wait_ge(cmp_in[2 * b + k // 2], i * 64 + 64)
                        tp(G_CMP + 4 * b + k, [(cmp_raw[:, 4 * b + k, 128 * m:128 * m + 128], 128 * m) for m in range(4)])
                l_out_done(pe, i, 7)
                for c in range(2):
                    for l in range(CB // 2):
                        last = nc.tensor.matmul(bank(2)[:, 4 * NCC * c:4 * NCC * (c + 1)], w1[:, c, l, :],
                                                cmpT[:, 2 * c:2 * c + 2, :, l:l + CS // 2 * (NCC - 1) + 1:CS // 2],
                                                start=(l == 0), stop=(l == CB // 2 - 1))
                last.then_inc(l_hid, 1)
                for b in range(2):
                    for k in range(2):
                        pe.wait_ge(sel_in[2 * b + k], (i + 1) * 64)
                        tp(G_SEL + 2 * b + k, [(sel_raw[:, b, 4 * k + h, 0:128], 128 * h) for h in range(4)])
                for b in range(2):
                    pe.wait_ge(win_in[b], (i + 1) * 16)
                    tp(G_WIN + b, [(win_raw[:, b, h, 0:128], 128 * h) for h in range(4)])
                pe.wait_ge(l_gelu, i + 1)
                for g in range(2):
                    nc.tensor.matmul(bank(2)[64 * g:64 * g + 64, 256:382], w2[:, 0, :], hid[:, 0, g, :], start=True, stop=True)
                for b in range(2):
                    for g in range(2):
                        last = nc.tensor.matmul(bank(3)[0:NCC, 256 + 128 * b + 64 * g:320 + 128 * b + 64 * g],
                                                hid[:, 1, g, NCC * b:NCC * b + NCC], w2[:, 1, :], start=True, stop=True)
                last.then_inc(l_kv, 1)
                pe.wait_ge(l_cur, (i + 1) * 3)
                l_out_done(pe, i, 13)
                past(pe, l_exp, i * 5)
                for k0, w in ((0, 512), (512, 512)):
                    for b in range(2):
                        nc.tensor.matmul(s_sel[64 * b:64 * b + 64, k0:k0 + w], cur_rot[:, b, :], selT[:, b, k0:k0 + w], start=True, stop=True)
                for b in range(2):
                    nc.tensor.matmul(s_sel[64 * b:64 * b + 64, PAST:SELW], cur_rot[:, b, :], ksT[:, SEQ:NTOK], start=True, stop=True)
                pe.wait_ge(l_kv_out, i + 1)
                for b in range(2):
                    nc.tensor.matmul(s_win[64 * b:64 * b + 64, 0:WIN], cur_rot[:, b, :], winT[:, b, :], start=True, stop=True)
                for b in range(2):
                    nc.tensor.matmul(s_win[64 * b:64 * b + 64, WIN:WINW], cur_rot[:, b, :], kwT[:, SEQ:NTOK], start=True, stop=True)
                for b in range(2):
                    last = nc.tensor.matmul(s_cmp[64 * b:64 * b + 64], cur_raw[:, b, :], kcT[:, b, :], start=True, stop=True)
                last.then_inc(l_sc, 1)

                def keys_t(b):
                    for pg in range(NPAGE):
                        if pg % 4 == 0:
                            pe.wait_ge(dk_in[pg // 4], i * 128 + 64 * (b + 1))
                        tp(G_KD[b] + pg, [(dk_raw[:, pg, 128 * h:128 * h + 128], 128 * h) for h in range(4)])
                        if b == 0 and pg == 5:
                            pe.wait_ge(l_pn, i + 1)
                            nc.tensor.matmul(bank(2)[:, 0:NCC], C("rsum"), pn, start=True, stop=True).then_inc(l_grp, 1)

                keys_t(0)
                past(pe, l_exp, i * 5 + 3)
                for k in range(2):
                    tp(G_P + k, [(e_sel[:, 512 * k + 128 * j:512 * k + 128 * j + 128], 128 * j) for j in range(4)])
                tp(G_P + 2, [(e_win[:, 128 * j:128 * j + 128], 128 * j) for j in range(4)])
                tp(G_P + 3, [(ebuf[:, PAST:PAST + 128], 0), (e_win[:, WIN:WINW], 128), (pn, 256)])
                l_out_done(pe, i, G_P + 3)
                for br, n, j0 in ((1, NPAGE, 0), (2, WIN // PAGE, J_WIN), (0, 0, 0)):
                    raw = sel_raw if br == 1 else win_raw
                    for j in range(n + 1):
                        for b in range(2):
                            for g in range(2):
                                r0 = 64 * b + 32 * g
                                out = pv_nsa[r0:r0 + 32, br]
                                if j < n:
                                    last = nc.tensor.matmul(out, ptl[:, j0 + j, r0:r0 + 32], raw[:, b, j, 128 + 64 * g:192 + 64 * g],
                                                            start=(j == 0), stop=False)
                                elif br:
                                    base = (P_SEL if br == 1 else P_WIN) + 128 + 64 * g
                                    last = nc.tensor.matmul(out, ptl[0:NS, J_NEW + br - 1, r0:r0 + 32], proj[0:NS, 2, base:base + 64],
                                                            start=False, stop=True)
                                else:
                                    last = nc.tensor.matmul(out, ptl[0:NCC, J_NEW + 2, r0:r0 + 32], vc[0:NCC, b, 64 * g:64 * g + 64],
                                                            start=True, stop=True)
                last.then_inc(l_pv, 1)

                def dif_scores(b):
                    l_out_done(pe, i, G_KD[b] + 7)
                    past(pe, l_exp, i * 5 + 3 + b)
                    for k0 in (0, 512):
                        for h in range(4):
                            nc.tensor.matmul(s_sel[32 * h:32 * h + 32, k0:k0 + 512], cur_dif[:, b, 32 * h:32 * h + 32], kdT[:, h, k0:k0 + 512], start=True, stop=True)
                    for h in range(4):
                        last = nc.tensor.matmul(s_new[32 * h:32 * h + 32], cur_dif[:, b, 32 * h:32 * h + 32], kdnT[:, h, SEQ:NTOK], start=True, stop=True)
                    last.then_inc(l_sc, 1)

                def dif_values(b):
                    past(pe, l_exp, i * 5 + 4 + b)
                    for k in range(2):
                        tp(G_PD[b] + k, [(e_sel[:, 512 * k + 128 * j:512 * k + 128 * j + 128], 128 * j) for j in range(4)])
                    tp(G_PD[b] + 2, [(ebuf[:, PAST:PAST + 128], 0)])
                    l_out_done(pe, i, G_PD[b] + 2)
                    for k in range(2):
                        pe.wait_ge(dv_in[2 * b + k], i * 64 + 64)
                    if b == 1:
                        pe.wait_ge(l_pv_out, i * 3 + 2)
                    for j in range(NPAGE + 1):
                        for h in range(4):
                            out = pv_dif[32 * h:32 * h + 32]
                            if j < NPAGE:
                                nc.tensor.matmul(out, ptl[:, j, 32 * h:32 * h + 32], dv_raw[b][j][:, 128 * h:128 * h + 128], start=(j == 0), stop=False)
                            else:
                                last = nc.tensor.matmul(out, ptl[0:NS, J_NEW, 32 * h:32 * h + 32], proj[0:NS, 2, P_VD + 128 * h:P_VD + 128 * h + 128], start=False, stop=True)
                    last.then_inc(l_pv, 1)
                    pe.wait_ge(l_on, i * 2 + b + 1)
                    nc.tensor.matmul(joined, cmat, onrm, start=True, stop=True).then_inc(l_join, 1)

                dif_scores(0)
                keys_t(1)
                pe.wait_ge(l_pv_out, i * 3 + 1)
                tp(G_O, [(osm, 0)])
                dif_values(0)
                dif_scores(1)
                dif_values(1)
                pe.wait_ge(l_odn, i + 1)
                tp(G_OD, [(odn[:, b, :], 128 * b) for b in range(2)])
            pe_merge(pe)

        def l_evac(eng, st, i, n, which, copy):
            assert n % 2 == which
            past(eng, l_tp, i * L_TP + n + 1)
            src = bank(n % 2)
            s4 = src.rearrange("p (k n) -> p k n", k=4)
            if n < G_SEL:
                b, k = n // 4, n % 4
                for odd in range(2):
                    for g in range(2):
                        st(copy(cmpT[64 * odd:64 * odd + 64, g:4:2, b, 128 * k:128 * k + 128],
                                s4[64 * g:64 * g + 64, 2 * odd:2 * odd + 2]), l_out[which] if odd and g else None)
            elif n < G_WIN:
                st(copy(selT[:, (n - G_SEL) // 2, 512 * (n % 2):512 * (n % 2) + 512], src), l_out[which])
            elif n < G_KD[0]:
                st(copy(winT[:, n - G_WIN, :], src), l_out[which])
            elif n < G_P or G_KD[1] <= n < G_O:
                b = 0 if n < G_P else 1
                pg = n - G_KD[b]
                if pg < 2:
                    if b == 0:
                        eng.wait_ge(l_hid, i + 1)
                    else:
                        past(eng, l_sc, i * 3 + 2)
                st(copy(kdT[:, :, 128 * pg:128 * pg + 128], s4), l_out[which])
            elif n < G_P + 3:
                j = {0: 0, 1: 4, 2: J_WIN}[n - G_P]
                st(copy(ptl[:, j:j + 4, :], s4), l_out[which])
            elif n == G_P + 3:
                st(copy(ptl[0:NS, J_NEW:J_NEW + 2, :], s4[0:NS, 0:2]))
                st(copy(ptl[0:NCC, J_NEW + 2, :], s4[0:NCC, 2]), l_out[which])
            elif n == G_O:
                for par in range(2):
                    for b in range(2):
                        d = onT[64 * par:64 * par + 64, :, bass.ds(i * 16 + (SEQ + NT * b), NT)]
                        s = src[64 * par:64 * par + 64, 64 * b:64 * b + 64].rearrange("p (k r t) -> p k r t", r=2, t=NT)[:, :, par]
                        st(copy(d, s), l_out[which] if par and b else None)
            elif n == G_OD:
                for b in range(2):
                    d = odT[:, :, bass.ds(i * 16 + (SEQ + NT * b), NT)]
                    s = src[:, 128 * b:128 * b + 128].rearrange("p (h x) -> p h x", h=4)[:, :, 0:NT]
                    st(nc.vector.tensor_scalar(d, s, sg, None, ALU.mult), l_out[which] if b else None)
            else:
                k = (n - G_PD[0]) % 3
                if k < 2:
                    if k == 0 and n == G_PD[0]:
                        past(eng, l_pv, i * 3 + 1)
                    if k == 1 and n == G_PD[0] + 1:
                        past(eng, l_pv, i * 3 + 1)
                    if n >= G_PD[1]:
                        past(eng, l_pv, i * 3 + 2)
                    st(copy(ptl[:, 4 * k:4 * k + 4, :], s4), l_out[which])
                else:
                    past(eng, l_pv, i * 3 + (1 if n < G_PD[1] else 2))
                    st(copy(ptl[0:NS, J_NEW, :], src[0:NS, 0:128]), l_out[which])

        pn = alloc(NCC)
        ACT_PER_TURN = {"l_act": 16, "l_out_act": 21, "l_gelu": 1, "l_exp": 5, "l_sq": 2, "l_root": 1}
        DVE_PER_TURN = {"l_out_dve": 21, "l_dve": 45, "l_osq": 2, "l_kv_out": 1, "l_nmx": 5, "l_pn": 1, "l_pv_out": 3, "l_on": 2, "l_var": 1,
                        "l_odn": 1}

        def act_attention(act, st):
            copy = lambda d, s: nc.scalar.activation(d, s, ACT.Copy)
            before, st = st, Steps(act, l_act, primed)
            with act.Fori(0, PAIRS_OF_SEQ) as i:
                st.enter(i, ACT_PER_TURN)
                ev = lambda *ns: [l_evac(act, st, i, n, 0, copy) for n in ns]

                def exp(k, out, src, sums):
                    act.wait_ge(l_nmx, i * 5 + k + 1)
                    st(nc.scalar.activation(out, src, ACT.Exp, bias=smx[:, k:k + 1], scale=SCALE, accum_out=sums), l_exp)

                ev(0, 2, 4, 6)
                act.wait_ge(l_hid, i + 1)
                for c in range(2):
                    ins = nc.scalar.activation(hid[:, c], bank(2)[:, 4 * NCC * c:4 * NCC * (c + 1)].rearrange("p (g n) -> p g n", g=2),
                                               ACT.Gelu_apprx_tanh, bias=hb[:, c:c + 1])
                    st(ins, l_gelu if c else None)
                    if c == 0:
                        ev(8)
                ev(10, 12, 14, 16)
                exp(0, e_win, s_win, lsum[:, 0:1])
                exp(1, pn, s_cmp, lsum[:, 1:2])
                ev(18, 20)
                exp(2, e_sel, s_sel, lsum[:, 2:3])
                ev(22, 24, 26, 28)
                exp(3, e_sel, s_sel, lsum[:, 3:4])
                ev(30, 32, 34, 36)
                def square(b):
                    act.wait_ge(l_osq, i * 2 + b + 1)
                    st(nc.scalar.activation(sqj, osq[:, b], ACT.Square, accum_out=lsum[:, 5 + b:6 + b]), l_sq)
                square(0)
                exp(4, e_sel, s_sel, lsum[:, 4:5])
                ev(38, 40)
                st.own()
                square(1)
                act.wait_ge(l_var, i + 1)
                st(nc.scalar.activation(lvar, lvar, ACT.Sqrt), l_root)
            st.leave(PAIRS_OF_SEQ)
            act_merge(act, before)

        lsum, lvar, lcf, sqj, osq = alloc(8), alloc(2), alloc(8), alloc(128), alloc(2, 128)

        def dve_attention(dve, st):
            V = nc.vector
            before, st = st, Steps(dve, l_dve, primed)
            arrived(dve, "gS")
            with dve.Fori(0, PAIRS_OF_SEQ) as i:
                st.enter(i, DVE_PER_TURN)
                ev = lambda *ns: [l_evac(dve, st, i, n, 1, V.tensor_copy) for n in ns]

                def negmax(k, s):
                    st.own()
                    st(V.reduce_max(lcf[:, k:k + 1], s, AX))
                    st.own()
                    st(V.tensor_scalar(smx[:, k:k + 1], lcf[:, k:k + 1], -SCALE, None, ALU.mult), l_nmx)

                if True:
                    past(dve, l_exp, i * 5)
                ev(1, 3, 5, 7, 9, 11, 13)
                dve.wait_ge(l_kv, i + 1)
                st(V.tensor_copy(kcT.rearrange("p b n -> p (b n)"), bank(2)[:, 256:382]))
                st(V.tensor_copy(vc[0:NCC].rearrange("p b n -> p (b n)"), bank(3)[0:NCC, 256:512]), l_kv_out)
                past(dve, l_sc, i * 3 + 1)
                st(V.tensor_tensor(s_win[:, 0:NT], s_win[:, 0:NT], C("oldw"), ALU.add))
                newn = C("newn", NB // 2, NS)[:, bass.ds(i, 1), :].rearrange("p a n -> p (a n)")
                st(V.tensor_tensor(s_win[:, WIN:WINW], s_win[:, WIN:WINW], newn, ALU.add))
                st(V.tensor_tensor(s_new, s_new, newn, ALU.add))
                negmax(0, s_win)
                negmax(1, s_cmp)
                ev(15, 17)
                past(dve, l_exp, i * 5 + 2)
                st(V.reciprocal(lcf[:, 1:2], lsum[:, 1:2]))
                st.own()
                st(V.tensor_scalar(pn, pn, lcf[:, 1:2], None, ALU.mult), l_pn)
                ev(19)
                dve.wait_ge(l_grp, i + 1)
                st(V.tensor_copy(pgs[:, 0:NCC], bank(2)[:, 0:NCC]))
                st.own()
                n14 = PAST // SB - 2
                st(V.tensor_tensor(mass, pgs[:, 4:4 + 4 * n14].rearrange("p (a b) -> p a b", b=4),
                                   pgs[:, 3:3 + 4 * n14].rearrange("p (a b) -> p a b", b=4), ALU.add))
                st.own()
                st(V.reduce_sum(imp, mass, AX))
                st.own()
                st(V.tensor_reduce(lcf[:, 5:6], imp, AX, ALU.min))
                st.own()
                st(V.scalar_tensor_tensor(imp, imp, lcf[:, 5:6], C("blk"), ALU.is_equal, ALU.mult))
                st.own()
                st(V.reduce_max(lcf[:, 6:7], imp, AX))
                st.own()
                st(V.tensor_scalar(dropm, C("blk"), lcf[:, 6:7], NEG, ALU.is_equal, ALU.mult))
                st.own()
                mid = s_sel[:, SB:SB + n14 * SB].rearrange("p (a b) -> p a b", b=SB)
                st(V.tensor_tensor(mid, mid, dropm.unsqueeze(2).to_broadcast([128, n14, SB]), ALU.add))
                negmax(2, s_sel)
                ev(21, 23, 25)
                past(dve, l_exp, i * 5 + 3)
                gi = gS[:, bass.ds(i, 1), :].rearrange("p a b -> p (a b)")
                st(V.reciprocal(lcf[:, 0:1], lsum[:, 0:1]))
                st(V.reciprocal(lcf[:, 2:3], lsum[:, 2:3]))
                st.own()
                st(V.tensor_copy(lgt, gi))
                st.own()
                st(V.tensor_tensor(lcf[:, 0:1], lcf[:, 0:1], lgt[:, 2:3], ALU.mult))
                st(V.tensor_tensor(lcf[:, 2:3], lcf[:, 2:3], lgt[:, 1:2], ALU.mult))
                past(dve, l_pv, i * 3 + 1)
                st.own()
                st(V.tensor_scalar(osm[:, 0:64], pv_nsa[:, 0], lgt[:, 0:1], None, ALU.mult))
                st.own()
                st(V.scalar_tensor_tensor(osm[:, 0:64], pv_nsa[:, 1], lcf[:, 2:3], osm[:, 0:64], ALU.mult, ALU.add))
                st.own()
                st(V.scalar_tensor_tensor(osm[:, 0:64], pv_nsa[:, 2], lcf[:, 0:1], osm[:, 0:64], ALU.mult, ALU.add))
                st.own()
                st(V.tensor_copy(osm[:, 64:128], osm[:, 0:64]), l_pv_out)

                def dif_mask(b):
                    past(dve, l_sc, i * 3 + 2 + b)
                    newd = C("newd", NB, NS)[:, bass.ds(2 * i + b, 1), :].rearrange("p a n -> p (a n)")
                    st(V.tensor_tensor(s_new, s_new, newd, ALU.add))
                    negmax(3 + b, s_sel)

                def dif_norm(b):
                    st(V.reciprocal(lcf[:, 3 + b:4 + b], lsum[:, 3 + b:4 + b]))
                    past(dve, l_pv, i * 3 + 2 + b)
                    st.own()
                    st(V.tensor_scalar(onrm, pv_dif, lcf[:, 3 + b:4 + b], None, ALU.mult), l_pv_out)
                    st(V.memset(lcf[:, 7:8], 0.0), l_on)
                    dve.wait_ge(l_join, i * 2 + b + 1)
                    st(V.tensor_copy(osq[:, b], joined), l_osq)

                dif_mask(0)
                ev(27, 29, 31, 33)
                past(dve, l_exp, i * 5 + 4)
                ev(35, 37)
                dif_norm(0)
                dif_mask(1)
                past(dve, l_exp, i * 5 + 5)
                ev(39)
                dif_norm(1)
                dve.wait_ge(l_sq, i * 2 + 2)
                st(V.tensor_scalar(lvar, lsum[:, 5:7], 1.0 / 128, EPS, ALU.mult, ALU.add), l_var)
                dve.wait_ge(l_root, i + 1)
                st(V.reciprocal(lvar, lvar))
                st.own()
                st(V.tensor_tensor(odn, osq, lvar.unsqueeze(2).to_broadcast([128, 2, 128]), ALU.mult), l_odn)
                ev(41)
            st.leave(PAIRS_OF_SEQ)
            dve_merge(dve, before)

        lgt = alloc(3)

        xnT5 = at(6144, KD, NTOK)
        gsig = at(27136, 3, 2 * D)
        x5 = at(33280, 3, D)
        mT = at(36352, KD, NTOK)
        bias16 = at(31744, 1536).bitcast(BF16)
        cstb = at(38912, const_b.shape[1])
        br_n, br_d = at(10240, 4, D), at(14336, 4, D)
        w_out = at(0, KD, D)
        hn, hT6 = at(27136, 3, D), at(24576, KD, NTOK)
        hg, hTm = at(24576, D), at(25600, KD, 2 * BS)
        g1, sg1, u1, av = (at(27648 + 512 * k, 512) for k in range(4))
        aT = [at(29696 + 512 * u, 4, 128) for u in range(2)]
        ysb = [at(30720 + 512 * u, 512) for u in range(2)]
        yk = [at(4096 * t, 4, D) for t in range(3)]
        ROLE = (8192, 16384, 0)
        wring = [at(r, KD, D) for r in ROLE]
        zo = 42440

        def zalloc(*dims):
            nonlocal zo
            zo += int(np.prod(dims))
            assert zo <= 53200, zo
            return at(zo - int(np.prod(dims)), *dims)

        b32, r32 = zalloc(3 * D), zalloc(3 * D)
        mid16 = b32[:, 0:1536].bitcast(BF16)
        nfin = zalloc(D)
        wr, rb, gffn = zalloc(KD, NE), zalloc(NE), zalloc(KD)
        lg, v8, i8 = zalloc(3, NE), zalloc(3, 8), zalloc(3, 8)
        i8u = i8.bitcast(U32)
        i8f, gt, gts = zalloc(3, TOPK), zalloc(3, TOPK), zalloc(3)
        oh, dtmp = zalloc(3, TOPK, NE), zalloc(3, TOPK, NE)
        msk, rk, nb = zalloc(3, NE), zalloc(128), zalloc(128)
        cc, ncol, nr, ovb = zalloc(1), zalloc(1), zalloc(NE), zalloc(NE + 1)
        qq, qa, qb_ = zalloc(3, NE), zalloc(3, NE), zalloc(3, NE)
        ebf, novp, dest = zalloc(NBLK), zalloc(1), zalloc(3, TOPK)
        ebi, novi, desti = zalloc(NBLK).bitcast(I32), zalloc(1).bitcast(I32), zalloc(3 * TOPK).bitcast(U32)
        etmp = zalloc(NBLK_OVER, NE)
        slots = zalloc(NBLK // 2 + 1).bitcast(U32)
        idx = zalloc(1).bitcast(U32)
        ohb = zalloc(NBLK // 2).bitcast(BF16)
        bsel = [zalloc(BS // 2).bitcast(BF16) for _ in range(2)]
        ssf, sq5 = zalloc(9), at(30208, D)
        pad = zalloc(4)
        pairn, slotn = zalloc(3 * TOPK), zalloc(3 * TOPK)
        at_slot, at_pair = b32[:, 0:12 * 2 * BS].rearrange("p (a s) -> p a s", a=12), r32[:, 0:12 * (NBLK // 2)].rearrange("p (a q) -> p a q", a=12)
        pair_cmp = r32[:, 512:512 + 12 * (NBLK // 2 - 1)].rearrange("p (a q) -> p a q", a=12)

        def CB_(name, *dims):
            off, n = at_b[name]
            return at(38912 + off, *(dims or (n,)))

        br_full, m_done, z_full, x2_done = (sem(n) for n in ("br_full", "m_done", "z_full", "x2_done"))
        m_tp, m_out = sem("m_tp"), [sem("m_out_act"), sem("m_out_dve")]
        sq_done, var5, root5, hn_ready = (sem(n) for n in ("sq_done", "var5", "root5", "hn_ready"))
        lg_full, gt_in, gt_exp, msk_ready, rk_full, nb_ready, ov_full = (
            sem(n) for n in ("lg_full", "gt_in", "gt_exp", "msk_ready", "rk_full", "nb_ready", "ov_full"))
        blocks_ready, slots_ready = sem("blocks_ready"), sem("slots_ready")
        pool_clear, marks_ready, pad_done = sem("pool_clear"), sem("marks_ready"), sem("pad_done")
        h_stored, bias_ready = sem("h_stored"), sem("bias_ready")
        e_in = place_in + w_arrived
        e_base = [64 * PAIRS_OF_SEQ] * 8 + [48, 48, 32, 32]
        e_used = sem("e_used")
        hg_in = sem("hg_in")
        i_ready, x_tp, x_out, g_full, u_full, g1_ready, sg_ready, a_ready, a_tp, a_out, yb_full, y_ready = (
            sem(n) for n in ("i_ready", "x_tp", "x_out", "g_full", "u_full", "g1_ready", "sg_ready", "a_ready",
                             "a_tp", "a_out", "yb_full", "y_ready"))
        y_stored, yk_in = [sem(f"y_stored{u}") for u in range(2)], [sem(f"yk_in{t}") for t in range(3)]
        sq8, var8, root8, out_ready, out_stored = (sem(n) for n in ("sq8", "var8", "root8", "out_ready", "out_stored"))
        dx, sum_ready = sem("dve_experts_own"), sem("sum_ready")

        primed += [x_tp, yb_full, a_out, a_ready, y_ready]
        Y_ZEROED = 16 * NBLK_OVER * BS // 256

        V3 = [(t, nh) for t in range(3) for nh in range(2)]

        def m_out_done(eng, n):
            eng.wait_ge(m_out[0], n // 2 + 1)
            if n >= 1:
                eng.wait_ge(m_out[1], (n + 1) // 2)

        wgu = io["w_gate_up"][0].rearrange("e (p k) n -> e p k n", k=KD)
        wdn = io["w_down"][0].rearrange("e (h p k) n -> e p h k n", h=2, k=4)

        def block_weights(eng, e, s):
            role, j = s // 4, s % 4
            if role < 2:
                src = wgu[e, :, 2 * j:2 * j + 2, D * role:D * role + D]
            else:
                src = wdn[e, :, j // 2, 2 * (j % 2):2 * (j % 2) + 2, :]
            if not isinstance(e, int):
                src = src.rearrange("a p k n -> (a p) k n")
            eng.dma_start(wring[role][:, 2 * j:2 * j + 2, :], src).then_inc(e_in[s], 16)

        def sync_merge(sp):
            nonlocal n_stored
            def gate_chunk(j):
                c0, w = CHUNKS[j]
                sp.dma_start(chunk_at(j), w_in[:, :, c0:c0 + w]).then_inc(w_arrived[CHUNK_SLOT[j]], 16)

            sp.wait_ge(l_hid, PAIRS_OF_SEQ)
            gate_chunk(6)
            gate_chunk(7)
            past(sp, l_pv, PAIRS_OF_SEQ * 3 - 2)
            gate_chunk(8)
            past(sp, l_pv, PAIRS_OF_SEQ * 3 - 1)
            load(sp, "xn5", xnT5.rearrange("p k n -> p (k n)"), xn_dram)
            past(sp, l_sc, PAIRS_OF_SEQ * 3)
            gate_chunk(9)
            past(sp, l_tp, PAIRS_OF_SEQ * L_TP)
            past(sp, l_out[1], PAIRS_OF_SEQ * L_TP // 2)
            load(sp, "late", cstb, io["const_b"])
            load(sp, "late", gffn, io["norm_ffn"].rearrange("a (p k) -> p (a k)", k=KD))
            load(sp, "late", wr, io["w_router"][0].rearrange("(p k) e -> p k e", k=KD))
            load(sp, "late", rb, io["b_router"].to_broadcast([128, NE]))
            load(sp, "late", nfin, io["norm_final"].rearrange("(a n) -> a n", a=1).to_broadcast([128, D]))
            for s in range(3):
                load(sp, "bias", b32[32 * s:32 * s + 32, 0:2 * D], io["b_gate_up"][0])
                load(sp, "bias", b32[32 * s:32 * s + 32, 2 * D:3 * D], io["b_down"][0])
            sp.wait_ge(pj_full, 20)
            load(sp, "br", br_n, io["w_br_nsa"][0].rearrange("(k p) n -> p k n", p=128))
            load(sp, "br", br_d, io["w_br_diff"][0].rearrange("(k p) n -> p k n", p=128))
            sp.wait_ge(pj_full, 25)
            for t in range(3):
                load(sp, "late", x5[0:ROWS[t], t, :], x_rows[t])
            load(sp, "wout", w_out, io["w_out"][0].rearrange("(k p) n -> p k n", p=128))
            sp.wait_ge(br_full, 5)
            for s in range(8):
                block_weights(sp, 0, s)
            sp.wait_ge(z_full, 5)
            for s in range(8, 12):
                block_weights(sp, 0, s)
            for t in range(3):
                sp.wait_ge(hn_ready, t + 1)
                sp.dma_start(h_dram[128 * t:128 * t + ROWS[t]], hn[0:ROWS[t], t, :]).then_inc(h_stored, 16)
            for s in range(12):
                sp.wait_ge(e_used, s + 1)
                block_weights(sp, 1, s)
            with sp.Fori(1, NE // 2) as i:
                for u in range(2):
                    for s in range(12):
                        sp.wait_ge(e_used, i * 24 + (12 * (u - 1) + s + 1))
                        block_weights(sp, bass.ds(2 * i + u, 1), s)
            sp.wait_ge(blocks_ready, 1)
            more = sp.value_load(novi[0:1, 0:1], min_val=0, max_val=NBLK_OVER // 2)
            with sp.If(more > 0):
                with sp.Fori(NE // 2, more + NE // 2) as i:
                    for u in range(2):
                        e = sp.value_load(ebi[0:1, bass.ds(2 * i + u, 1)], min_val=0, max_val=NE - 1)
                        for s in range(12):
                            sp.wait_ge(e_used, i * 24 + (12 * (u - 1) + s + 1))
                            block_weights(sp, bass.ds(e, 1), s)
            yp, ys = io["y_prompt"][0], io["y_sample"].rearrange("b t d -> (b t) d")
            for t in range(3):
                sp.wait_ge(out_ready, t + 1)
                sp.dma_start(yp[128 * t:128 * t + 128] if t < 2 else ys, x5[0:ROWS[t], t, :]).then_inc(out_stored, 16)
            sp.wait_ge(out_stored, 48)

        def pool_moe(pool, st):
            G = nc.gpsimd
            for k in range(NE * BS // 128, NBLK * BS // 128):
                pool.dma_start(y_dram[128 * k:128 * k + 128].rearrange("p (c n) -> p c n", n=256),
                               zero.unsqueeze(1).to_broadcast([128, 4, 256])).then_inc(y_stored[k % 2], 16)
            pool.wait_ge(l_odn, PAIRS_OF_SEQ)
            for u in range(2):
                pool.wait_ge(y_stored[u], Y_ZEROED)
            G.memset(pad, 0.0).then_inc(pool_clear, 1)
            pool.wait_ge(slots_ready, 1)
            pool.wait_ge(h_stored, 48)
            pool.wait_ge(blocks_ready, 1)
            more = pool.value_load(novi[0:1, 0:1], min_val=0, max_val=NBLK_OVER // 2)
            def rows_in(column):
                G.indirect_dma_start(out=hg, out_offset=None, in_=h_dram,
                                     in_offset=bass.IndirectOffsetOnAxis(ap=idx, axis=0)).then_inc(hg_in, 16)

            G.tensor_copy(idx, slots[:, 0:1]).then_inc(i_ready, 1)
            pool.wait_ge(i_ready, 1)
            rows_in(0)
            with pool.Fori(0, more + NE // 2) as i:
                past(pool, yb_full, i * 2)
                for u in range(2):
                    G.tensor_copy(bsel[u][0:96], ohb[0:96, bass.ds(2 * i + u, 1)].to_broadcast([96, BS])).then_inc(i_ready, 1)
                pool.wait_ge(hg_in, (i + 1) * 16)
                G.tensor_copy(idx, slots[:, bass.ds(i + 1, 1)]).then_inc(i_ready, 1)
                past(pool, x_tp, i + 1)
                pool.wait_ge(i_ready, i * 4 + 4)
                G.tensor_tensor(pad[:, 0:1], pad[:, 1:2], pad[:, 2:3], ALU.add).then_inc(i_ready, 1)
                rows_in(1)
                for u in range(2):
                    for h in range(2):
                        past(pool, y_ready, i * 2 + (u + 1))
                        pool.dma_start(y_dram[bass.ds(i * (2 * BS) + u * BS, BS), 512 * h:512 * h + 512], ysb[u][64 * h:64 * h + 64]).then_inc(y_stored[u], 16)
            for u in range(2):
                pool.wait_ge(y_stored[u], (more + NE // 2) * 32 + Y_ZEROED)
            G.tensor_tensor(pad[:, 3:4], pad[:, 1:2], pad[:, 2:3], ALU.add).then_inc(pad_done, 1)
            pool.wait_ge(pad_done, 1)
            for t in range(3):
                for k in range(TOPK):
                    r = ROWS[t]
                    G.indirect_dma_start(out=yk[t][0:r, k, :], out_offset=None, in_=y_dram,
                                         in_offset=bass.IndirectOffsetOnAxis(ap=desti[0:r, TOPK * t + k:TOPK * t + k + 1], axis=0)).then_inc(yk_in[t], 16)

        def pe_merge(pe):
            def tp(n, items):
                if n >= 2:
                    pe.wait_ge(m_out[n % 2], n // 2)
                for src, col in items:
                    r, c = src.shape[0], src.free_size()
                    last = nc.tensor.transpose(bank(n % 2)[0:c, col:col + r], src, ident[0:r, 0:r])
                last.then_inc(m_tp, 1)

            l_out_done(pe, PAIRS_OF_SEQ - 1, L_TP - 1)
            arrived(pe, "xn5")
            pe_projection(pe, PAIRS[3:5], 3, xnT5)
            arrived(pe, "br")
            arrived(pe, "br")
            for e in range(2):
                pe.wait_ge(pj_out[e], 15)
            for v in range(5):
                if v >= 3:
                    pe.wait_ge(m_done, v - 2)
                b = 2 + 2 * (v % 3)
                for src, w, bb in ((onT, br_n, b), (odT, br_d, b + 1)):
                    for k in range(4):
                        for v2 in ((v,) if v < 4 else (4, 5)):
                            t, nh = V3[v2]
                            r, p = ROWS[t], 64 * (v2 - 4) if v2 > 4 else 0
                            last = nc.tensor.matmul(bank(bb)[p:p + r], src[:, k, 128 * t:128 * t + r], w[:, k, 512 * nh:512 * nh + 512], start=(k == 0), stop=(k == 3))
                last.then_inc(br_full, 1)
            for v, (t, nh) in enumerate(V3):
                pe.wait_ge(m_done, v + 1)
                tp(v, [(gsig[0:ROWS[t], t, 512 * nh + 128 * k:512 * nh + 128 * k + 128], ROWS[t] * k) for k in range(4)])
            arrived(pe, "wout")
            for v in range(5):
                m_out_done(pe, 2 * (v // 2) + 1)
                for k in range(KD):
                    for v2 in ((v,) if v < 4 else (4, 5)):
                        t, nh = V3[v2]
                        r, p = ROWS[t], 64 * (v2 - 4) if v2 > 4 else 0
                        last = nc.tensor.matmul(bank(2 + v)[p:p + r], mT[:, k, 128 * t:128 * t + r], w_out[:, k, 512 * nh:512 * nh + 512], start=(k == 0), stop=(k == KD - 1))
                last.then_inc(z_full, 1)
            for t in range(3):
                pe.wait_ge(hn_ready, t + 1)
                for half in range(2):
                    tp(6 + 2 * t + half, [(hn[0:ROWS[t], t, 4 * half + k:D:KD], ROWS[t] * k) for k in range(4)])
            arrived(pe, "late")
            pe.wait_ge(x2_done, 6)
            for t in range(3):
                m_out_done(pe, 7 + 2 * t)
                for k in range(KD):
                    last = nc.tensor.matmul(bank(2)[0:ROWS[t], NE * t:NE * t + NE], hT6[:, k, 128 * t:128 * t + ROWS[t]], wr[:, k, :], start=(k == 0), stop=(k == KD - 1))
            last.then_inc(lg_full, 1)
            pe.wait_ge(msk_ready, 1)
            ones, lower = CB_("ones"), CB_("lower")
            for t in range(4):
                terms = [(ones[0:ROWS[s]], msk[0:ROWS[s], s]) for s in range(min(t, 3))]
                if t < 3:
                    terms.append((lower[0:ROWS[t]], msk[0:ROWS[t], t]))
                for n, (l, r) in enumerate(terms):
                    nc.tensor.matmul(bank(3)[:, NE * t:NE * t + NE], l, r, start=(n == 0), stop=(n == len(terms) - 1))
            for t in range(3):
                last = nc.tensor.matmul(bank(3)[0:NE, 128:129], msk[0:ROWS[t], t], ones[0:ROWS[t], 0:1], start=(t == 0), stop=(t == 2))
            last.then_inc(rk_full, 1)
            pe.wait_ge(nb_ready, 1)
            nc.tensor.matmul(bank(4)[:, 0:NE], nb[0:NE], CB_("before")[0:NE], start=True, stop=True)
            nc.tensor.matmul(bank(4)[:, NE:NE + 1], nb[0:NE], ones[0:NE, 0:1], start=True, stop=True).then_inc(ov_full, 1)
            pe.wait_ge(marks_ready, 1)
            for a in range(12):
                r = ROWS[a // TOPK]
                last = nc.tensor.matmul(bank(0)[:, 0:NBLK // 2], at_slot[0:r, a], at_pair[0:r, a], start=(a == 0), stop=(a == 11))
            last.then_inc(m_tp, 1)
            m_out_done(pe, 12)
            pe.wait_ge(blocks_ready, 1)
            pe.wait_ge(bias_ready, 1)
            more = pe.value_load(novi[0:1, 0:1], min_val=0, max_val=NBLK_OVER // 2)
            with pe.Fori(0, more + NE // 2) as i:
                pe.wait_ge(hg_in, (i + 1) * 16)
                past(pe, a_out, i * 2)
                for k in range(KD):
                    last = nc.tensor.transpose(bank(k // 4)[:, 128 * (k % 4):128 * (k % 4) + 128], hg[:, k:D:KD], ident)
                last.then_inc(x_tp, 1)
                pe.wait_ge(i_ready, i * 4 + 3)
                pe.wait_ge(x_out, i + 1)
                for u in range(2):
                    for role, full in ((0, g_full), (1, u_full)):
                        b = 2 + 2 * role + u
                        past(pe, a_ready, i * 2)
                        for k in range(KD):
                            if k % 2 == 0:
                                pe.wait_ge(e_in[4 * role + k // 2], i * 32 + (e_base[4 * role + k // 2] + 16 * (u + 1)))
                            for h in range(2):
                                last = nc.tensor.matmul(bank(b)[64 * h:64 * h + 64], hTm[:, k, BS * u:BS * u + BS], wring[role][:, k, 512 * h:512 * h + 512],
                                                        start=(k == 0), stop=False)
                            if k % 2:
                                last.then_inc(e_used, 1)
                        for h in range(2):
                            last = nc.tensor.matmul(bank(b)[64 * h:64 * h + 64], bsel[u][0:96, 0:BS], bias16[0:96, D * role + 512 * h:D * role + 512 * h + 512],
                                                    start=False, stop=True)
                        last.then_inc(full, 1)
                    past(pe, a_ready, i * 2 + (u + 1))
                    if u:
                        past(pe, a_out, i * 2 + 1)
                    for k in range(4):
                        last = nc.tensor.transpose(bank(1)[:, 128 * k:128 * k + 128], av[:, k:512:4], ident)
                    last.then_inc(a_tp, 1)
                    past(pe, a_out, i * 2 + (u + 1))
                    past(pe, y_ready, i * 2)
                    for c in range(KD):
                        if c % 2 == 0:
                            pe.wait_ge(e_in[8 + c // 2], i * 32 + (e_base[8 + c // 2] + 16 * (u + 1)))
                        for h in range(2):
                            last = nc.tensor.matmul(bank(6 + u)[64 * h:64 * h + 64], aT[u][:, c % 4, 64 * (c // 4):64 * (c // 4) + 64],
                                                    wring[2][:, c, 512 * h:512 * h + 512], start=(c == 0), stop=False)
                        if c % 2:
                            last.then_inc(e_used, 1)
                    for h in range(2):
                        last = nc.tensor.matmul(bank(6 + u)[64 * h:64 * h + 64], bsel[u][0:96, 0:BS], bias16[0:96, 2 * D + 512 * h:2 * D + 512 * h + 512],
                                                start=False, stop=True)
                    last.then_inc(yb_full, 1)

        def act_merge(act, st):
            A = nc.scalar.activation
            for q in (3, 4):
                for s in range(4):
                    j, t = PAIRS[q][s // 2], s % 2
                    act.wait_ge(pj_full, 5 * q + s + 1)
                    st(A(gsig[:, t, 512 * (j - 6):512 * (j - 6) + 512], bank(proj_bank(q, s)), ACT.Sigmoid), pj_out[t])
                act.wait_ge(pj_full, 5 * q + 5)
                for s in range(2):
                    j = PAIRS[q][s]
                    st(A(gsig[0:NS, 2, 512 * (j - 6):512 * (j - 6) + 512], bank(proj_bank(q, 4))[64 * s:64 * s + 64], ACT.Sigmoid), pj_out[s])

            def evac(n, gain):
                act.wait_ge(m_tp, n + 1)
                t, r = (n % 6) // 2, ROWS[(n % 6) // 2]
                for k in range(4 if gain else 1):
                    if gain:
                        st(A(hT6[:, k, 128 * t:128 * t + r], bank(0)[:, r * k:r * k + r], ACT.Copy, scale=gffn[:, k:k + 1]),
                           m_out[0] if k == 3 else None)
                    else:
                        st(A(mT[:, 0:4, 128 * t:128 * t + r], bank(0)[:, 0:4 * r].rearrange("p (k n) -> p k n", k=4), ACT.Copy), m_out[0])

            for n in (0, 2, 4):
                evac(n, False)
            arrived(act, "late")
            for t in range(3):
                r = ROWS[t]
                act.wait_ge(x2_done, 2 * t + 2)
                if t:
                    st.own()
                st(A(sq5[0:r], x5[0:r, t], ACT.Square, accum_out=ssf[0:r, t:t + 1]), sq_done)
                act.wait_ge(var5, t + 1)
                st(A(ssf[0:r, 3 + t:4 + t], ssf[0:r, 3 + t:4 + t], ACT.Sqrt), root5)
            for n in (6, 8, 10):
                evac(n, True)
            act.wait_ge(gt_in, 1)
            st(A(gt, gt, ACT.Exp), gt_exp)
            act.wait_ge(m_tp, 13)
            st(A(slots[:, 0:NBLK // 2], bank(0)[:, 0:NBLK // 2], ACT.Copy), m_out[0])
            act.wait_ge(blocks_ready, 1)
            more = act.value_load(novi[0:1, 0:1], min_val=0, max_val=NBLK_OVER // 2)
            with act.Fori(0, more + NE // 2) as i:
                for u in range(2):
                    act.wait_ge(g1_ready, i * 2 + (u + 1))
                    A(sg1, g1, ACT.Sigmoid, scale=ALPHA).then_inc(sg_ready, 1)
                    act.wait_ge(a_tp, i * 2 + (u + 1))
                    past(act, yb_full, i * 2)
                    A(aT[u], bank(1).rearrange("p (k n) -> p k n", k=4), ACT.Copy).then_inc(a_out, 1)
                    past(act, yb_full, i * 2 + (u + 1))
                    act.wait_ge(y_stored[u], i * 32 + Y_ZEROED)
                    A(ysb[u], bank(6 + u), ACT.Copy).then_inc(y_ready, 1)
            for t in range(3):
                r = ROWS[t]
                act.wait_ge(sum_ready, t + 1)
                st(A(yk[t][0:r, 1, :], x5[0:r, t], ACT.Square, accum_out=ssf[0:r, t:t + 1]), sq8)
                act.wait_ge(var8, t + 1)
                st(A(ssf[0:r, 3 + t:4 + t], ssf[0:r, 3 + t:4 + t], ACT.Sqrt), root8)

        def dve_merge(dve, st):
            V = nc.vector
            for v, (t, nh) in enumerate(V3):
                r, b, p = ROWS[t], 2 + 2 * (min(v, 4) % 3), 64 if v == 5 else 0
                if v == 0:
                    for e in range(2):
                        dve.wait_ge(pj_out[e], 15)
                dve.wait_ge(br_full, min(v, 4) + 1)
                gn = gsig[0:r, t, 512 * nh:512 * nh + 512]
                gd = gsig[0:r, t, D + 512 * nh:D + 512 * nh + 512]
                st(V.tensor_tensor(gn, gn, bank(b)[p:p + r], ALU.mult))
                st(V.tensor_tensor(gd, gd, bank(b + 1)[p:p + r], ALU.mult))
                st.own()
                st(V.tensor_tensor(gn, gn, gd, ALU.add), m_done)
            for n in (1, 3, 5):
                t, r = n // 2, ROWS[n // 2]
                dve.wait_ge(m_tp, n + 1)
                st(V.tensor_copy(mT[:, 4:8, 128 * t:128 * t + r], bank(1)[:, 0:4 * r].rearrange("p (k n) -> p k n", k=4)), m_out[1])
            arrived(dve, "bias")
            dve.wait_ge(m_tp, 6)
            r96 = slice(0, 96)
            st(V.tensor_copy(bias16[r96], b32[r96]))
            st.own()
            st(V.tensor_tensor(r32[r96], b32[r96], bias16[r96], ALU.subtract))
            st.own()
            st(V.tensor_copy(mid16[r96], r32[r96]))
            st.own()
            st(V.tensor_tensor(r32[64:96], r32[64:96], mid16[64:96], ALU.subtract))
            st(V.tensor_copy(bias16[32:64], mid16[32:64]))
            st.own()
            st(V.tensor_copy(bias16[64:96], r32[64:96]), bias_ready)
            arrived(dve, "late")
            for t in range(3):
                r = ROWS[t]
                for nh in range(2):
                    v, p = min(2 * t + nh, 4), 64 if 2 * t + nh == 5 else 0
                    dve.wait_ge(z_full, v + 1)
                    xv = x5[0:r, t, 512 * nh:512 * nh + 512]
                    st(V.tensor_tensor(xv, xv, bank(2 + v)[p:p + r], ALU.add), x2_done)
                dve.wait_ge(sq_done, t + 1)
                s = ssf[0:r, 3 + t:4 + t]
                st(V.tensor_scalar(s, ssf[0:r, t:t + 1], 1.0 / D, EPS, ALU.mult, ALU.add), var5)
                dve.wait_ge(root5, t + 1)
                st(V.reciprocal(s, s))
                st.own()
                if t == 0:
                    dve.wait_ge(z_full, 5)
                st(V.tensor_scalar(hn[0:r, t], x5[0:r, t], s, None, ALU.mult), hn_ready)
            arrived(dve, "late")
            for n in (7, 9, 11):
                t, r = (n - 6) // 2, ROWS[(n - 6) // 2]
                dve.wait_ge(m_tp, n + 1)
                st(V.tensor_tensor(hT6[:, 4:8, 128 * t:128 * t + r], bank(1)[:, 0:4 * r].rearrange("p (k n) -> p k n", k=4),
                                   gffn[:, 4:8].unsqueeze(2).to_broadcast([128, 4, r]), ALU.mult), m_out[1])

            def op(f, *a):
                st(f(*a))
                st.own()

            dve.wait_ge(pool_clear, 1)
            op(V.memset, lg, 0.0)
            arrived(dve, "late")
            arrived(dve, "late")
            dve.wait_ge(lg_full, 1)
            st(V.tensor_tensor(lg[:, 0:2], bank(2)[:, 0:2 * NE].rearrange("p (t e) -> p t e", t=2), rb.unsqueeze(1).to_broadcast([128, 2, NE]), ALU.add))
            op(V.tensor_tensor, lg[0:NS, 2], bank(2)[0:NS, 2 * NE:3 * NE], rb[0:NS], ALU.add)
            for t in range(3):
                op(V.max, v8[:, t], lg[:, t])
                op(V.max_index, i8u.rearrange("p (t k) -> p t k", k=8)[:, t] if len(i8u.shape) == 2 else i8u[:, t], v8[:, t], lg[:, t])
            st(V.tensor_tensor(gt, v8[:, :, 0:TOPK], v8[:, :, 0:1].to_broadcast([128, 3, TOPK]), ALU.subtract), gt_in)
            op(V.tensor_copy, i8f, i8u[:, :, 0:TOPK])
            ex12 = CB_("expert").unsqueeze(1).to_broadcast([128, 12, NE])
            oh12, dt12 = oh.rearrange("p t k e -> p (t k) e"), dtmp.rearrange("p t k e -> p (t k) e")
            op(V.tensor_tensor, oh12, ex12, i8f.rearrange("p t k -> p (t k)").unsqueeze(2).to_broadcast([128, 12, NE]), ALU.is_equal)
            st(V.reduce_sum(msk, oh.rearrange("p t k e -> p t e k"), AX), msk_ready)
            dve.wait_ge(gt_exp, 1)
            op(V.reduce_sum, gts, gt, AX)
            op(V.reciprocal, gts, gts)
            op(V.tensor_tensor, gt, gt, gts.unsqueeze(2).to_broadcast([128, 3, TOPK]), ALU.mult)
            dve.wait_ge(rk_full, 1)
            st(V.tensor_copy(rk, bank(3)[:, 0:128]))
            op(V.tensor_copy, cc[0:NE], bank(3)[0:NE, 128:129])

            def steps_over(out, src, ge):
                cmp = ALU.is_ge if ge else ALU.is_gt
                op(V.tensor_scalar, out, src, float(BS), None, cmp)
                for c in range(2, NTOK // BS if NTOK % BS == 0 else NTOK // BS + 1):
                    op(V.scalar_tensor_tensor, out, src, float(BS * c), out, cmp, ALU.add)

            steps_over(ncol[0:NE], cc[0:NE], False)
            st(V.tensor_copy(nb[0:NE], ncol[0:NE].to_broadcast([NE, 128])), nb_ready)
            steps_over(nr, rk[:, 96:128], False)
            rk3 = rk[:, 0:96].rearrange("p (t e) -> p t e", t=3)
            steps_over(qq, rk3, True)
            dve.wait_ge(ov_full, 1)
            op(V.tensor_copy, ovb, bank(4)[:, 0:NE + 1])
            ovb3 = ovb[:, 0:NE].unsqueeze(1).to_broadcast([128, 3, NE])
            ex3 = CB_("expert").unsqueeze(1).to_broadcast([128, 3, NE])
            op(V.tensor_tensor, qa, qq, ovb3, ALU.add)
            op(V.tensor_tensor, qa, qa, ex3, ALU.subtract)
            op(V.tensor_scalar, qb_, qq, 0.0, None, ALU.is_gt)
            op(V.scalar_tensor_tensor, qa, qa, float(NE - 1), qb_, ALU.add, ALU.mult)
            op(V.tensor_tensor, qa, qa, ex3, ALU.add)
            op(V.scalar_tensor_tensor, qb_, qq, -float(BS), rk3, ALU.mult, ALU.add)
            op(V.scalar_tensor_tensor, qa, qa, float(BS), qb_, ALU.mult, ALU.add)
            for t in range(3):
                op(V.tensor_tensor, dtmp[:, t], oh[:, t], qa[:, t].unsqueeze(1).to_broadcast([128, TOPK, NE]), ALU.mult)
            op(V.reduce_sum, dest.rearrange("p t k -> p (t k)"), dt12, AX)
            st(V.tensor_copy(desti, dest.rearrange("p t k -> p (t k)")))
            pf, sf = pairn.unsqueeze(2), slotn.unsqueeze(2)
            dflat = dest.rearrange("p t k -> p (t k)")
            op(V.tensor_tensor, pair_cmp, dflat.unsqueeze(2).to_broadcast([128, 12, NBLK // 2 - 1]),
               CB_("pair128").unsqueeze(1).to_broadcast([128, 12, NBLK // 2 - 1]), ALU.is_ge)
            op(V.reduce_sum, pairn, pair_cmp, AX)
            op(V.scalar_tensor_tensor, slotn, pairn, -float(2 * BS), dflat, ALU.mult, ALU.add)
            st(V.tensor_tensor(at_slot, CB_("slot").unsqueeze(1).to_broadcast([128, 12, 2 * BS]), sf.to_broadcast([128, 12, 2 * BS]), ALU.is_equal))
            op(V.tensor_tensor, at_pair, CB_("pair").unsqueeze(1).to_broadcast([128, 12, NBLK // 2]), pf.to_broadcast([128, 12, NBLK // 2]), ALU.is_equal)
            st(V.tensor_tensor(at_pair.rearrange("p (t k) q -> p t (k q)", t=3), at_pair.rearrange("p (t k) q -> p t (k q)", t=3),
                               CB_("tokid").unsqueeze(2).to_broadcast([128, 3, TOPK * NBLK // 2]), ALU.mult), marks_ready)
            op(V.tensor_tensor, nr, nr, ovb[:, 0:NE], ALU.add)
            op(V.tensor_tensor, etmp, nr.unsqueeze(1).to_broadcast([128, NBLK_OVER, NE]), CB_("over").unsqueeze(2).to_broadcast([128, NBLK_OVER, NE]), ALU.is_le)
            op(V.reduce_sum, ebf[:, NE:NBLK], etmp, AX)
            op(V.tensor_scalar, ebf[:, NE:NBLK], ebf[:, NE:NBLK], float(NE - 1), None, ALU.min)
            op(V.tensor_copy, ebf[:, 0:NE], CB_("expert"))
            st(V.tensor_copy(ebi, ebf))
            op(V.tensor_scalar, ohb[0:96], ebf[0:96], CB_("pmod")[0:96], None, ALU.is_equal)
            op(V.tensor_scalar, etmp[:, 0, 0:NBLK_OVER // 2], CB_("pairs"), ovb[:, NE:NE + 1], None, ALU.is_lt)
            op(V.reduce_sum, novp, etmp[:, 0, 0:NBLK_OVER // 2], AX)
            st(V.tensor_copy(novi, novp), blocks_ready)
            m_out_done(dve, 12)
            st(V.memset(slots[:, NBLK // 2:NBLK // 2 + 1].bitcast(F32), 0.0), slots_ready)
            dve.wait_ge(blocks_ready, 1)
            more = dve.value_load(novi[0:1, 0:1], min_val=0, max_val=NBLK_OVER // 2)
            before, st = st, Steps(dve, dx, primed)
            with dve.Fori(0, more + NE // 2) as i:
                st.enter(i, {"dve_experts_own": 4, "x_out": 1, "g1_ready": 2, "a_ready": 2})
                past(dve, x_tp, i + 1)
                st(V.tensor_tensor(hTm, PS[:, 0:1024].rearrange("p (k n) -> p k n", k=KD), gffn.unsqueeze(2).to_broadcast([128, KD, 2 * BS]), ALU.mult), x_out)
                for u in range(2):
                    dve.wait_ge(g_full, i * 2 + (u + 1))
                    st(V.tensor_scalar(g1, bank(2 + u), LIM, None, ALU.min), g1_ready)
                    dve.wait_ge(u_full, i * 2 + (u + 1))
                    st(V.tensor_scalar(u1, bank(4 + u), -LIM, LIM, ALU.max, ALU.min))
                    st.own()
                    st(V.scalar_tensor_tensor(u1, u1, 1.0, g1, ALU.add, ALU.mult))
                    dve.wait_ge(sg_ready, i * 2 + (u + 1))
                    st.own()
                    if u:
                        dve.wait_ge(a_tp, i * 2 + 1)
                    st(V.tensor_tensor(av, u1, sg1, ALU.mult), a_ready)
            st.leave(None)
            st = before
            for t in range(3):
                r = ROWS[t]
                y = yk[t]
                dve.wait_ge(yk_in[t], 64)
                op_ = lambda ins: (st(ins), st.own())
                op_(V.tensor_scalar(y[0:r, 0], y[0:r, 0], gt[0:r, t, 0:1], None, ALU.mult))
                for k in range(1, TOPK):
                    op_(V.scalar_tensor_tensor(y[0:r, 0], y[0:r, k], gt[0:r, t, k:k + 1], y[0:r, 0], ALU.mult, ALU.add))
                st(V.tensor_tensor(x5[0:r, t], x5[0:r, t], y[0:r, 0], ALU.add), sum_ready)
                s = ssf[0:r, 3 + t:4 + t]
                dve.wait_ge(sq8, t + 1)
                st(V.tensor_scalar(s, ssf[0:r, t:t + 1], 1.0 / D, EPS, ALU.mult, ALU.add), var8)
                dve.wait_ge(root8, t + 1)
                st(V.reciprocal(s, s))
                st.own()
                if t == 0:
                    arrived(dve, "late")
                st(V.scalar_tensor_tensor(x5[0:r, t], x5[0:r, t], s, nfin[0:r], ALU.mult, ALU.mult), out_ready)

        block = ctx.enter_context(nc.Block())

        @block.sync
        def _(sp):
            nonlocal n_stored

            def store(dst, src):
                nonlocal n_stored
                n_stored += 16
                sp.dma_start(dst, src).then_inc(stored, 16)

            def load_chunk(j, slot, n):
                c0, w = CHUNKS[j]
                sp.dma_start(chunk_at(j)[:, :, 0:w], w_in[:, :, c0:c0 + w]).then_inc(w_arrived[slot], 16)

            for t in range(3):
                load(sp, f"x{t}", xin[0:ROWS[t], t, :], x_rows[t])
            load(sp, "const", cst, io["const_a"])
            load(sp, "const", gmix, io["norm_mix"].rearrange("a (k p) -> p (a k)", p=128),
                 allow_slow_non_contiguous=True)
            for j in range(4):
                load_chunk(j, j, 0)
            load(sp, "small", peraw[0:CB, :], io["cmp_pe"].rearrange("a c (l q) d -> (a c l) (q d)", q=2))
            load(sp, "small", w2, io["w_cmp2"].rearrange("a c h d -> h (a c) d"))
            load(sp, "small", dl, io["diff_lambda"].rearrange("a m d -> a (m d)").to_broadcast([128, 256]))
            load(sp, "small", sg, io["diff_subln"].rearrange("a (p o) -> (a p) o", o=1))
            load(sp, "small", ptab[:, :], io["page_table"].rearrange("(a b) n -> a (b n)", a=1))
            sp.wait_ge(pj_full, 5)
            load_chunk(4, 0, 1)
            load_chunk(5, 1, 1)
            sp.wait_ge(pj_full, 10)
            for c in range(2):
                load(sp, "w1", w1[:, c], io["w_cmp1"][0, c].rearrange("(l p) h -> p l h", p=128))
            arrived(sp, "small")
            sp.wait_ge(pj_full, 15)
            sync_attention(sp, True)
            sp.wait_ge(xn_ready, 6)
            out_done(sp, 5)
            sp.dma_start(xn_dram, xnT.rearrange("p k n -> p (k n)")).then_inc(xn_stored, 16)
            sp.wait_ge(gates_ready, 1)
            store(gate_dram, gates[0:NS, 2, :])

            def rows(name, p0, w):
                inner = io[name]
                return inner, p0, w

            sp.wait_ge(zeroed, 1)
            wp = io["new_win_kv_prompt"].rearrange("a b s c g d -> (a b s) (c g d)")
            for k in range(2):
                store(wp[128 * k:128 * k + 128], zero)
            for b in range(NB):
                store(io["new_win_kv_sample"].rearrange("a b s c g d -> (a b) s (c g d)")[b, 0:WIN - NT],
                      io["state_win_kv"].rearrange("a b s c g d -> (a b) s (c g d)")[b, NT:WIN])
            sp.wait_ge(pj_out[0], 9)
            sp.wait_ge(pj_out[1], 9)
            sp.wait_ge(roped, 5)
            for name, p0, w in (("cmp_kv", P_CMP, 256), ("sel_kv", P_SEL, 256), ("diff_k", P_KD, 512), ("diff_v", P_VD, 512)):
                pr, sa = io[f"new_{name}_prompt"], io[f"new_{name}_sample"]
                fl = "a b s c g d -> (a b s) (c g d)" if len(pr.shape) == 6 else "a b s h d -> (a b s) (h d)"
                for t in range(2):
                    store(pr.rearrange(fl)[128 * t:128 * t + 128], proj[:, t, p0:p0 + w])
                store(sa.rearrange(fl), proj[0:NS, 2, p0:p0 + w])
            for t in range(2):
                store(wp[256 + 128 * t:384 + 128 * t], proj[:, t, P_WIN:P_WIN + 256])
            for b in range(NB):
                store(io["new_win_kv_sample"].rearrange("a b s c g d -> (a b) s (c g d)")[b, WIN - NT:WIN],
                      proj[NT * b:NT * b + NT, 2, P_WIN:P_WIN + 256])
            sp.wait_ge(stored, n_stored)
            for b in range(NB):
                for h in range(8):
                    load(sp, "gS", gS[64 * (b % 2) + 8 * h:64 * (b % 2) + 8 * h + 8, b // 2, :],
                         gate_dram[NT * b:NT * b + NT, 3 * h:3 * h + 3])
            sync_attention(sp, False)

        @block.gpsimd
        def _(pool):
            st = Steps(pool, pool_own)
            for v in (bd_raw, bd_rot, bd_dif, proj[64:128, 2], qraw[64:128, 2], qrot[64:128, 2], qdif[64:128, 2]):
                st(nc.gpsimd.memset(v, 0.0))
                st.own()
            nc.gpsimd.memset(zero, 0.0).then_inc(zeroed, 1)
            for k, s in enumerate(primed):
                nc.gpsimd.memset(primer[:, k:k + 1], 0.0).then_inc(s, 1)
            pool.wait_ge(zeroed, 1)
            pool_attention(pool, st)

        @block.tensor
        def _(pe):
            def tp(n, items):
                if n >= 2:
                    pe.wait_ge(tp_out[n % 2], n // 2)
                for src, col in items:
                    r, c = src.shape[0], src.free_size()
                    last = nc.tensor.transpose(bank(n % 2)[0:c, col:col + r], src, ident[0:r, 0:r])
                last.then_inc(tp_full, 1)

            arrived(pe, "const")
            for t in range(3):
                r = ROWS[t]
                pe.wait_ge(xn_ready, 2 * t + 2)
                for half in range(2):
                    tp(2 * t + half, [(xin[0:r, t, 128 * (4 * half + k):128 * (4 * half + k) + 128], r * k) for k in range(4)])
            arrived(pe, "small")
            tp(G_PE, [(peraw[0:CB, :], 0)])
            out_done(pe, G_PE)
            pe_projection(pe, PAIRS[0:3], 0)

            for n, (t, what) in enumerate(qk_groups):
                r = ROWS[t]
                if n == 0:
                    pe.wait_ge(pj_out[0], 9)
                    pe.wait_ge(pj_out[1], 9)
                pe.wait_ge(roped, {"raw": 0, "rot": 1, "dif": 4, "kd": 5, "kc": 3}[what])
                src = {"raw": qraw[0:r, t], "rot": qrot[0:r, t], "dif": qdif[0:r, t], "kd": proj[0:r, t, P_KD:P_KD + 512]}
                if what == "kc":
                    cols = [P_SEL, P_WIN] + ([P_CMP, P_CMP + 128] if t < 2 else [])
                    tp(G_QK + n, [(proj[0:r, t, c:c + 128], r * k) for k, c in enumerate(cols)])
                else:
                    tp(G_QK + n, [(src[what][:, 128 * k:128 * k + 128], r * k) for k in range(4)])

            arrived(pe, "w1")
            out_done(pe, G_QK + 14)
            for c in range(2):
                for l in range(CB // 2):
                    last = nc.tensor.matmul(bank(7)[:, c:c + 1], w1[:, c, l, :], peT[:, c * (CB // 2) + l:c * (CB // 2) + l + 1],
                                            start=(l == 0), stop=(l == CB // 2 - 1))
            last.then_inc(hb_full, 1)
            for c in range(2):
                for l in range(CB // 2):
                    last = nc.tensor.matmul(bank(2)[:, 2 * NCP * c:2 * NCP * c + 2 * NCP], w1[:, c, l, :],
                                            pcT[:, c, :, l:l + CS // 2 * (NCP - 1) + 1:CS // 2],
                                            start=(l == 0), stop=(l == CB // 2 - 1))
            last.then_inc(ph_full, 1)
            arrived(pe, "small")
            pe.wait_ge(ph_out, 1)
            for g in range(2):
                nc.tensor.matmul(bank(6)[64 * g:64 * g + 64, 0:NCP], w2[:, 0, :], hid[:, 0, g, 0:NCP], start=True, stop=True)
            for g in range(2):
                last = nc.tensor.matmul(bank(6)[0:NCP, 64 + 64 * g:128 + 64 * g], hid[:, 1, g, 0:NCP], w2[:, 1, :], start=True, stop=True)
            last.then_inc(pkv_full, 1)
            pe.wait_ge(pkv_out, 1)

            def scores(u):
                kind, t, g = UNITS[u]
                if u >= 2:
                    pe.wait_ge(s_read, u - 1)
                nk = unit_keys(u)
                b0 = 512 * (2 + 2 * (u % 2))
                for m in range(4):
                    out = PS[:, b0 + 256 * m:b0 + 256 * m + nk]
                    if kind == "dif":
                        h, c = 2 * g + m % 2, m // 2
                        q, k = qTd[64 * c:64 * c + 64, h], kdnT[64 * c:64 * c + 64, h, 0:nk]
                    else:
                        q = (qTraw if kind == "cmp" else qTrot)[64 * g:64 * g + 64, m]
                        k = {"sel": ksT, "win": kwT, "cmp": kcT.rearrange("p b n -> p (b n)")}[kind][64 * g:64 * g + 64, 0:nk]
                    last = nc.tensor.matmul(out, q[:, 128 * t:128 * t + 128], k, start=True, stop=True)
                last.then_inc(s_full, 1)

            def probs_t(u):
                nk, e0 = unit_keys(u), 1024 * (u % 2)
                pe.wait_ge(e_ready, u + 1)
                for j in range(unit_groups(u)):
                    w = min(128, nk)
                    tp(G_UNIT[u] + j, [(ebuf[:, e0 + m * nk + 128 * j:e0 + m * nk + 128 * j + w], 128 * m) for m in range(4)])

            def values(u):
                kind, t, g = UNITS[u]
                out_done(pe, G_UNIT[u + 1] - 1)
                if u >= 2:
                    pe.wait_ge(pv_read, u - 1)
                ng, dv = unit_groups(u), 128 if kind == "dif" else 64
                rows = NCP if kind == "cmp" else 128
                for m in range(4):
                    for j in range(ng):
                        p0 = 1024 * (u % 2) + 512 * j + 128 * m
                        if kind == "cmp":
                            v = vc[0:NCP, 0, 64 * g:64 * g + 64]
                        elif kind == "dif":
                            h = 2 * g + m % 2
                            v = proj[:, j, P_VD + 128 * h:P_VD + 128 * h + 128]
                        else:
                            base = (P_SEL if kind == "sel" else P_WIN) + 128 + 64 * g
                            v = proj[:, j, base:base + 64]
                        last = nc.tensor.matmul(bank(6 + u % 2)[:, dv * m:dv * m + dv], ptb[0:rows, p0:p0 + 128], v,
                                                start=(j == 0), stop=(j == ng - 1))
                last.then_inc(pv_full, 1)

            n = len(UNITS)
            for s in range(n + 2):
                if s < n:
                    scores(s)
                if 1 <= s <= n:
                    probs_t(s - 1)
                if s >= 2:
                    values(s - 2)
            pe.wait_ge(od_ready, 1)
            for t in range(2):
                tp(G_OUT + 2 * t, [(ons[:, t, 128 * k:128 * k + 128], 128 * k) for k in range(4)])
                tp(G_OUT + 2 * t + 1, [(ods[:, t, k, :], 128 * k) for k in range(4)])
            pe_attention(pe)

        def projection_out(eng, st, q, which, copy):
            for s in range(2):
                j = PAIRS[q][s]
                eng.wait_ge(pj_full, 5 * (q % 3) + 2 * s + which + 1)
                place(copy, st, j, which, bank(proj_bank(q, 2 * s + which)), 128, which)
            eng.wait_ge(pj_full, 5 * (q % 3) + 5)
            place(copy, st, PAIRS[q][which], 2, bank(proj_bank(q, 4))[64 * which:64 * which + 64], 64, which)

        def place(copy, st, j, t, src, r, which):
            w = CHUNKS[j][1]
            src = src[:, 0:w]
            if j == 0:
                dst = qraw[0:r, t].rearrange("p (r g d) -> p r g d", r=4, g=2)
                src = src.rearrange("p (g r d) -> p r g d", r=4, g=2)
            elif j == 3:
                dst = qdif[0:r, t]
            else:
                off = {1: P_CMP, 2: P_WIN, 4: P_KD, 5: P_VD}[j]
                dst = proj[0:r, t, off:off + w]
            st(copy(dst, src), pj_out[which])

        def qk_out(st, n, which, copy):
            t, what = qk_groups[n]
            g, r = G_QK + n, ROWS[t]
            src = bank(g % 2)[:, 0:4 * r].rearrange("p (k n) -> p k n", k=4)
            if what == "kc":
                parts = [(ksT[:, 128 * t:128 * t + r], src[:, 0]), (kwT[:, 128 * t:128 * t + r], src[:, 1])]
                if t < 2:
                    for gg in range(2):
                        for odd in range(2):
                            parts.append((pcT[64 * odd:64 * odd + 64, :, gg, 64 * t:64 * t + 64],
                                          src[64 * gg:64 * gg + 64, 2:4, odd:r:2]))
            elif what == "kd":
                parts = [(kdnT[:, :, 128 * t:128 * t + r], src)]
            elif t < 2:
                parts = [({"raw": qTraw, "rot": qTrot, "dif": qTd}[what][:, :, 128 * t:128 * t + r], src)]
            elif what == "dif":
                parts = []
                for c in range(2):
                    d = bd_dif[64 * c:64 * c + 64].rearrange("p b (h x) -> p h b x", h=4)[:, :, :, 8 * c:8 * c + 8]
                    parts.append((d, src[64 * c:64 * c + 64].rearrange("p h (b t) -> p h b t", b=NB)))
            else:
                parts = []
                for gg in range(2):
                    d = (bd_raw if what == "raw" else bd_rot)[64 * gg:64 * gg + 64, :, 32 * gg:32 * gg + 32]
                    parts.append((d.rearrange("p b (r t) -> p r b t", r=4),
                                  src[64 * gg:64 * gg + 64].rearrange("p r (b t) -> p r b t", b=NB)))
            for k, (d, s) in enumerate(parts):
                st(copy(d, s), tp_out[which] if k == len(parts) - 1 else None)

        def prompt_evac(eng, st, u, which, copy):
            if u >= 2:
                eng.wait_ge(pv_full, u - 1)
            for j in range(unit_groups(u)):
                g = G_UNIT[u] + j
                if g % 2 == which:
                    eng.wait_ge(tp_full, g + 1)
                    rows = min(128, unit_keys(u))
                    p0 = 1024 * (u % 2) + 512 * j
                    st(copy(ptb[0:rows, p0:p0 + 512], bank(g % 2)[0:rows, :]), tp_out[which])

        def prompt_out(st, g, t, k, which):
            src = bank(g % 2).rearrange("p (k n) -> p k n", k=4)
            dst = (onT if k == 0 else odT)[:, :, 128 * t:128 * t + 128]
            if k == 0:
                ins = nc.scalar.activation(dst, src, ACT.Copy) if which == 0 else nc.vector.tensor_copy(dst, src)
            else:
                ins = (nc.scalar.activation(dst, src, ACT.Copy, scale=sg) if which == 0
                       else nc.vector.tensor_scalar(dst, src, sg, None, ALU.mult))
            st(ins, tp_out[which])

        @block.scalar
        def _(act):
            st = Steps(act, act_own)
            copy = lambda d, s: nc.scalar.activation(d, s, ACT.Copy)
            def root(v):
                n = st.n.get("root_ready", 0) + 1
                act.wait_ge(var_ready, n)
                st(nc.scalar.activation(v, v, ACT.Sqrt), root_ready)

            for t in range(3):
                arrived(act, f"x{t}")
                st(nc.scalar.activation(at(31232 + 1024 * t, 1024)[0:ROWS[t]], xin[0:ROWS[t], t, :], ACT.Square,
                                        accum_out=ssq[0:ROWS[t], t:t + 1]), squares)
            arrived(act, "const")
            for n in (0, 2, 4):
                t, r = n // 2, ROWS[n // 2]
                root(ssq[0:r, 3 + t:4 + t])
                act.wait_ge(tp_full, n + 1)
                for k in range(4):
                    st(nc.scalar.activation(xnT[:, k, 128 * t:128 * t + r], bank(0)[:, r * k:r * k + r], ACT.Copy,
                                            scale=gmix[:, k:k + 1]), tp_out[0] if k == 3 else None)
            act.wait_ge(tp_full, G_PE + 1)
            st(copy(peT, bank(0)[:, 0:CB]), tp_out[0])
            act.wait_ge(pool_own, 7)
            for q in range(3):
                projection_out(act, st, q, 0, copy)
                if q == 1:
                    act.wait_ge(pj_out[0], 6)
                    act.wait_ge(pj_out[1], 6)
                    nc.scalar.activation(gates, proj[:, :, P_GN:P_GN + 24], ACT.Sigmoid).then_inc(gates_ready, 1)
            for n in range(15):
                if (G_QK + n) % 2 == 0:
                    act.wait_ge(tp_full, G_QK + n + 1)
                    qk_out(st, n, 0, copy)
            act.wait_ge(lam_sums, 1)
            nc.scalar.activation(lam[:, 2:4], lam[:, 0:2], ACT.Exp).then_inc(lam_exp, 1)
            act.wait_ge(hb_full, 1)
            st(copy(hb, bank(7)[:, 0:2]))
            act.wait_ge(ph_full, 1)
            st.own()
            for c in range(2):
                last = nc.scalar.activation(hid[:, c, :, 0:NCP], bank(2)[:, 2 * NCP * c:2 * NCP * c + 2 * NCP].rearrange("p (g n) -> p g n", g=2),
                                            ACT.Gelu_apprx_tanh, bias=hb[:, c:c + 1])
            st(last, ph_out)
            act.wait_ge(pkv_full, 1)
            st(copy(kcT.rearrange("p b n -> p (b n)")[:, 0:NCP], bank(6)[:, 0:NCP]))
            st(copy(vc[0:NCP, 0, :], bank(6)[0:NCP, 64:192]), pkv_out)
            n = len(UNITS)
            for s in range(n + 1):
                if s >= 1:
                    prompt_evac(act, st, s - 1, 0, copy)
                if s < n:
                    nk, e0 = unit_keys(s), 1024 * (s % 2)
                    act.wait_ge(nmx_ready, s + 1)
                    if s >= 4:
                        act.wait_ge(pv_read, s - 3)
                    for m in range(4):
                        e = ebuf[:, e0 + m * nk:e0 + (m + 1) * nk]
                        st(nc.scalar.activation(e, e, ACT.Exp, bias=nmx[:, s % 2, m:m + 1], scale=SCALE,
                                                accum_out=sm[:, s % 4, m:m + 1]), e_ready if m == 3 else None)
            root(ssq)
            for t in range(2):
                for k in range(2):
                    g = G_OUT + 2 * t + k
                    if g % 2 == 0:
                        act.wait_ge(tp_full, g + 1)
                        prompt_out(st, g, t, k, 0)
            act_attention(act, st)

        @block.vector
        def _(dve):
            st = Steps(dve, dve_own)
            V = nc.vector

            def rstd(dst, src, n):
                st(V.tensor_scalar(dst, src, 1.0 / n, EPS, ALU.mult, ALU.add), var_ready)
                dve.wait_ge(root_ready, st.n["var_ready"])
                st(V.reciprocal(dst, dst))
                st.own()

            for t in range(3):
                r = ROWS[t]
                dve.wait_ge(squares, t + 1)
                rstd(ssq[0:r, 3 + t:4 + t], ssq[0:r, t:t + 1], D)
                for half in range(2):
                    v = xin[0:r, t, 512 * half:512 * half + 512]
                    st(V.tensor_scalar(v, v, ssq[0:r, 3 + t:4 + t], None, ALU.mult), xn_ready)
                n = 2 * t + 1
                if t == 0:
                    arrived(dve, "const")
                dve.wait_ge(tp_full, n + 1)
                st(V.tensor_tensor(xnT[:, 4:8, 128 * t:128 * t + r], bank(1)[:, 0:4 * r].rearrange("p (k n) -> p k n", k=4),
                                   gmix[:, 4:8].unsqueeze(2).to_broadcast([128, 4, r]), ALU.mult), tp_out[1])
            arrived(dve, "small")
            l4 = dl.rearrange("p (a b d) -> p a b d", a=2, b=2)
            st(V.tensor_tensor(l4[:, :, 0], l4[:, :, 0], l4[:, :, 1], ALU.mult))
            st.own()
            st(V.reduce_sum(lam[:, 0:2], l4[:, :, 0], AX), lam_sums)
            arrived(dve, "small")
            st(V.tensor_scalar(sg, sg, 1.0 - LAMBDA0, None, ALU.mult))
            dve.wait_ge(pool_own, 7)
            copy = V.tensor_copy

            def rope(src, dst, nh, t0):
                x1, x2 = src[:, :, :, 0:8], src[:, :, :, 8:16]
                cos = C("cos", 3, 8).unsqueeze(2).to_broadcast([128, 3, nh, 8])
                sin = C("sin", 3, 8).unsqueeze(2).to_broadcast([128, 3, nh, 8])
                tmp = [v[:, 0:24 * nh].rearrange("p (t h d) -> p t h d", t=3, h=nh) for v in ropet]
                for d, a, b in ((tmp[0], x1, cos), (tmp[1], x2, sin), (tmp[2], x1, sin), (tmp[3], x2, cos)):
                    st(V.tensor_tensor(d, a, b, ALU.mult))
                st.own()
                st(V.tensor_tensor(dst[:, :, :, 0:8], tmp[0], tmp[1], ALU.subtract))
                st(V.tensor_tensor(dst[:, :, :, 8:16], tmp[2], tmp[3], ALU.add), roped)
                st.own()

            heads = lambda v: v.rearrange("p t (h d) -> p t h d", d=HD)
            projection_out(dve, st, 0, 1, copy)
            dve.wait_ge(pj_out[0], 3)
            st.own()
            st(copy(qrot, qraw))
            st.own()
            rope(heads(qraw), heads(qrot), 8, 0)
            rope(heads(proj[:, :, P_SEL:P_SEL + 128]), heads(proj[:, :, P_SEL:P_SEL + 128]), 2, 0)
            projection_out(dve, st, 1, 1, copy)
            dve.wait_ge(pj_out[0], 6)
            st.own()
            rope(heads(proj[:, :, P_WIN:P_WIN + 128]), heads(proj[:, :, P_WIN:P_WIN + 128]), 2, 0)
            rope(heads(qdif), heads(qdif), 8, 0)
            projection_out(dve, st, 2, 1, copy)
            dve.wait_ge(pj_out[0], 9)
            st.own()
            rope(heads(proj[:, :, P_KD:P_KD + 512]), heads(proj[:, :, P_KD:P_KD + 512]), 8, 0)
            for n in range(15):
                if (G_QK + n) % 2 == 1:
                    dve.wait_ge(tp_full, G_QK + n + 1)
                    qk_out(st, n, 1, copy)
            dve.wait_ge(lam_exp, 1)
            st(V.tensor_tensor(lam[:, 4:5], lam[:, 3:4], lam[:, 2:3], ALU.subtract))
            st.own()
            st(V.tensor_scalar(lam[:, 4:5], lam[:, 4:5], LAMBDA0, None, ALU.subtract))
            st(V.memset(lv[:, 0:2], 1.0))
            st.own()
            st(V.tensor_copy(lv[:, 2:4], lam[:, 4:5].to_broadcast([128, 2])))
            st(V.scalar_tensor_tensor(cmat, C("c1"), lam[:, 4:5], C("c0"), ALU.mult, ALU.add), lam_done)

            def masked(u):
                kind, t, g = UNITS[u]
                nk, e0, b0 = unit_keys(u), 1024 * (u % 2), 512 * (2 + 2 * (u % 2))
                dve.wait_ge(s_full, u + 1)
                if u >= 2:
                    dve.wait_ge(tp_full, G_UNIT[u - 1])
                m = (C("cmpm", 2, NCP) if kind == "cmp" else C("causal", 2, SEQ))[:, t, 0:nk]
                e = ebuf[:, e0:e0 + 4 * nk].rearrange("p (m k) -> p m k", m=4)
                s = PS[:, b0:b0 + 1024].rearrange("p (m k) -> p m k", m=4)[:, :, 0:nk]
                st(V.tensor_tensor(e, s, m.unsqueeze(1).to_broadcast([128, 4, nk]), ALU.add), s_read)
                st.own()
                st(V.reduce_max(mx[:, u % 2], e, AX))
                st.own()
                if u >= 2:
                    dve.wait_ge(e_ready, u - 1)
                st(V.tensor_scalar(nmx[:, u % 2], mx[:, u % 2], -SCALE, None, ALU.mult), nmx_ready)

            def combine(u):
                kind, t, g = UNITS[u]
                c = cf[:, u % 2]
                dve.wait_ge(pv_full, u + 1)
                st(V.reciprocal(c, sm[:, u % 4]))
                st.own()
                if kind == "dif":
                    st(V.tensor_tensor(c, c, lv, ALU.mult))
                else:
                    br = {"cmp": 0, "sel": 1, "win": 2}[kind]
                    st(V.tensor_tensor(c, c, gates[:, t, 12 * g:12 * g + 12].rearrange("p (r b) -> p r b", b=3)[:, :, br], ALU.mult))
                    if kind == "cmp":
                        st.own()
                        st(V.tensor_scalar(c, c, C("cmpv")[:, t:t + 1], None, ALU.mult))
                st.own()
                if kind == "dif":
                    pv = bank(6 + u % 2).rearrange("p (m e) -> p m e", m=4)
                    tm = pvt.rearrange("p (m e) -> p m e", m=4)
                    st(V.tensor_tensor(tm, pv, c.unsqueeze(2).to_broadcast([128, 4, 128]), ALU.mult), pv_read)
                    st.own()
                    st(V.tensor_tensor(ods[:, t, 2 * g:2 * g + 2, :], tm[:, 0:2], tm[:, 2:4], ALU.add))
                else:
                    pv = bank(6 + u % 2)[:, 0:256].rearrange("p (m e) -> p m e", m=4)
                    dst = ons[:, t, 256 * g:256 * g + 256].rearrange("p (m e) -> p m e", m=4)
                    out = dst if kind == "sel" else pvt[:, 0:256].rearrange("p (m e) -> p m e", m=4)
                    st(V.tensor_tensor(out, pv, c.unsqueeze(2).to_broadcast([128, 4, 64]), ALU.mult), pv_read)
                    if kind != "sel":
                        st.own()
                        st(V.tensor_tensor(dst, dst, out, ALU.add))
                st.own()

            dve.wait_ge(gates_ready, 1)
            dve.wait_ge(xn_stored, 16)
            n = len(UNITS)
            for s in range(n + 2):
                if s < n:
                    masked(s)
                if 1 <= s <= n:
                    prompt_evac(dve, st, s - 1, 1, copy)
                if s >= 2:
                    combine(s - 2)
            sq = at(24576, 1024)
            st(V.tensor_tensor(sq, ods.rearrange("p t h e -> p (t h e)"), ods.rearrange("p t h e -> p (t h e)"), ALU.mult))
            st.own()
            st(V.reduce_sum(ssq, sq.rearrange("p (a e) -> p a e", e=128), AX))
            st.own()
            rstd(ssq, ssq, 128)
            o8 = ods.rearrange("p t h e -> p (t h) e")
            st(V.tensor_tensor(o8, o8, ssq.unsqueeze(2).to_broadcast([128, 8, 128]), ALU.mult), od_ready)
            for t in range(2):
                for k in range(2):
                    g = G_OUT + 2 * t + k
                    if g % 2 == 1:
                        dve.wait_ge(tp_full, g + 1)
                        prompt_out(st, g, t, k, 1)
            dve_attention(dve, st)


_INS = ['x_prompt', 'x_sample', 'cache_cmp_kv', 'cache_sel_kv', 'state_win_kv', 'cache_diff_k', 'cache_diff_v',
        'page_table', 'norm_mix', 'w_in', 'cmp_pe', 'w_cmp1', 'w_cmp2', 'diff_lambda', 'diff_subln', 'w_br_nsa',
        'w_br_diff', 'w_out', 'norm_ffn', 'w_router', 'b_router', 'w_gate_up', 'b_gate_up', 'w_down', 'b_down',
        'norm_final']
_OUTS = [('y_prompt', (1, SEQ, D)), ('y_sample', (NB, NT, D)),
         ('new_cmp_kv_prompt', (1, 1, SEQ, 2, 2, HD)), ('new_cmp_kv_sample', (1, NB, NT, 2, 2, HD)),
         ('new_sel_kv_prompt', (1, 1, SEQ, 2, 2, HD)), ('new_sel_kv_sample', (1, NB, NT, 2, 2, HD)),
         ('new_win_kv_prompt', (1, 1, WIN, 2, 2, HD)), ('new_win_kv_sample', (1, NB, WIN, 2, 2, HD)),
         ('new_diff_k_prompt', (1, 1, SEQ, 4, 2, HD)), ('new_diff_k_sample', (1, NB, NT, 4, 2, HD)),
         ('new_diff_v_prompt', (1, 1, SEQ, 4, 128)), ('new_diff_v_sample', (1, NB, NT, 4, 128))]


def kernel(**inputs):
    import numpy as _np
    import concourse.bacc as _bacc
    from concourse import mybir as _mybir
    from concourse.bass_utils import run_bass_kernel_spmd as _run

    nc = _bacc.Bacc("TRN2", target_bir_lowering=False, num_devices=1)
    const_a, at_a, const_b, at_b = shape_constants()
    arrays, io = {}, {}
    for name in _INS:
        a = _np.ascontiguousarray(inputs[name])
        arrays["in_" + name] = a
        io[name] = nc.dram_tensor("in_" + name, a.shape, _mybir.dt.from_np(a.dtype), kind="ExternalInput").ap()
    for name, a in (("const_a", const_a), ("const_b", const_b)):
        arrays["in_" + name] = a
        io[name] = nc.dram_tensor("in_" + name, a.shape, _mybir.dt.from_np(a.dtype), kind="ExternalInput").ap()
    for name, shape in _OUTS:
        io[name] = nc.dram_tensor("out_" + name, shape, F32, kind="ExternalOutput").ap()
    build(nc, io, const_a, at_a, const_b, at_b)
    r = _run(nc, [arrays], core_ids=[0])
    return tuple(r.results[0]["out_" + name] for name, _ in _OUTS)
```

```python
import numpy as np
import concourse.bass as bass
from concourse import mybir
from contextlib import ExitStack

F32 = mybir.dt.float32
BF16 = mybir.dt.bfloat16
I32 = mybir.dt.int32
U32 = mybir.dt.uint32
ALU = mybir.AluOpType
ACT = mybir.ActivationFunctionType
AX = mybir.AxisListType.X

D = 1024
KD = D // 128
SEQ = 256
NB, NT = 8, 8
NS = NB * NT
NTOK = SEQ + NS
ROWS = (128, 128, NS)
PAST, PAGE = 1024, 128
NPAGE = PAST // PAGE
NPOOL = (5 * NB * NPAGE + 3) // 4
WIN = 512
HD = 64
SCALE = HD ** -0.5
EPS = 1e-5
CB, CS = 32, 16
NCP = (SEQ - CB) // CS + 1
NCC = (PAST + NT - CB) // CS + 1
SB = 64
NE, TOPK, DFF = 32, 4, 1024
LIM, ALPHA = 7.0, 1.702
LAMBDA0 = 0.8 - 0.6 * 1.0
NEG = -1e30
THETA = 500000.0

CHUNKS = ((0, 512), (512, 512), (1024, 280), (1304, 512), (1816, 512), (2328, 512),
          (2840, 512), (3352, 512), (3864, 512), (4376, 512))
P_CMP, P_SEL, P_WIN, P_GN, P_KD, P_VD, PW = 0, 256, 512, 768, 792, 1304, 1816

BS = 64
NBLK_OVER = 20
NBLK = NE + NBLK_OVER


def shape_constants():
    f = np.float32
    p = np.arange(128)
    tok = np.stack([p, 128 + p, PAST + p % NT])
    half = HD // 8
    inv = (f(THETA) ** (-np.arange(half, dtype=f) / f(half))).astype(f)
    ang = tok.astype(f)[:, :, None] * inv
    cos, sin = np.cos(ang).astype(f), np.sin(ang).astype(f)
    a = {}
    a["ident"] = np.eye(128)
    k = np.arange(SEQ)
    a["causal"] = np.where(k[None, None] <= tok[:2, :, None], 0, NEG).transpose(1, 0, 2).reshape(128, -1)
    ends = np.arange(NCP) * CS + CB - 1
    a["cmpm"] = np.where(ends[None, None] <= tok[:2, :, None], 0, NEG).transpose(1, 0, 2).reshape(128, -1)
    a["cmpv"] = (tok[:2] >= CB - 1).T
    a["cos"] = cos.transpose(1, 0, 2).reshape(128, -1)
    a["sin"] = sin.transpose(1, 0, 2).reshape(128, -1)
    kb, kt = np.arange(NS) // NT, np.arange(NS) % NT
    t = p % NT
    nsa = np.full((128, NB // 2, NS), NEG)
    for i in range(NB // 2):
        b = 2 * i + p // 64
        nsa[:, i] = np.where((kb[None] == b[:, None]) & (kt[None] <= t[:, None]), 0, NEG)
    a["newn"] = nsa.reshape(128, -1)
    dif = np.full((128, NB, NS), NEG)
    for b in range(NB):
        dif[:, b] = np.where((kb[None] == b) & (kt[None] <= t[:, None]), 0, NEG)
    a["newd"] = dif.reshape(128, -1)
    a["oldw"] = np.where(np.arange(NT)[None] > t[:, None], 0, NEG)
    a["rsum"] = (p[:, None] // 32 == p[None] // 32) & (t[:, None] == t[None])
    row, col = p[:, None], p[None]
    own = (row // 32 == col // 32) & (col % 32 < NT)
    a["c0"] = own & (row % 32 == col % 32)
    a["c1"] = own & (row % 32 == col % 32 + NT)
    a["blk"] = np.tile(np.arange(1, PAST // SB - 1), (128, 1))
    d = {}
    d["lower"] = row < col
    d["ones"] = np.ones((128, 128))
    d["before"] = np.where((row < col) & (row < NE), 1, 0)[:, :NE]
    d["expert"] = np.tile(np.arange(NE), (128, 1))
    d["over"] = np.tile(np.arange(NBLK_OVER), (128, 1))
    d["pairs"] = np.tile(2 * np.arange(NBLK_OVER // 2), (128, 1))
    d["pmod"] = (p % NE)[:, None]
    d["pair128"] = np.tile(2 * BS * np.arange(1, NBLK // 2), (128, 1))
    d["slot"] = np.tile(np.arange(2 * BS), (128, 1))
    d["pair"] = np.tile(np.arange(NBLK // 2), (128, 1))
    d["tokid"] = np.stack([p, 128 + p, SEQ + p], 1)
    out = []
    for group in (a, d):
        at, where = 0, {}
        for name, v in group.items():
            where[name] = (at, v.shape[1])
            at += v.shape[1]
        out += [np.ascontiguousarray(np.concatenate([np.asarray(v, f) for v in group.values()], 1)), where]
    return out


class Steps:

    def __init__(self, eng, own, primed=()):
        self.eng, self.default, self.base, self.last = eng, own, {}, None
        self.n = {s.name: 1 for s in primed}

    def __call__(self, ins, sem=None):
        sem = sem or self.default
        self.n[sem.name] = self.n.get(sem.name, 0) + 1
        ins.then_inc(sem, 1)
        self.last = (sem, self.n[sem.name])

    def own(self):
        sem, n = self.last
        self.eng.wait_ge(sem, self.base.get(sem.name, 0) + n)

    def enter(self, i, per):
        self.start, self.per = dict(self.n), per
        self.base = {s: i * k for s, k in per.items()}

    def leave(self, trips):
        for s in set(self.n) | set(self.per):
            k = self.per.get(s, 0)
            got = self.n.get(s, 0) - self.start.get(s, 0)
            assert got == k, (s, got, k, {q: self.n[q] - self.start.get(q, 0) for q in self.n})
            self.n[s] = self.start.get(s, 0) + (trips * k if trips else 0)
        self.base, self.last = {}, None


def build(nc, io, const_a, at_a, const_b, at_b):
    ctx = ExitStack()
    with ctx:
        sem = lambda name: ctx.enter_context(nc.semaphore(name))
        arena = ctx.enter_context(nc.sbuf_tensor("arena", [128, 53200], F32))
        PS = ctx.enter_context(nc.psum_tensor("PS", [128, 8 * 512], F32))

        def at(off, *dims):
            n = int(np.prod(dims))
            v = arena[:, off:off + n]
            if len(dims) == 2:
                return v.rearrange("p (a b) -> p a b", b=dims[1])
            if len(dims) == 3:
                return v.rearrange("p (a b c) -> p a b c", b=dims[1], c=dims[2])
            if len(dims) == 4:
                return v.rearrange("p (a b c d) -> p a b c d", b=dims[1], c=dims[2], d=dims[3])
            return v

        def bank(k, n=512, off=0):
            return PS[:, 512 * k + off:512 * k + off + n]

        wslot = [at(4096 * s, KD, 512) for s in range(4)]
        sel_raw = at(0, 2, NPAGE, 256)
        win_raw = at(4096, 2, WIN // PAGE, 256)
        dv_raw = [[at(6144 + 512 * j, 512) for j in range(NPAGE)],
                  [at(34304 + 512 * j if j < NPAGE - 1 else 30720, 512) for j in range(NPAGE)]]
        w1 = at(10240, 2, CB // 2, 128)
        xin = at(18432, 3, D)
        hrows = at(18432, 3, 256)
        cmpT = at(18432, 4, 2, PAST // 2)
        kdT = at(18432, 4, PAST)
        xnT = at(22528, KD, NTOK)
        ropet = [at(25088 + 384 * k, 384) for k in range(4)]
        ebuf = at(22528, 2048)
        ptb = at(24576, 2048)
        qraw, qrot, qdif = (at(26624 + 1536 * k, 3, 512) for k in range(3))
        ons, ods = at(19456, 2, 512), at(20480, 2, 4, 128)
        pvt = at(21504, 512)
        cmp_raw = at(14336, NPAGE, 512)
        dk_raw = at(26624, NPAGE, 512)
        qTraw, qTrot, qTd = (at(31232 + 1024 * k, 4, SEQ) for k in range(3))
        winT, selT = at(31232, 2, WIN), at(32256, 2, PAST)
        proj = at(34304, 3, PW)
        onT, odT = at(39752, 4, NTOK), at(41032, 4, NTOK)
        cst = at(42312, const_a.shape[1])
        o = 42312 + const_a.shape[1]

        def alloc(*dims):
            nonlocal o
            o += int(np.prod(dims))
            assert o <= 53200, o
            return at(o - int(np.prod(dims)), *dims)

        cmat = alloc(128)
        bd_raw, bd_rot, bd_dif = alloc(NB, 64), alloc(NB, 64), alloc(NB, 128)
        cur_raw, cur_rot, cur_dif = alloc(2, 64), alloc(2, 64), alloc(2, 128)
        ksT, kwT, kdnT = alloc(NTOK), alloc(NTOK), alloc(4, NTOK)
        hid = alloc(2, 2, 126)
        kcT, vc = alloc(2, NCC), alloc(2, 128)
        pcT, w2 = alloc(2, 2, SEQ // 2), alloc(2, 64)
        gmix, sg, hb, peT = alloc(KD), alloc(1), alloc(2), alloc(CB)
        ssq, lam, lv = alloc(8), alloc(8), alloc(4)
        gates, gS = alloc(3, 24), alloc(NB // 2, 3)
        mx, nmx, sm, cf = alloc(2, 4), alloc(2, 4), alloc(4, 4), alloc(2, 4)
        dl, peraw = alloc(256), alloc(128)
        osm, onrm, odn = alloc(128), alloc(128), alloc(2, 128)
        pgs, mass, imp, dropm = alloc(NCC + 1), alloc(14, 4), alloc(14), alloc(14)
        smx, primer = alloc(8), alloc(12)
        zero = alloc(256)
        ptab = alloc(NB * NPAGE)[0:1, :].bitcast(I32)

        def const(name, *dims):
            off, n = at_a[name]
            return at(42312 + off, *(dims or (n,)))

        ident = const("ident")

        xn_dram = nc.dram_tensor("xn_scratch", [128, KD * NTOK], F32, kind="Internal").ap()
        gate_dram = nc.dram_tensor("gate_scratch", [NS, 24], F32, kind="Internal").ap()
        h_dram = nc.dram_tensor("h_scratch", [NTOK, D], F32, kind="Internal").ap()
        y_dram = nc.dram_tensor("y_scratch", [NBLK * BS, D], F32, kind="Internal").ap()

        w_in = io["w_in"][0].rearrange("(k p) n -> p k n", p=128)
        x_rows = [io["x_prompt"][0, 0:128], io["x_prompt"][0, 128:256],
                  io["x_sample"].rearrange("b t d -> (b t) d")]

        loaded = {}

        def load(eng, name, dst, src, **kw):
            if name not in loaded:
                loaded[name] = [sem("load_" + name), 0]
            loaded[name][1] += 16
            eng.dma_start(dst, src, **kw).then_inc(loaded[name][0], 16)

        def arrived(eng, name):
            eng.wait_ge(loaded[name][0], loaded[name][1])

        stored = sem("stored")
        n_stored = 0
        w_arrived = [sem(f"w_arrived{s}") for s in range(4)]
        tp_full = sem("tp_full")
        tp_out = [sem("tp_out_act"), sem("tp_out_dve")]
        pj_full = sem("pj_full")
        pj_out = [sem("pj_out_act"), sem("pj_out_dve")]
        var_ready, root_ready = sem("var_ready"), sem("root_ready")
        act_own, dve_own, pool_own = sem("act_own"), sem("dve_own"), sem("pool_own")
        squares = sem("squares")
        xn_stored = sem("xn_stored")
        xn_ready = sem("xn_ready")
        zeroed = sem("zeroed")
        roped = sem("roped")
        gates_ready = sem("gates_ready")
        lam_sums, lam_exp, lam_done = sem("lam_sums"), sem("lam_exp"), sem("lam_done")
        ph_full, ph_out, pkv_full, pkv_out = (sem(n) for n in ("ph_full", "ph_out", "pkv_full", "pkv_out"))
        s_full, s_read, nmx_ready, e_ready = (sem(n) for n in ("s_full", "s_read", "nmx_ready", "e_ready"))
        pv_full, pv_read = sem("pv_full"), sem("pv_read")
        od_ready = sem("od_ready")

        CHUNK_SLOT = (0, 1, 2, 3, 0, 1, 2, 3, 0, 1)
        CHUNK_USE = (1, 1, 1, 1, 2, 2, 2, 2, 3, 3)

        def chunk_at(j):
            return {6: at(10240, KD, 512), 7: at(14336, KD, 512), 9: at(18432, KD, 512)}.get(j, wslot[CHUNK_SLOT[j]])

        PAIRS = tuple((2 * q, 2 * q + 1) for q in range(5))

        def proj_bank(q, slot):
            return (2, 3, 5, 6, 4 if q % 2 == 0 else 7)[slot]

        UNITS = [(kind, t, g) for t in range(2) for kind in ("sel", "win", "cmp", "dif") for g in range(2)]

        def unit_keys(u):
            kind, t, _ = UNITS[u]
            return NCP if kind == "cmp" else 128 * (t + 1)

        def unit_groups(u):
            kind, t, _ = UNITS[u]
            return 1 if kind == "cmp" else t + 1

        qk_groups = [(t, what) for t in range(3) for what in ("raw", "rot", "dif", "kd", "kc")]
        G_PE = 6
        G_QK = G_PE + 1
        G_UNIT = [G_QK + len(qk_groups) + sum(unit_groups(v) for v in range(u)) for u in range(len(UNITS) + 1)]
        G_OUT = G_UNIT[-1]
        G_END = G_OUT + 4

        def out_done(eng, n, sems=tp_out):
            eng.wait_ge(sems[0], n // 2 + 1)
            if n >= 1:
                eng.wait_ge(sems[1], (n + 1) // 2)

        def pe_projection(pe, pairs, first, xnT=xnT):
            for n, (j0, j1) in enumerate(pairs):
                q = first + n
                for s, j in enumerate((j0, j1)):
                    w, slot = CHUNKS[j][1], CHUNK_SLOT[j]
                    pe.wait_ge(w_arrived[slot], 16 * CHUNK_USE[j])
                    for t in range(2):
                        if n >= 1:
                            pe.wait_ge(pj_out[t], 3 * (q - 1) + s + 1)
                        for k in range(KD):
                            last = nc.tensor.matmul(bank(proj_bank(q, 2 * s + t))[:, 0:w], xnT[:, k, 128 * t:128 * t + 128],
                                                    chunk_at(j)[:, k, 0:w], start=(k == 0), stop=(k == KD - 1))
                        last.then_inc(pj_full, 1)
                if n >= 2:
                    for e in range(2):
                        pe.wait_ge(pj_out[e], 3 * (q - 1))
                for k in range(KD):
                    for s, j in enumerate((j0, j1)):
                        w = CHUNKS[j][1]
                        last = nc.tensor.matmul(bank(proj_bank(q, 4))[64 * s:64 * s + 64, 0:w], xnT[:, k, 256:NTOK],
                                                chunk_at(j)[:, k, 0:w], start=(k == 0), stop=(k == KD - 1))
                last.then_inc(pj_full, 1)

        PAIRS_OF_SEQ = NB // 2
        L_TP = 42
        place_in = [sem(f"place_in{k}") for k in range(8)]
        cmp_in = place_in[0:4]
        sel_in = place_in[4:8]
        dk_in = [sem(f"dk_in{k}") for k in range(2)]
        win_in = [sem(f"win_in{k}") for k in range(2)]
        dv_in = [sem(f"dv_in{k}") for k in range(4)]
        l_tp, l_out = sem("l_tp"), [sem("l_out_act"), sem("l_out_dve")]
        l_hid, l_gelu, l_kv, l_kv_out = sem("l_hid"), sem("l_gelu"), sem("l_kv"), sem("l_kv_out")
        l_cur = sem("l_cur")
        l_sc = sem("l_sc")
        l_nmx, l_exp = sem("l_nmx"), sem("l_exp")
        l_pn, l_grp = sem("l_pn"), sem("l_grp")
        l_pv, l_pv_out = sem("l_pv"), sem("l_pv_out")
        l_on, l_join, l_osq, l_sq, l_var, l_root, l_odn = (sem(n) for n in ("l_on", "l_join", "l_osq", "l_sq", "l_var", "l_root", "l_odn"))
        l_act, l_dve = sem("l_act"), sem("l_dve")
        primed = [l_tp, l_out[0], l_out[1], l_sc, l_exp, l_pv]

        def past(eng, s, n):
            eng.wait_ge(s, n + 1)


        SELW, WINW = PAST + NS, WIN + NS
        E_SEL, E_WIN, E_CMP = 0, SELW, SELW + WINW
        e_sel, e_win, e_cmp = ebuf[:, 0:SELW], ebuf[:, E_WIN:E_WIN + WINW], ebuf[:, E_CMP:E_CMP + NCC]
        s_sel, s_win = PS[:, 5 * 512:5 * 512 + SELW], PS[:, 3 * 512:3 * 512 + WINW]
        s_cmp = bank(7)[:, 128:128 + NCC]
        s_new = PS[:, 5 * 512 + PAST:5 * 512 + SELW]
        pv_nsa = bank(4)[:, 128:320].rearrange("p (b d) -> p b d", b=3)
        pv_dif = bank(4)[:, 320:448]
        joined = bank(2)[:, 0:128]
        ptl = ptb[:, 0:1920].rearrange("p (j r) -> p j r", r=128)
        J_WIN, J_NEW = 8, 12
        G_KD, G_CMP, G_PD, G_SEL, G_WIN, G_P, G_O, G_OD = (0, 25), 8, (16, 38), 19, 23, 33, 37, 41

        def l_out_done(eng, i, n):
            past(eng, l_out[0], i * (L_TP // 2) + n // 2 + 1)
            if n >= 1:
                past(eng, l_out[1], i * (L_TP // 2) + (n + 1) // 2)

        def page_of(eng, i, b, pg):
            return eng.value_load(ptab[0:1, bass.ds(i * (2 * NPAGE) + (b * NPAGE + pg), 1)], min_val=0, max_val=NPOOL - 1)

        def sync_attention(sp, early):
            flat = lambda name: io[name][0].rearrange("n p c g d -> n p (c g d)")
            cmp_d, sel_d, win_d = flat("cache_cmp_kv"), flat("cache_sel_kv"), flat("state_win_kv")
            kd_d = io["cache_diff_k"][0].rearrange("n p h c d -> n p (h c d)")
            def cmp_pages(i, first=False):
                for b in range(2):
                    for k in range(4):
                        for h in range(2):
                            pg = page_of(sp, i, b, 2 * k + h)
                            if h == 0 and not first:
                                past(sp, l_tp, i * L_TP + (G_CMP + 4 * b + k + 1 - L_TP))
                            for q in range(2):
                                sp.dma_start(cmp_raw[64 * h:64 * h + 64, 4 * b + k].rearrange("p (m q d) -> p q m d", m=4, q=2)[:, q],
                                             cmp_d[bass.ds(pg, 1)].rearrange("a (p q) (m d) -> (a p) q m d", q=2, m=4)[:, q]).then_inc(cmp_in[2 * b + k // 2], 16)

            def sel_win_pages(i, first=False):
                for b in range(2):
                    for k in range(2):
                        for h in range(4):
                            pg = page_of(sp, i, b, 4 * k + h)
                            if b + k + h == 0 and not first:
                                past(sp, l_pv, i * 3 - 1)
                            sp.dma_start(sel_raw[:, b, 4 * k + h], sel_d[bass.ds(pg, 1)].rearrange("a p n -> (a p) n")).then_inc(sel_in[2 * b + k], 16)
                for b in range(2):
                    sp.dma_start(win_raw[:, b], win_d[bass.ds(2 * i + b, 1)].rearrange("a (s p) n -> p (a s) n", p=128)).then_inc(win_in[b], 16)

            def dk_pages(i, b, first=False):
                for pg in range(NPAGE):
                    page = page_of(sp, i, b, pg)
                    if not first:
                        past(sp, l_tp, i * L_TP + (G_KD[0] + pg + 1 if b else G_KD[1] + pg + 1 - L_TP))
                    sp.dma_start(dk_raw[:, pg], kd_d[bass.ds(page, 1)].rearrange("a p n -> (a p) n")).then_inc(dk_in[pg // 4], 16)

            if early:
                cmp_pages(0, True)
                sel_win_pages(0, True)
                out_done(sp, G_QK + 14)
                dk_pages(0, 0, True)
                return
            with sp.Fori(1, PAIRS_OF_SEQ) as i:
                dk_pages(i - 1, 1)
                cmp_pages(i)
                dk_pages(i, 0)
                sel_win_pages(i)
            dk_pages(PAIRS_OF_SEQ - 1, 1)
            sync_merge(sp)

        def pool_attention(pool, st):
            vd_d = io["cache_diff_v"][0].rearrange("n p h e -> n p (h e)")

            def values_in(i, b, first=False):
                for pg in range(NPAGE):
                    page = page_of(pool, i, b, pg)
                    if pg == 0 and not first:
                        past(pool, l_pv, i * 3 + (0 if b else -2))
                    pool.dma_start(dv_raw[b][pg], vd_d[bass.ds(page, 1)].rearrange("a p n -> (a p) n")).then_inc(dv_in[2 * b + pg // 4], 16)

            def queries_of(i, first=False):
                if not first:
                    past(pool, l_sc, i * 3)
                for src, dst in ((bd_raw, cur_raw), (bd_rot, cur_rot), (bd_dif, cur_dif)):
                    nc.gpsimd.tensor_copy(dst, src[:, bass.ds(2 * i, 2), :]).then_inc(l_cur, 1)

            arrived(pool, "small")
            pool.wait_ge(pj_full, 15)
            values_in(0, 0, True)
            out_done(pool, G_QK + 14)
            queries_of(0, True)
            pool.wait_ge(tp_full, G_END)
            pool.wait_ge(stored, n_stored)
            values_in(0, 1, True)
            with pool.Fori(1, PAIRS_OF_SEQ) as i:
                values_in(i, 0)
                queries_of(i)
                values_in(i, 1)
            pool_moe(pool, st)

        def pe_attention(pe):
            out_done(pe, G_END - 1)
            with pe.Fori(0, PAIRS_OF_SEQ) as i:
                def tp(n, items):
                    if n >= 2:
                        past(pe, l_out[n % 2], i * (L_TP // 2) + n // 2)
                    else:
                        past(pe, l_out[n % 2], i * (L_TP // 2))
                    for src, col in items:
                        r, c = src.shape[0], src.free_size()
                        last = nc.tensor.transpose(bank(n % 2)[0:c, col:col + r], src, ident[0:r, 0:r])
                    last.then_inc(l_tp, 1)

                def keys_t(b):
                    for pg in range(NPAGE):
                        if pg % 4 == 0:
                            pe.wait_ge(dk_in[pg // 4], i * 128 + 64 * (b + 1))
                        tp(G_KD[b] + pg, [(dk_raw[:, pg, 128 * h:128 * h + 128], 128 * h) for h in range(4)])
                        if b == 1 and pg == 4:
                            pe.wait_ge(l_pn, i + 1)
                            nc.tensor.matmul(bank(2)[:, 0:NCC], const("rsum"), pn, start=True, stop=True).then_inc(l_grp, 1)

                def dif_scores(b):
                    l_out_done(pe, i, G_KD[b] + 7)
                    past(pe, l_exp, i * 5 + 4 * b)
                    for k0 in (0, 512):
                        for h in range(4):
                            nc.tensor.matmul(s_sel[32 * h:32 * h + 32, k0:k0 + 512], cur_dif[:, b, 32 * h:32 * h + 32], kdT[:, h, k0:k0 + 512], start=True, stop=True)
                    for h in range(4):
                        last = nc.tensor.matmul(s_new[32 * h:32 * h + 32], cur_dif[:, b, 32 * h:32 * h + 32], kdnT[:, h, SEQ:NTOK], start=True, stop=True)
                    last.then_inc(l_sc, 1)

                def dif_values(b):
                    past(pe, l_exp, i * 5 + 4 * b + 1)
                    for k in range(2):
                        tp(G_PD[b] + k, [(e_sel[:, 512 * k + 128 * j:512 * k + 128 * j + 128], 128 * j) for j in range(4)])
                    tp(G_PD[b] + 2, [(ebuf[:, PAST:PAST + 128], 0)])
                    l_out_done(pe, i, G_PD[b] + 2)
                    for k in range(2):
                        pe.wait_ge(dv_in[2 * b + k], i * 64 + 64)
                    if b == 1:
                        pe.wait_ge(l_pv_out, i * 3 + 2)
                    for j in range(NPAGE + 1):
                        for h in range(4):
                            out = pv_dif[32 * h:32 * h + 32]
                            if j < NPAGE:
                                nc.tensor.matmul(out, ptl[:, j, 32 * h:32 * h + 32], dv_raw[b][j][:, 128 * h:128 * h + 128], start=(j == 0), stop=False)
                            else:
                                last = nc.tensor.matmul(out, ptl[0:NS, J_NEW, 32 * h:32 * h + 32], proj[0:NS, 2, P_VD + 128 * h:P_VD + 128 * h + 128], start=False, stop=True)
                    last.then_inc(l_pv, 1)
                    pe.wait_ge(l_on, i * 2 + b + 1)
                    pe.wait_ge(l_gelu, i + 1)
                    nc.tensor.matmul(joined, cmat, onrm, start=True, stop=True).then_inc(l_join, 1)

                pe.wait_ge(l_cur, (i + 1) * 3)
                keys_t(0)
                dif_scores(0)
                for b in range(2):
                    for k in range(4):
                        if k % 2 == 0:
                            pe.wait_ge(cmp_in[2 * b + k // 2], i * 128 + 128)
                        tp(G_CMP + 4 * b + k, [(cmp_raw[:, 4 * b + k, 128 * m:128 * m + 128], 128 * m) for m in range(4)])
                l_out_done(pe, i, G_CMP + 7)
                for c in range(2):
                    for l in range(CB // 2):
                        last = nc.tensor.matmul(bank(2)[:, 4 * NCC * c:4 * NCC * (c + 1)], w1[:, c, l, :],
                                                cmpT[:, 2 * c:2 * c + 2, :, l:l + CS // 2 * (NCC - 1) + 1:CS // 2],
                                                start=(l == 0), stop=(l == CB // 2 - 1))
                last.then_inc(l_hid, 1)
                dif_values(0)
                for b in range(2):
                    for k in range(2):
                        pe.wait_ge(sel_in[2 * b + k], (i + 1) * 64)
                        tp(G_SEL + 2 * b + k, [(sel_raw[:, b, 4 * k + h, 0:128], 128 * h) for h in range(4)])
                for b in range(2):
                    pe.wait_ge(win_in[b], (i + 1) * 16)
                    tp(G_WIN + b, [(win_raw[:, b, h, 0:128], 128 * h) for h in range(4)])
                pe.wait_ge(l_osq, i * 2 + 1)
                for g in range(2):
                    nc.tensor.matmul(bank(2)[64 * g:64 * g + 64, 256:382], w2[:, 0, :], hid[:, 0, g, :], start=True, stop=True)
                for b in range(2):
                    for g in range(2):
                        last = nc.tensor.matmul(bank(3)[0:NCC, 256 + 128 * b + 64 * g:320 + 128 * b + 64 * g],
                                                hid[:, 1, g, NCC * b:NCC * b + NCC], w2[:, 1, :], start=True, stop=True)
                last.then_inc(l_kv, 1)
                l_out_done(pe, i, G_WIN + 1)
                past(pe, l_exp, i * 5 + 1)
                for k0, w in ((0, 512), (512, 512)):
                    for b in range(2):
                        nc.tensor.matmul(s_sel[64 * b:64 * b + 64, k0:k0 + w], cur_rot[:, b, :], selT[:, b, k0:k0 + w], start=True, stop=True)
                for b in range(2):
                    nc.tensor.matmul(s_sel[64 * b:64 * b + 64, PAST:SELW], cur_rot[:, b, :], ksT[:, SEQ:NTOK], start=True, stop=True)
                pe.wait_ge(l_kv_out, i + 1)
                pe.wait_ge(l_pv_out, i * 3 + 1)
                for b in range(2):
                    nc.tensor.matmul(s_win[64 * b:64 * b + 64, 0:WIN], cur_rot[:, b, :], winT[:, b, :], start=True, stop=True)
                for b in range(2):
                    nc.tensor.matmul(s_win[64 * b:64 * b + 64, WIN:WINW], cur_rot[:, b, :], kwT[:, SEQ:NTOK], start=True, stop=True)
                for b in range(2):
                    last = nc.tensor.matmul(s_cmp[64 * b:64 * b + 64], cur_raw[:, b, :], kcT[:, b, :], start=True, stop=True)
                last.then_inc(l_sc, 1)

                keys_t(1)
                past(pe, l_exp, i * 5 + 4)
                for k in range(2):
                    tp(G_P + k, [(e_sel[:, 512 * k + 128 * j:512 * k + 128 * j + 128], 128 * j) for j in range(4)])
                tp(G_P + 2, [(e_win[:, 128 * j:128 * j + 128], 128 * j) for j in range(4)])
                tp(G_P + 3, [(ebuf[:, PAST:PAST + 128], 0), (e_win[:, WIN:WINW], 128), (pn, 256)])
                dif_scores(1)
                l_out_done(pe, i, G_P + 3)
                for br, n, j0 in ((1, NPAGE, 0), (2, WIN // PAGE, J_WIN), (0, 0, 0)):
                    raw = sel_raw if br == 1 else win_raw
                    for j in range(n + 1):
                        for b in range(2):
                            for g in range(2):
                                r0 = 64 * b + 32 * g
                                out = pv_nsa[r0:r0 + 32, br]
                                if j < n:
                                    last = nc.tensor.matmul(out, ptl[:, j0 + j, r0:r0 + 32], raw[:, b, j, 128 + 64 * g:192 + 64 * g],
                                                            start=(j == 0), stop=False)
                                elif br:
                                    base = (P_SEL if br == 1 else P_WIN) + 128 + 64 * g
                                    last = nc.tensor.matmul(out, ptl[0:NS, J_NEW + br - 1, r0:r0 + 32], proj[0:NS, 2, base:base + 64],
                                                            start=False, stop=True)
                                else:
                                    last = nc.tensor.matmul(out, ptl[0:NCC, J_NEW + 2, r0:r0 + 32], vc[0:NCC, b, 64 * g:64 * g + 64],
                                                            start=True, stop=True)
                last.then_inc(l_pv, 1)

                pe.wait_ge(l_pv_out, i * 3 + 2)
                tp(G_O, [(osm, 0)])
                dif_values(1)
                pe.wait_ge(l_odn, i + 1)
                tp(G_OD, [(odn[:, b, :], 128 * b) for b in range(2)])
            pe_merge(pe)

        def l_evac(eng, st, i, n, which, copy):
            assert n % 2 == which
            past(eng, l_tp, i * L_TP + n + 1)
            src = bank(n % 2)
            s4 = src.rearrange("p (k n) -> p k n", k=4)
            if G_CMP <= n < G_CMP + 8:
                b, k = (n - G_CMP) // 4, (n - G_CMP) % 4
                if n < G_CMP + 2:
                    past(eng, l_sc, i * 3 + 1)
                st(copy(cmpT[:, :, b, 128 * k:128 * k + 128], s4), l_out[which])
            elif G_SEL <= n < G_WIN:
                b, k = (n - G_SEL) // 2, (n - G_SEL) % 2
                st(copy(selT[:, b, 512 * k:512 * k + 512], src), l_out[which])
            elif G_WIN <= n < G_WIN + 2:
                st(copy(winT[:, n - G_WIN, :], src), l_out[which])
            elif n < 8 or G_KD[1] <= n < G_KD[1] + 8:
                b = 0 if n < 8 else 1
                pg = n - G_KD[b]
                if pg < 2:
                    if b:
                        eng.wait_ge(l_hid, i + 1)
                    else:
                        past(eng, l_sc, i * 3)
                st(copy(kdT[:, :, 128 * pg:128 * pg + 128], s4), l_out[which])
            elif G_P <= n < G_P + 3:
                if n < G_P + 2:
                    past(eng, l_pv, i * 3 + 1)
                j = {0: 0, 1: 4, 2: J_WIN}[n - G_P]
                st(copy(ptl[:, j:j + 4, :], s4), l_out[which])
            elif n == G_P + 3:
                st(copy(ptl[0:NS, J_NEW:J_NEW + 2, :], s4[0:NS, 0:2]))
                st(copy(ptl[0:NCC, J_NEW + 2, :], s4[0:NCC, 2]), l_out[which])
            elif n == G_O:
                for par in range(2):
                    for b in range(2):
                        d = onT[64 * par:64 * par + 64, :, bass.ds(i * 16 + (SEQ + NT * b), NT)]
                        s = src[64 * par:64 * par + 64, 64 * b:64 * b + 64].rearrange("p (k r t) -> p k r t", r=2, t=NT)[:, :, par]
                        st(copy(d, s), l_out[which] if par and b else None)
            elif n == G_OD:
                for b in range(2):
                    d = odT[:, :, bass.ds(i * 16 + (SEQ + NT * b), NT)]
                    s = src[:, 128 * b:128 * b + 128].rearrange("p (h x) -> p h x", h=4)[:, :, 0:NT]
                    st(nc.vector.tensor_scalar(d, s, sg, None, ALU.mult), l_out[which] if b else None)
            else:
                b = 0 if n < G_PD[1] else 1
                k = n - G_PD[b]
                past(eng, l_pv, i * 3 + 2 * b)
                if k < 2:
                    st(copy(ptl[:, 4 * k:4 * k + 4, :], s4), l_out[which])
                else:
                    st(copy(ptl[0:NS, J_NEW, :], src[0:NS, 0:128]), l_out[which])

        pn = alloc(NCC)
        ACT_PER_TURN = {"l_act": 2, "l_out_act": 21, "l_gelu": 1, "l_exp": 5, "l_sq": 2, "l_root": 1}
        DVE_PER_TURN = {"l_out_dve": 21, "l_dve": 35, "l_osq": 2, "l_kv_out": 1, "l_nmx": 5, "l_pn": 1, "l_pv_out": 3, "l_on": 2, "l_var": 1,
                        "l_odn": 1}

        def act_attention(act, st):
            copy = lambda d, s: nc.scalar.activation(d, s, ACT.Copy)
            before, st = st, Steps(act, l_act, primed)
            with act.Fori(0, PAIRS_OF_SEQ) as i:
                st.enter(i, ACT_PER_TURN)
                ev = lambda *ns: [l_evac(act, st, i, n, 0, copy) for n in ns]

                def exp(k, turn_k, out, src, sums):
                    act.wait_ge(l_nmx, i * 5 + turn_k)
                    st(nc.scalar.activation(out, src, ACT.Exp, bias=smx[:, k:k + 1], scale=SCALE, accum_out=sums), l_exp)

                def square(b):
                    act.wait_ge(l_osq, i * 2 + b + 1)
                    st(nc.scalar.activation(sqj, osq[:, b], ACT.Square, accum_out=lsum[:, 5 + b:6 + b]), l_sq)

                ev(0, 2, 4, 6, 8, 10)
                exp(3, 1, e_sel, s_sel, lsum[:, 3:4])
                ev(12, 14)
                act.wait_ge(l_hid, i + 1)
                for c in range(2):
                    ins = nc.scalar.activation(hid[:, c], bank(2)[:, 4 * NCC * c:4 * NCC * (c + 1)].rearrange("p (g n) -> p g n", g=2),
                                               ACT.Gelu_apprx_tanh, bias=hb[:, c:c + 1])
                    st(ins, l_gelu if c else None)
                ev(16, 18)
                square(0)
                ev(20, 22, 24)
                exp(1, 2, pn, s_cmp, lsum[:, 1:2])
                exp(0, 3, e_win, s_win, lsum[:, 0:1])
                ev(26, 28, 30, 32)
                exp(2, 4, e_sel, s_sel, lsum[:, 2:3])
                ev(34, 36)
                exp(4, 5, e_sel, s_sel, lsum[:, 4:5])
                ev(38, 40)
                square(1)
                act.wait_ge(l_var, i + 1)
                st(nc.scalar.activation(lvar, lvar, ACT.Sqrt), l_root)
            st.leave(PAIRS_OF_SEQ)
            act_merge(act, before)

        lsum, lvar, lcf, sqj, osq = alloc(8), alloc(2), alloc(8), alloc(128), alloc(2, 128)

        def dve_attention(dve, st):
            V = nc.vector
            before, st = st, Steps(dve, l_dve, primed)
            arrived(dve, "gS")
            with dve.Fori(0, PAIRS_OF_SEQ) as i:
                st.enter(i, DVE_PER_TURN)
                ev = lambda *ns: [l_evac(dve, st, i, n, 1, V.tensor_copy) for n in ns]

                def negmax(k, s):
                    st.own()
                    st(V.reduce_max(lcf[:, k:k + 1], s, AX))
                    st.own()
                    st(V.tensor_scalar(smx[:, k:k + 1], lcf[:, k:k + 1], -SCALE, None, ALU.mult), l_nmx)

                def dif_mask(b):
                    past(dve, l_sc, i * 3 + 1 + 2 * b)
                    newd = const("newd", NB, NS)[:, bass.ds(2 * i + b, 1), :].rearrange("p a n -> p (a n)")
                    st(V.tensor_tensor(s_new, s_new, newd, ALU.add))
                    negmax(3 + b, s_sel)

                def dif_norm(b):
                    st(V.reciprocal(lcf[:, 3 + b:4 + b], lsum[:, 3 + b:4 + b]))
                    past(dve, l_pv, i * 3 + 1 + 2 * b)
                    st.own()
                    st(V.tensor_scalar(onrm, pv_dif, lcf[:, 3 + b:4 + b], None, ALU.mult), l_pv_out)
                    st(V.memset(lcf[:, 7:8], 0.0), l_on)
                    dve.wait_ge(l_join, i * 2 + b + 1)
                    st(V.tensor_copy(osq[:, b], joined), l_osq)

                past(dve, l_exp, i * 5)
                ev(1, 3, 5, 7)
                ev(9)
                dif_mask(0)
                ev(11, 13, 15)
                past(dve, l_exp, i * 5 + 1)
                ev(17)
                dif_norm(0)
                ev(19, 21, 23)
                dve.wait_ge(l_kv, i + 1)
                st(V.tensor_copy(kcT.rearrange("p b n -> p (b n)"), bank(2)[:, 256:382]))
                st(V.tensor_copy(vc[0:NCC].rearrange("p b n -> p (b n)"), bank(3)[0:NCC, 256:512]), l_kv_out)
                past(dve, l_sc, i * 3 + 2)
                newn = const("newn", NB // 2, NS)[:, bass.ds(i, 1), :].rearrange("p a n -> p (a n)")
                st(V.tensor_tensor(s_new, s_new, newn, ALU.add))
                negmax(1, s_cmp)
                st(V.tensor_tensor(s_win[:, 0:NT], s_win[:, 0:NT], const("oldw"), ALU.add))
                st(V.tensor_tensor(s_win[:, WIN:WINW], s_win[:, WIN:WINW], newn, ALU.add))
                negmax(0, s_win)
                ev(25, 27)
                past(dve, l_exp, i * 5 + 2)
                st(V.reciprocal(lcf[:, 1:2], lsum[:, 1:2]))
                st.own()
                st(V.tensor_scalar(pn, pn, lcf[:, 1:2], None, ALU.mult), l_pn)
                ev(29)
                dve.wait_ge(l_grp, i + 1)
                st(V.tensor_copy(pgs[:, 0:NCC], bank(2)[:, 0:NCC]))
                st.own()
                n14 = PAST // SB - 2
                st(V.tensor_tensor(mass, pgs[:, 4:4 + 4 * n14].rearrange("p (a b) -> p a b", b=4),
                                   pgs[:, 3:3 + 4 * n14].rearrange("p (a b) -> p a b", b=4), ALU.add))
                st.own()
                st(V.reduce_sum(imp, mass, AX))
                st.own()
                st(V.tensor_reduce(lcf[:, 5:6], imp, AX, ALU.min))
                st.own()
                st(V.scalar_tensor_tensor(imp, imp, lcf[:, 5:6], const("blk"), ALU.is_equal, ALU.mult))
                st.own()
                st(V.reduce_max(lcf[:, 6:7], imp, AX))
                st.own()
                st(V.tensor_scalar(dropm, const("blk"), lcf[:, 6:7], NEG, ALU.is_equal, ALU.mult))
                st.own()
                mid = s_sel[:, SB:SB + n14 * SB].rearrange("p (a b) -> p a b", b=SB)
                st(V.tensor_tensor(mid, mid, dropm.unsqueeze(2).to_broadcast([128, n14, SB]), ALU.add))
                negmax(2, s_sel)
                ev(31, 33, 35)
                dif_mask(1)
                past(dve, l_exp, i * 5 + 4)
                gi = gS[:, bass.ds(i, 1), :].rearrange("p a b -> p (a b)")
                st(V.reciprocal(lcf[:, 0:1], lsum[:, 0:1]))
                st(V.reciprocal(lcf[:, 2:3], lsum[:, 2:3]))
                st.own()
                st(V.tensor_copy(lgt, gi))
                st.own()
                st(V.tensor_tensor(lcf[:, 0:1], lcf[:, 0:1], lgt[:, 2:3], ALU.mult))
                st(V.tensor_tensor(lcf[:, 2:3], lcf[:, 2:3], lgt[:, 1:2], ALU.mult))
                past(dve, l_pv, i * 3 + 2)
                st.own()
                st(V.tensor_scalar(osm[:, 0:64], pv_nsa[:, 0], lgt[:, 0:1], None, ALU.mult))
                st.own()
                st(V.scalar_tensor_tensor(osm[:, 0:64], pv_nsa[:, 1], lcf[:, 2:3], osm[:, 0:64], ALU.mult, ALU.add))
                st.own()
                st(V.scalar_tensor_tensor(osm[:, 0:64], pv_nsa[:, 2], lcf[:, 0:1], osm[:, 0:64], ALU.mult, ALU.add))
                st.own()
                st(V.tensor_copy(osm[:, 64:128], osm[:, 0:64]), l_pv_out)

                ev(37)
                past(dve, l_exp, i * 5 + 5)
                ev(39)
                dif_norm(1)
                dve.wait_ge(l_sq, i * 2 + 2)
                st(V.tensor_scalar(lvar, lsum[:, 5:7], 1.0 / 128, EPS, ALU.mult, ALU.add), l_var)
                dve.wait_ge(l_root, i + 1)
                st(V.reciprocal(lvar, lvar))
                st.own()
                st(V.tensor_tensor(odn, osq, lvar.unsqueeze(2).to_broadcast([128, 2, 128]), ALU.mult), l_odn)
                ev(41)
            st.leave(PAIRS_OF_SEQ)
            dve_merge(dve, before)

        lgt = alloc(3)

        xnT5 = at(6144, KD, NTOK)
        gsig = at(27136, 3, 2 * D)
        x5 = at(33280, 3, D)
        mT = at(36352, KD, NTOK)
        bias16 = at(31744, 1536).bitcast(BF16)
        cstb = at(38912, const_b.shape[1])
        br_n, br_d = at(10240, 4, D), at(14336, 4, D)
        w_out = at(0, KD, D)
        hn, hT6 = at(27136, 3, D), at(24576, KD, NTOK)
        hg, hTm = at(24576, D), at(25600, KD, 2 * BS)
        g1, sg1, u1, av = (at(27648 + 512 * k, 512) for k in range(4))
        aT = [at(29696 + 512 * u, 4, 128) for u in range(2)]
        ysb = [at(30720 + 512 * u, 512) for u in range(2)]
        yk = [at(4096 * t, 4, D) for t in range(3)]
        ROLE = (8192, 16384, 0)
        wring = [at(r, KD, D) for r in ROLE]
        wdown2 = [at(o2, 2, D) for o2 in (36352, 39752, 42440, 44488)]
        zo = 42440

        def zalloc(*dims):
            nonlocal zo
            zo += int(np.prod(dims))
            assert zo <= 53200, zo
            return at(zo - int(np.prod(dims)), *dims)

        b32, r32 = zalloc(3 * D), zalloc(3 * D)
        mid16 = b32[:, 0:1536].bitcast(BF16)
        nfin = zalloc(D)
        wr, rb, gffn = zalloc(KD, NE), zalloc(NE), zalloc(KD)
        lg, v8, i8 = zalloc(3, NE), zalloc(3, 8), zalloc(3, 8)
        i8u = i8.bitcast(U32)
        i8f, gt, gts = zalloc(3, TOPK), zalloc(3, TOPK), zalloc(3)
        oh, dtmp = zalloc(3, TOPK, NE), zalloc(3, TOPK, NE)
        msk, rk, nb = zalloc(3, NE), zalloc(128), zalloc(128)
        cc, ncol, nr, ovb = zalloc(1), zalloc(1), zalloc(NE), zalloc(NE + 1)
        qq, qa, qb_ = zalloc(3, NE), zalloc(3, NE), zalloc(3, NE)
        ebf, novp, dest = zalloc(NBLK), zalloc(1), zalloc(3, TOPK)
        ebi, novi, desti = zalloc(NBLK).bitcast(I32), zalloc(1).bitcast(I32), zalloc(3 * TOPK).bitcast(U32)
        etmp = zalloc(NBLK_OVER, NE)
        slots = zalloc(NBLK // 2 + 1).bitcast(U32)
        idx = zalloc(1).bitcast(U32)
        ohb = zalloc(NBLK // 2).bitcast(BF16)
        bsel = [zalloc(BS // 2).bitcast(BF16) for _ in range(2)]
        ssf, sq5 = zalloc(9), at(30208, D)
        pad = zalloc(4)
        pairn, slotn = zalloc(3 * TOPK), zalloc(3 * TOPK)
        at_slot, at_pair = b32[:, 0:12 * 2 * BS].rearrange("p (a s) -> p a s", a=12), r32[:, 0:12 * (NBLK // 2)].rearrange("p (a q) -> p a q", a=12)
        pair_cmp = r32[:, 512:512 + 12 * (NBLK // 2 - 1)].rearrange("p (a q) -> p a q", a=12)

        def dispatch_const(name, *dims):
            off, n = at_b[name]
            return at(38912 + off, *(dims or (n,)))

        br_full, m_done, z_full, x2_done = (sem(n) for n in ("br_full", "m_done", "z_full", "x2_done"))
        m_tp, m_out = sem("m_tp"), [sem("m_out_act"), sem("m_out_dve")]
        sq_done, var5, root5, hn_ready = (sem(n) for n in ("sq_done", "var5", "root5", "hn_ready"))
        lg_full, gt_in, gt_exp, msk_ready, rk_full, nb_ready, ov_full = (
            sem(n) for n in ("lg_full", "gt_in", "gt_exp", "msk_ready", "rk_full", "nb_ready", "ov_full"))
        blocks_ready, slots_ready = sem("blocks_ready"), sem("slots_ready")
        pool_clear, marks_ready, pad_done = sem("pool_clear"), sem("marks_ready"), sem("pad_done")
        h_stored, bias_ready = sem("h_stored"), sem("bias_ready")
        e_in = place_in + w_arrived
        e_base = [128 * PAIRS_OF_SEQ] * 4 + [64 * PAIRS_OF_SEQ] * 4 + [48, 48, 32, 32]
        e2_in = [sem(f"e2_in{j}") for j in range(4)]
        e_used = sem("e_used")
        hg_in = sem("hg_in")
        i_ready, x_tp, x_out, g_full, u_full, g1_ready, sg_ready, a_ready, a_tp, a_out, yb_full, y_ready = (
            sem(n) for n in ("i_ready", "x_tp", "x_out", "g_full", "u_full", "g1_ready", "sg_ready", "a_ready",
                             "a_tp", "a_out", "yb_full", "y_ready"))
        y_stored, yk_in = [sem(f"y_stored{u}") for u in range(2)], [sem(f"yk_in{t}") for t in range(3)]
        sq8, var8, root8, out_ready, out_stored = (sem(n) for n in ("sq8", "var8", "root8", "out_ready", "out_stored"))
        dx, sum_ready = sem("dve_experts_own"), sem("sum_ready")

        primed += [x_tp, yb_full, a_out, a_ready, y_ready]
        Y_ZEROED = 16 * NBLK_OVER * BS // 256

        V3 = [(t, nh) for t in range(3) for nh in range(2)]

        def m_out_done(eng, n):
            eng.wait_ge(m_out[0], n // 2 + 1)
            if n >= 1:
                eng.wait_ge(m_out[1], (n + 1) // 2)

        wgu = io["w_gate_up"][0].rearrange("e (p k) n -> e p k n", k=KD)
        wdn = io["w_down"][0].rearrange("e (h p k) n -> e p h k n", h=2, k=4)

        def block_weights(eng, e, s, u):
            role, j = s // 4, s % 4
            dst, arrival = wring[role][:, 2 * j:2 * j + 2, :], e_in[s]
            if role < 2:
                src = wgu[e, :, 2 * j:2 * j + 2, D * role:D * role + D]
            else:
                src = wdn[e, :, j // 2, 2 * (j % 2):2 * (j % 2) + 2, :]
                if u:
                    dst, arrival = wdown2[j], e2_in[j]
            if not isinstance(e, int):
                src = src.rearrange("a p k n -> (a p) k n")
            eng.dma_start(dst, src).then_inc(arrival, 16)

        GATE_UP, DOWN = range(8), range(8, 12)

        def sync_merge(sp):
            def gate_chunk(j):
                c0, w = CHUNKS[j]
                sp.dma_start(chunk_at(j), w_in[:, :, c0:c0 + w]).then_inc(w_arrived[CHUNK_SLOT[j]], 16)

            sp.wait_ge(l_hid, PAIRS_OF_SEQ)
            gate_chunk(6)
            gate_chunk(7)
            past(sp, l_pv, PAIRS_OF_SEQ * 3 - 1)
            gate_chunk(8)
            load(sp, "xn5", xnT5.rearrange("p k n -> p (k n)"), xn_dram)
            past(sp, l_sc, PAIRS_OF_SEQ * 3)
            gate_chunk(9)
            past(sp, l_tp, PAIRS_OF_SEQ * L_TP)
            past(sp, l_out[1], PAIRS_OF_SEQ * L_TP // 2)
            load(sp, "late", cstb, io["const_b"])
            load(sp, "late", gffn, io["norm_ffn"].rearrange("a (p k) -> p (a k)", k=KD))
            load(sp, "late", wr, io["w_router"][0].rearrange("(p k) e -> p k e", k=KD))
            load(sp, "late", rb, io["b_router"].to_broadcast([128, NE]))
            load(sp, "late", nfin, io["norm_final"].rearrange("(a n) -> a n", a=1).to_broadcast([128, D]))
            for s in range(3):
                load(sp, "bias", b32[32 * s:32 * s + 32, 0:2 * D], io["b_gate_up"][0])
                load(sp, "bias", b32[32 * s:32 * s + 32, 2 * D:3 * D], io["b_down"][0])
            sp.wait_ge(pj_full, 20)
            load(sp, "br", br_n, io["w_br_nsa"][0].rearrange("(k p) n -> p k n", p=128))
            load(sp, "br", br_d, io["w_br_diff"][0].rearrange("(k p) n -> p k n", p=128))
            sp.wait_ge(pj_full, 25)
            for t in range(3):
                load(sp, "late", x5[0:ROWS[t], t, :], x_rows[t])
            load(sp, "wout", w_out, io["w_out"][0].rearrange("(k p) n -> p k n", p=128))
            sp.wait_ge(br_full, 5)
            for s in GATE_UP:
                block_weights(sp, 0, s, 0)
            sp.wait_ge(z_full, 5)
            for s in DOWN:
                block_weights(sp, 0, s, 0)
            for s in DOWN[0:2]:
                block_weights(sp, 1, s, 1)
            for t in range(3):
                sp.wait_ge(hn_ready, t + 1)
                sp.dma_start(h_dram[128 * t:128 * t + ROWS[t]], hn[0:ROWS[t], t, :]).then_inc(h_stored, 16)
            sp.wait_ge(m_tp, 13)
            for s in DOWN[2:4]:
                block_weights(sp, 1, s, 1)
            for s in GATE_UP:
                sp.wait_ge(e_used, s + 1)
                block_weights(sp, 1, s, 1)

            def pair_weights(i, experts):
                for u in range(2):
                    for s in (*GATE_UP, *DOWN) if u else (*DOWN, *GATE_UP):
                        sp.wait_ge(e_used, i * 24 + (12 * (u - (2 if s in DOWN else 1)) + s + 1))
                        block_weights(sp, experts[u], s, u)

            with sp.Fori(1, NE // 2) as i:
                pair_weights(i, [bass.ds(2 * i + u, 1) for u in range(2)])
            sp.wait_ge(blocks_ready, 1)
            more = sp.value_load(novi[0:1, 0:1], min_val=0, max_val=NBLK_OVER // 2)
            with sp.If(more > 0):
                with sp.Fori(NE // 2, more + NE // 2) as i:
                    e2 = [sp.value_load(ebi[0:1, bass.ds(2 * i + u, 1)], min_val=0, max_val=NE - 1) for u in range(2)]
                    pair_weights(i, [bass.ds(e, 1) for e in e2])
            yp, ys = io["y_prompt"][0], io["y_sample"].rearrange("b t d -> (b t) d")
            for t in range(3):
                sp.wait_ge(out_ready, t + 1)
                sp.dma_start(yp[128 * t:128 * t + 128] if t < 2 else ys, x5[0:ROWS[t], t, :]).then_inc(out_stored, 16)
            sp.wait_ge(out_stored, 48)

        def pool_moe(pool, st):
            G = nc.gpsimd
            for k in range(NE * BS // 128, NBLK * BS // 128):
                pool.dma_start(y_dram[128 * k:128 * k + 128].rearrange("p (c n) -> p c n", n=256),
                               zero.unsqueeze(1).to_broadcast([128, 4, 256])).then_inc(y_stored[k % 2], 16)
            pool.wait_ge(l_odn, PAIRS_OF_SEQ)
            for u in range(2):
                pool.wait_ge(y_stored[u], Y_ZEROED)
            G.memset(pad, 0.0).then_inc(pool_clear, 1)
            pool.wait_ge(slots_ready, 1)
            pool.wait_ge(h_stored, 48)
            pool.wait_ge(blocks_ready, 1)
            more = pool.value_load(novi[0:1, 0:1], min_val=0, max_val=NBLK_OVER // 2)
            def rows_in():
                G.indirect_dma_start(out=hg, out_offset=None, in_=h_dram,
                                     in_offset=bass.IndirectOffsetOnAxis(ap=idx, axis=0)).then_inc(hg_in, 16)

            G.tensor_copy(idx, slots[:, 0:1]).then_inc(i_ready, 1)
            pool.wait_ge(i_ready, 1)
            rows_in()
            with pool.Fori(0, more + NE // 2) as i:
                past(pool, yb_full, i * 2)
                for u in range(2):
                    G.tensor_copy(bsel[u][0:96], ohb[0:96, bass.ds(2 * i + u, 1)].to_broadcast([96, BS])).then_inc(i_ready, 1)
                pool.wait_ge(hg_in, (i + 1) * 16)
                G.tensor_copy(idx, slots[:, bass.ds(i + 1, 1)]).then_inc(i_ready, 1)
                past(pool, x_tp, i + 1)
                pool.wait_ge(i_ready, i * 4 + 4)
                G.tensor_tensor(pad[:, 0:1], pad[:, 1:2], pad[:, 2:3], ALU.add).then_inc(i_ready, 1)
                rows_in()
                for u in range(2):
                    past(pool, y_ready, i * 2 + (u + 1))
                    pool.dma_start(y_dram[bass.ds(i * (2 * BS) + u * BS, BS)].rearrange("r (h n) -> h r n", h=2),
                                   ysb[u]).then_inc(y_stored[u], 16)
            for u in range(2):
                pool.wait_ge(y_stored[u], (more + NE // 2) * 16 + Y_ZEROED)
            G.tensor_tensor(pad[:, 3:4], pad[:, 1:2], pad[:, 2:3], ALU.add).then_inc(pad_done, 1)
            pool.wait_ge(pad_done, 1)
            for t in range(3):
                for k in range(TOPK):
                    r = ROWS[t]
                    G.indirect_dma_start(out=yk[t][0:r, k, :], out_offset=None, in_=y_dram,
                                         in_offset=bass.IndirectOffsetOnAxis(ap=desti[0:r, TOPK * t + k:TOPK * t + k + 1], axis=0)).then_inc(yk_in[t], 16)

        def pe_merge(pe):
            def tp(n, items):
                if n >= 2:
                    pe.wait_ge(m_out[n % 2], n // 2)
                for src, col in items:
                    r, c = src.shape[0], src.free_size()
                    last = nc.tensor.transpose(bank(n % 2)[0:c, col:col + r], src, ident[0:r, 0:r])
                last.then_inc(m_tp, 1)

            l_out_done(pe, PAIRS_OF_SEQ - 1, L_TP - 1)
            arrived(pe, "xn5")
            pe_projection(pe, PAIRS[3:5], 3, xnT5)
            arrived(pe, "br")
            arrived(pe, "br")
            for e in range(2):
                pe.wait_ge(pj_out[e], 15)
            for v in range(5):
                if v >= 3:
                    pe.wait_ge(m_done, v - 2)
                b = 2 + 2 * (v % 3)
                for src, w, bb in ((onT, br_n, b), (odT, br_d, b + 1)):
                    for k in range(4):
                        for v2 in ((v,) if v < 4 else (4, 5)):
                            t, nh = V3[v2]
                            r, p = ROWS[t], 64 * (v2 - 4) if v2 > 4 else 0
                            last = nc.tensor.matmul(bank(bb)[p:p + r], src[:, k, 128 * t:128 * t + r], w[:, k, 512 * nh:512 * nh + 512], start=(k == 0), stop=(k == 3))
                last.then_inc(br_full, 1)
            for v, (t, nh) in enumerate(V3):
                pe.wait_ge(m_done, v + 1)
                tp(v, [(gsig[0:ROWS[t], t, 512 * nh + 128 * k:512 * nh + 128 * k + 128], ROWS[t] * k) for k in range(4)])
            arrived(pe, "wout")
            def out_proj(v):
                m_out_done(pe, 2 * (v // 2) + 1)
                for k in range(KD):
                    for v2 in ((v,) if v < 4 else (4, 5)):
                        t, nh = V3[v2]
                        r, p = ROWS[t], 64 * (v2 - 4) if v2 > 4 else 0
                        last = nc.tensor.matmul(bank(2 + v)[p:p + r], mT[:, k, 128 * t:128 * t + r], w_out[:, k, 512 * nh:512 * nh + 512], start=(k == 0), stop=(k == KD - 1))
                last.then_inc(z_full, 1)

            def hn_t(t):
                pe.wait_ge(hn_ready, t + 1)
                for half in range(2):
                    tp(6 + 2 * t + half, [(hn[0:ROWS[t], t, 4 * half + k:D:KD], ROWS[t] * k) for k in range(4)])

            def logits(t):
                m_out_done(pe, 7 + 2 * t)
                for k in range(KD):
                    last = nc.tensor.matmul(bank(2)[0:ROWS[t], NE * t:NE * t + NE], hT6[:, k, 128 * t:128 * t + ROWS[t]], wr[:, k, :], start=(k == 0), stop=(k == KD - 1))
                return last

            for v in range(4):
                out_proj(v)
            hn_t(0)
            out_proj(4)
            arrived(pe, "late")
            hn_t(1)
            pe.wait_ge(x2_done, 1)
            logits(0)
            hn_t(2)
            logits(1)
            logits(2).then_inc(lg_full, 1)
            pe.wait_ge(msk_ready, 1)
            ones, lower = dispatch_const("ones"), dispatch_const("lower")
            for t in range(4):
                terms = [(ones[0:ROWS[s]], msk[0:ROWS[s], s]) for s in range(min(t, 3))]
                if t < 3:
                    terms.append((lower[0:ROWS[t]], msk[0:ROWS[t], t]))
                for n, (l, r) in enumerate(terms):
                    nc.tensor.matmul(bank(3)[:, NE * t:NE * t + NE], l, r, start=(n == 0), stop=(n == len(terms) - 1))
            for t in range(3):
                last = nc.tensor.matmul(bank(3)[0:NE, 128:129], msk[0:ROWS[t], t], ones[0:ROWS[t], 0:1], start=(t == 0), stop=(t == 2))
            last.then_inc(rk_full, 1)
            pe.wait_ge(nb_ready, 1)
            nc.tensor.matmul(bank(4)[:, 0:NE], nb[0:NE], dispatch_const("before")[0:NE], start=True, stop=True)
            nc.tensor.matmul(bank(4)[:, NE:NE + 1], nb[0:NE], ones[0:NE, 0:1], start=True, stop=True).then_inc(ov_full, 1)
            pe.wait_ge(marks_ready, 1)
            for a in range(12):
                r = ROWS[a // TOPK]
                last = nc.tensor.matmul(bank(0)[:, 0:NBLK // 2], at_slot[0:r, a], at_pair[0:r, a], start=(a == 0), stop=(a == 11))
            last.then_inc(m_tp, 1)
            m_out_done(pe, 12)
            pe.wait_ge(blocks_ready, 1)
            pe.wait_ge(bias_ready, 1)
            more = pe.value_load(novi[0:1, 0:1], min_val=0, max_val=NBLK_OVER // 2)
            with pe.Fori(0, more + NE // 2) as i:
                pe.wait_ge(hg_in, (i + 1) * 16)
                past(pe, a_out, i * 2)
                for k in range(KD):
                    last = nc.tensor.transpose(bank(k // 4)[:, 128 * (k % 4):128 * (k % 4) + 128], hg[:, k:D:KD], ident)
                last.then_inc(x_tp, 1)
                pe.wait_ge(i_ready, i * 4 + 3)
                pe.wait_ge(x_out, i + 1)
                for u in range(2):
                    for role, full in ((0, g_full), (1, u_full)):
                        b = 2 + 2 * role + u
                        past(pe, a_ready, i * 2)
                        for k in range(KD):
                            if k % 2 == 0:
                                pe.wait_ge(e_in[4 * role + k // 2], i * 32 + (e_base[4 * role + k // 2] + 16 * (u + 1)))
                            for h in range(2):
                                last = nc.tensor.matmul(bank(b)[64 * h:64 * h + 64], hTm[:, k, BS * u:BS * u + BS], wring[role][:, k, 512 * h:512 * h + 512],
                                                        start=(k == 0), stop=False)
                            if k % 2:
                                last.then_inc(e_used, 1)
                        for h in range(2):
                            last = nc.tensor.matmul(bank(b)[64 * h:64 * h + 64], bsel[u][0:96, 0:BS], bias16[0:96, D * role + 512 * h:D * role + 512 * h + 512],
                                                    start=False, stop=True)
                        last.then_inc(full, 1)
                    past(pe, a_ready, i * 2 + (u + 1))
                    if u:
                        past(pe, a_out, i * 2 + 1)
                    for k in range(4):
                        last = nc.tensor.transpose(bank(1)[:, 128 * k:128 * k + 128], av[:, k:512:4], ident)
                    last.then_inc(a_tp, 1)
                    past(pe, a_out, i * 2 + (u + 1))
                    past(pe, y_ready, i * 2)
                    for c in range(KD):
                        if c % 2 == 0:
                            pe.wait_ge(e2_in[c // 2] if u else e_in[8 + c // 2], i * 16 + (16 + (0 if u else e_base[8 + c // 2])))
                        for h in range(2):
                            last = nc.tensor.matmul(bank(6 + u)[64 * h:64 * h + 64], aT[u][:, c % 4, 64 * (c // 4):64 * (c // 4) + 64],
                                                    (wdown2[c // 2][:, c % 2] if u else wring[2][:, c])[:, 512 * h:512 * h + 512], start=(c == 0), stop=False)
                        if c % 2:
                            last.then_inc(e_used, 1)
                    for h in range(2):
                        last = nc.tensor.matmul(bank(6 + u)[64 * h:64 * h + 64], bsel[u][0:96, 0:BS], bias16[0:96, 2 * D + 512 * h:2 * D + 512 * h + 512],
                                                start=False, stop=True)
                    last.then_inc(yb_full, 1)

        def act_merge(act, st):
            A = nc.scalar.activation
            for q in (3, 4):
                for s in range(4):
                    j, t = PAIRS[q][s // 2], s % 2
                    act.wait_ge(pj_full, 5 * q + s + 1)
                    st(A(gsig[:, t, 512 * (j - 6):512 * (j - 6) + 512], bank(proj_bank(q, s)), ACT.Sigmoid), pj_out[t])
                act.wait_ge(pj_full, 5 * q + 5)
                for s in range(2):
                    j = PAIRS[q][s]
                    st(A(gsig[0:NS, 2, 512 * (j - 6):512 * (j - 6) + 512], bank(proj_bank(q, 4))[64 * s:64 * s + 64], ACT.Sigmoid), pj_out[s])

            def evac(n, gain):
                act.wait_ge(m_tp, n + 1)
                t, r = (n % 6) // 2, ROWS[(n % 6) // 2]
                for k in range(4 if gain else 1):
                    if gain:
                        st(A(hT6[:, k, 128 * t:128 * t + r], bank(0)[:, r * k:r * k + r], ACT.Copy, scale=gffn[:, k:k + 1]),
                           m_out[0] if k == 3 else None)
                    else:
                        st(A(mT[:, 0:4, 128 * t:128 * t + r], bank(0)[:, 0:4 * r].rearrange("p (k n) -> p k n", k=4), ACT.Copy), m_out[0])

            for n in (0, 2, 4):
                evac(n, False)
            arrived(act, "late")
            for t in range(3):
                r = ROWS[t]
                act.wait_ge(x2_done, 2 * t + 2)
                if t:
                    st.own()
                st(A(sq5[0:r], x5[0:r, t], ACT.Square, accum_out=ssf[0:r, t:t + 1]), sq_done)
                act.wait_ge(var5, t + 1)
                st(A(ssf[0:r, 3 + t:4 + t], ssf[0:r, 3 + t:4 + t], ACT.Sqrt), root5)
            for n in (6, 8, 10):
                evac(n, True)
            act.wait_ge(gt_in, 1)
            st(A(gt, gt, ACT.Exp), gt_exp)
            act.wait_ge(m_tp, 13)
            st(A(slots[:, 0:NBLK // 2], bank(0)[:, 0:NBLK // 2], ACT.Copy), m_out[0])
            act.wait_ge(blocks_ready, 1)
            more = act.value_load(novi[0:1, 0:1], min_val=0, max_val=NBLK_OVER // 2)
            with act.Fori(0, more + NE // 2) as i:
                for u in range(2):
                    act.wait_ge(g1_ready, i * 2 + (u + 1))
                    A(sg1, g1, ACT.Sigmoid, scale=ALPHA).then_inc(sg_ready, 1)
                    act.wait_ge(a_tp, i * 2 + (u + 1))
                    past(act, yb_full, i * 2)
                    A(aT[u], bank(1).rearrange("p (k n) -> p k n", k=4), ACT.Copy).then_inc(a_out, 1)
                    past(act, yb_full, i * 2 + (u + 1))
                    act.wait_ge(y_stored[u], i * 16 + Y_ZEROED)
                    A(ysb[u], bank(6 + u), ACT.Copy).then_inc(y_ready, 1)
            def square(t):
                r = ROWS[t]
                act.wait_ge(sum_ready, t + 1)
                st(A(yk[t][0:r, 1, :], x5[0:r, t], ACT.Square, accum_out=ssf[0:r, t:t + 1]), sq8)

            def root(t):
                r = ROWS[t]
                act.wait_ge(var8, t + 1)
                st(A(ssf[0:r, 3 + t:4 + t], ssf[0:r, 3 + t:4 + t], ACT.Sqrt), root8)

            for t in range(3):
                square(t)
                root(t)

        def dve_merge(dve, st):
            V = nc.vector
            for v, (t, nh) in enumerate(V3):
                r, b, p = ROWS[t], 2 + 2 * (min(v, 4) % 3), 64 if v == 5 else 0
                if v == 0:
                    for e in range(2):
                        dve.wait_ge(pj_out[e], 15)
                dve.wait_ge(br_full, min(v, 4) + 1)
                gn = gsig[0:r, t, 512 * nh:512 * nh + 512]
                gd = gsig[0:r, t, D + 512 * nh:D + 512 * nh + 512]
                st(V.tensor_tensor(gn, gn, bank(b)[p:p + r], ALU.mult))
                st(V.tensor_tensor(gd, gd, bank(b + 1)[p:p + r], ALU.mult))
                st.own()
                st(V.tensor_tensor(gn, gn, gd, ALU.add), m_done)
            for n in (1, 3, 5):
                t, r = n // 2, ROWS[n // 2]
                dve.wait_ge(m_tp, n + 1)
                st(V.tensor_copy(mT[:, 4:8, 128 * t:128 * t + r], bank(1)[:, 0:4 * r].rearrange("p (k n) -> p k n", k=4)), m_out[1])
            arrived(dve, "bias")
            dve.wait_ge(m_tp, 6)
            r96 = slice(0, 96)
            st(V.tensor_copy(bias16[r96], b32[r96]))
            st.own()
            st(V.tensor_tensor(r32[r96], b32[r96], bias16[r96], ALU.subtract))
            st.own()
            st(V.tensor_copy(mid16[r96], r32[r96]))
            st.own()
            st(V.tensor_tensor(r32[64:96], r32[64:96], mid16[64:96], ALU.subtract))
            st(V.tensor_copy(bias16[32:64], mid16[32:64]))
            st.own()
            st(V.tensor_copy(bias16[64:96], r32[64:96]), bias_ready)
            arrived(dve, "late")
            for t in range(3):
                r = ROWS[t]
                for nh in range(2):
                    v, p = min(2 * t + nh, 4), 64 if 2 * t + nh == 5 else 0
                    dve.wait_ge(z_full, v + 1)
                    xv = x5[0:r, t, 512 * nh:512 * nh + 512]
                    st(V.tensor_tensor(xv, xv, bank(2 + v)[p:p + r], ALU.add), x2_done)
                dve.wait_ge(sq_done, t + 1)
                s = ssf[0:r, 3 + t:4 + t]
                st(V.tensor_scalar(s, ssf[0:r, t:t + 1], 1.0 / D, EPS, ALU.mult, ALU.add), var5)
                dve.wait_ge(root5, t + 1)
                st(V.reciprocal(s, s))
                st.own()
                st(V.tensor_scalar(hn[0:r, t], x5[0:r, t], s, None, ALU.mult), hn_ready)
            arrived(dve, "late")
            for n in (7, 9, 11):
                t, r = (n - 6) // 2, ROWS[(n - 6) // 2]
                dve.wait_ge(m_tp, n + 1)
                st(V.tensor_tensor(hT6[:, 4:8, 128 * t:128 * t + r], bank(1)[:, 0:4 * r].rearrange("p (k n) -> p k n", k=4),
                                   gffn[:, 4:8].unsqueeze(2).to_broadcast([128, 4, r]), ALU.mult), m_out[1])

            def op(f, *a):
                st(f(*a))
                st.own()

            dve.wait_ge(pool_clear, 1)
            op(V.memset, lg, 0.0)
            arrived(dve, "late")
            arrived(dve, "late")
            dve.wait_ge(lg_full, 1)
            st(V.tensor_tensor(lg[:, 0:2], bank(2)[:, 0:2 * NE].rearrange("p (t e) -> p t e", t=2), rb.unsqueeze(1).to_broadcast([128, 2, NE]), ALU.add))
            op(V.tensor_tensor, lg[0:NS, 2], bank(2)[0:NS, 2 * NE:3 * NE], rb[0:NS], ALU.add)
            for t in range(3):
                op(V.max, v8[:, t], lg[:, t])
                op(V.max_index, i8u[:, t], v8[:, t], lg[:, t])
            st(V.tensor_tensor(gt, v8[:, :, 0:TOPK], v8[:, :, 0:1].to_broadcast([128, 3, TOPK]), ALU.subtract), gt_in)
            op(V.tensor_copy, i8f, i8u[:, :, 0:TOPK])
            ex12 = dispatch_const("expert").unsqueeze(1).to_broadcast([128, 12, NE])
            oh12, dt12 = oh.rearrange("p t k e -> p (t k) e"), dtmp.rearrange("p t k e -> p (t k) e")
            op(V.tensor_tensor, oh12, ex12, i8f.rearrange("p t k -> p (t k)").unsqueeze(2).to_broadcast([128, 12, NE]), ALU.is_equal)
            st(V.reduce_sum(msk, oh.rearrange("p t k e -> p t e k"), AX), msk_ready)
            dve.wait_ge(gt_exp, 1)
            op(V.reduce_sum, gts, gt, AX)
            op(V.reciprocal, gts, gts)
            op(V.tensor_tensor, gt, gt, gts.unsqueeze(2).to_broadcast([128, 3, TOPK]), ALU.mult)
            dve.wait_ge(rk_full, 1)
            st(V.tensor_copy(rk, bank(3)[:, 0:128]))
            op(V.tensor_copy, cc[0:NE], bank(3)[0:NE, 128:129])

            def steps_over(out, src, ge):
                cmp = ALU.is_ge if ge else ALU.is_gt
                op(V.tensor_scalar, out, src, float(BS), None, cmp)
                for c in range(2, NTOK // BS if NTOK % BS == 0 else NTOK // BS + 1):
                    op(V.scalar_tensor_tensor, out, src, float(BS * c), out, cmp, ALU.add)

            steps_over(ncol[0:NE], cc[0:NE], False)
            st(V.tensor_copy(nb[0:NE], ncol[0:NE].to_broadcast([NE, 128])), nb_ready)
            steps_over(nr, rk[:, 96:128], False)
            rk3 = rk[:, 0:96].rearrange("p (t e) -> p t e", t=3)
            steps_over(qq, rk3, True)
            dve.wait_ge(ov_full, 1)
            op(V.tensor_copy, ovb, bank(4)[:, 0:NE + 1])
            ovb3 = ovb[:, 0:NE].unsqueeze(1).to_broadcast([128, 3, NE])
            ex3 = dispatch_const("expert").unsqueeze(1).to_broadcast([128, 3, NE])
            op(V.tensor_tensor, qa, qq, ovb3, ALU.add)
            op(V.tensor_tensor, qa, qa, ex3, ALU.subtract)
            op(V.tensor_scalar, qb_, qq, 0.0, None, ALU.is_gt)
            op(V.scalar_tensor_tensor, qa, qa, float(NE - 1), qb_, ALU.add, ALU.mult)
            op(V.tensor_tensor, qa, qa, ex3, ALU.add)
            op(V.scalar_tensor_tensor, qb_, qq, -float(BS), rk3, ALU.mult, ALU.add)
            op(V.scalar_tensor_tensor, qa, qa, float(BS), qb_, ALU.mult, ALU.add)
            for t in range(3):
                op(V.tensor_tensor, dtmp[:, t], oh[:, t], qa[:, t].unsqueeze(1).to_broadcast([128, TOPK, NE]), ALU.mult)
            op(V.reduce_sum, dest.rearrange("p t k -> p (t k)"), dt12, AX)
            st(V.tensor_copy(desti, dest.rearrange("p t k -> p (t k)")))
            pf, sf = pairn.unsqueeze(2), slotn.unsqueeze(2)
            dflat = dest.rearrange("p t k -> p (t k)")
            op(V.tensor_tensor, pair_cmp, dflat.unsqueeze(2).to_broadcast([128, 12, NBLK // 2 - 1]),
               dispatch_const("pair128").unsqueeze(1).to_broadcast([128, 12, NBLK // 2 - 1]), ALU.is_ge)
            op(V.reduce_sum, pairn, pair_cmp, AX)
            op(V.scalar_tensor_tensor, slotn, pairn, -float(2 * BS), dflat, ALU.mult, ALU.add)
            st(V.tensor_tensor(at_slot, dispatch_const("slot").unsqueeze(1).to_broadcast([128, 12, 2 * BS]), sf.to_broadcast([128, 12, 2 * BS]), ALU.is_equal))
            op(V.tensor_tensor, at_pair, dispatch_const("pair").unsqueeze(1).to_broadcast([128, 12, NBLK // 2]), pf.to_broadcast([128, 12, NBLK // 2]), ALU.is_equal)
            st(V.tensor_tensor(at_pair.rearrange("p (t k) q -> p t (k q)", t=3), at_pair.rearrange("p (t k) q -> p t (k q)", t=3),
                               dispatch_const("tokid").unsqueeze(2).to_broadcast([128, 3, TOPK * NBLK // 2]), ALU.mult), marks_ready)
            op(V.tensor_tensor, nr, nr, ovb[:, 0:NE], ALU.add)
            op(V.tensor_tensor, etmp, nr.unsqueeze(1).to_broadcast([128, NBLK_OVER, NE]), dispatch_const("over").unsqueeze(2).to_broadcast([128, NBLK_OVER, NE]), ALU.is_le)
            op(V.reduce_sum, ebf[:, NE:NBLK], etmp, AX)
            op(V.tensor_scalar, ebf[:, NE:NBLK], ebf[:, NE:NBLK], float(NE - 1), None, ALU.min)
            op(V.tensor_copy, ebf[:, 0:NE], dispatch_const("expert"))
            st(V.tensor_copy(ebi, ebf))
            op(V.tensor_scalar, ohb[0:96], ebf[0:96], dispatch_const("pmod")[0:96], None, ALU.is_equal)
            op(V.tensor_scalar, etmp[:, 0, 0:NBLK_OVER // 2], dispatch_const("pairs"), ovb[:, NE:NE + 1], None, ALU.is_lt)
            op(V.reduce_sum, novp, etmp[:, 0, 0:NBLK_OVER // 2], AX)
            st(V.tensor_copy(novi, novp), blocks_ready)
            m_out_done(dve, 12)
            st(V.memset(slots[:, NBLK // 2:NBLK // 2 + 1].bitcast(F32), 0.0), slots_ready)
            dve.wait_ge(blocks_ready, 1)
            more = dve.value_load(novi[0:1, 0:1], min_val=0, max_val=NBLK_OVER // 2)
            before, st = st, Steps(dve, dx, primed)
            with dve.Fori(0, more + NE // 2) as i:
                st.enter(i, {"dve_experts_own": 4, "x_out": 1, "g1_ready": 2, "a_ready": 2})
                past(dve, x_tp, i + 1)
                st(V.tensor_tensor(hTm, PS[:, 0:1024].rearrange("p (k n) -> p k n", k=KD), gffn.unsqueeze(2).to_broadcast([128, KD, 2 * BS]), ALU.mult), x_out)
                for u in range(2):
                    dve.wait_ge(g_full, i * 2 + (u + 1))
                    st(V.tensor_scalar(g1, bank(2 + u), LIM, None, ALU.min), g1_ready)
                    dve.wait_ge(u_full, i * 2 + (u + 1))
                    st(V.tensor_scalar(u1, bank(4 + u), -LIM, LIM, ALU.max, ALU.min))
                    st.own()
                    st(V.scalar_tensor_tensor(u1, u1, 1.0, g1, ALU.add, ALU.mult))
                    dve.wait_ge(sg_ready, i * 2 + (u + 1))
                    st.own()
                    if u:
                        dve.wait_ge(a_tp, i * 2 + 1)
                    st(V.tensor_tensor(av, u1, sg1, ALU.mult), a_ready)
            st.leave(None)
            st = before

            def add_experts(t):
                r = ROWS[t]
                dve.wait_ge(yk_in[t], 64)
                for k in range(TOPK):
                    st(V.scalar_tensor_tensor(x5[0:r, t], yk[t][0:r, k], gt[0:r, t, k:k + 1], x5[0:r, t], ALU.mult, ALU.add),
                       sum_ready if k == TOPK - 1 else None)
                    if k < TOPK - 1:
                        st.own()

            def final_norm(t):
                r = ROWS[t]
                s = ssf[0:r, 3 + t:4 + t]
                dve.wait_ge(sq8, t + 1)
                st(V.tensor_scalar(s, ssf[0:r, t:t + 1], 1.0 / D, EPS, ALU.mult, ALU.add), var8)
                dve.wait_ge(root8, t + 1)
                st(V.reciprocal(s, s))
                st.own()
                st(V.scalar_tensor_tensor(x5[0:r, t], x5[0:r, t], s, nfin[0:r], ALU.mult, ALU.mult), out_ready)

            add_experts(0)
            add_experts(1)
            final_norm(0)
            add_experts(2)
            final_norm(1)
            final_norm(2)
        block = ctx.enter_context(nc.Block())

        @block.sync
        def _(sp):
            def store(dst, src):
                nonlocal n_stored
                n_stored += 16
                sp.dma_start(dst, src).then_inc(stored, 16)

            def load_chunk(j):
                c0, w, slot = *CHUNKS[j], CHUNK_SLOT[j]
                sp.dma_start(chunk_at(j)[:, :, 0:w], w_in[:, :, c0:c0 + w]).then_inc(w_arrived[slot], 16)

            for t in range(3):
                load(sp, f"x{t}", xin[0:ROWS[t], t, :], x_rows[t])
            load(sp, "const", cst, io["const_a"])
            load(sp, "const", gmix, io["norm_mix"].rearrange("a (k p) -> p (a k)", p=128),
                 allow_slow_non_contiguous=True)
            for j in range(4):
                load_chunk(j)
            load(sp, "small", peraw[0:CB, :], io["cmp_pe"].rearrange("a c (l q) d -> (a c l) (q d)", q=2))
            load(sp, "small", w2, io["w_cmp2"].rearrange("a c h d -> h (a c) d"))
            load(sp, "small", dl, io["diff_lambda"].rearrange("a m d -> a (m d)").to_broadcast([128, 256]))
            load(sp, "small", sg, io["diff_subln"].rearrange("a (p o) -> (a p) o", o=1))
            load(sp, "small", ptab[:, :], io["page_table"].rearrange("(a b) n -> a (b n)", a=1))
            sp.wait_ge(xn_ready, 6)
            out_done(sp, 5)
            sp.dma_start(xn_dram, xnT.rearrange("p k n -> p (k n)")).then_inc(xn_stored, 16)
            sp.wait_ge(pj_full, 5)
            load_chunk(4)
            load_chunk(5)
            sp.wait_ge(pj_full, 10)
            for c in range(2):
                load(sp, "w1", w1[:, c], io["w_cmp1"][0, c].rearrange("(l p) h -> p l h", p=128))
            arrived(sp, "small")
            sp.wait_ge(pj_full, 15)
            sync_attention(sp, True)
            sp.wait_ge(gates_ready, 1)
            store(gate_dram, gates[0:NS, 2, :])

            sp.wait_ge(zeroed, 1)
            wp = io["new_win_kv_prompt"].rearrange("a b s c g d -> (a b s) (c g d)")
            for k in range(2):
                store(wp[128 * k:128 * k + 128], zero)
            for b in range(NB):
                store(io["new_win_kv_sample"].rearrange("a b s c g d -> (a b) s (c g d)")[b, 0:WIN - NT],
                      io["state_win_kv"].rearrange("a b s c g d -> (a b) s (c g d)")[b, NT:WIN])
            sp.wait_ge(pj_out[0], 9)
            sp.wait_ge(pj_out[1], 9)
            sp.wait_ge(roped, 5)
            for name, p0, w in (("cmp_kv", P_CMP, 256), ("sel_kv", P_SEL, 256), ("diff_k", P_KD, 512), ("diff_v", P_VD, 512)):
                pr, sa = io[f"new_{name}_prompt"], io[f"new_{name}_sample"]
                fl = "a b s c g d -> (a b s) (c g d)" if len(pr.shape) == 6 else "a b s h d -> (a b s) (h d)"
                for t in range(2):
                    store(pr.rearrange(fl)[128 * t:128 * t + 128], proj[:, t, p0:p0 + w])
                store(sa.rearrange(fl), proj[0:NS, 2, p0:p0 + w])
            for t in range(2):
                store(wp[256 + 128 * t:384 + 128 * t], proj[:, t, P_WIN:P_WIN + 256])
            for b in range(NB):
                store(io["new_win_kv_sample"].rearrange("a b s c g d -> (a b) s (c g d)")[b, WIN - NT:WIN],
                      proj[NT * b:NT * b + NT, 2, P_WIN:P_WIN + 256])
            sp.wait_ge(stored, n_stored)
            for b in range(NB):
                for h in range(8):
                    load(sp, "gS", gS[64 * (b % 2) + 8 * h:64 * (b % 2) + 8 * h + 8, b // 2, :],
                         gate_dram[NT * b:NT * b + NT, 3 * h:3 * h + 3])
            sync_attention(sp, False)

        @block.gpsimd
        def _(pool):
            st = Steps(pool, pool_own)
            for v in (bd_raw, bd_rot, bd_dif, proj[64:128, 2], qraw[64:128, 2], qrot[64:128, 2], qdif[64:128, 2]):
                st(nc.gpsimd.memset(v, 0.0))
                st.own()
            nc.gpsimd.memset(zero, 0.0).then_inc(zeroed, 1)
            for k, s in enumerate(primed):
                nc.gpsimd.memset(primer[:, k:k + 1], 0.0).then_inc(s, 1)
            pool.wait_ge(zeroed, 1)
            pool_attention(pool, st)

        @block.tensor
        def _(pe):
            def tp(n, items):
                if n >= 2:
                    pe.wait_ge(tp_out[n % 2], n // 2)
                for src, col in items:
                    r, c = src.shape[0], src.free_size()
                    last = nc.tensor.transpose(bank(n % 2)[0:c, col:col + r], src, ident[0:r, 0:r])
                last.then_inc(tp_full, 1)

            arrived(pe, "const")
            for t in range(3):
                r = ROWS[t]
                pe.wait_ge(xn_ready, 2 * t + 2)
                for half in range(2):
                    tp(2 * t + half, [(xin[0:r, t, 128 * (4 * half + k):128 * (4 * half + k) + 128], r * k) for k in range(4)])
            out_done(pe, G_PE - 1)
            pe_projection(pe, PAIRS[0:3], 0)
            arrived(pe, "small")
            tp(G_PE, [(peraw[0:CB, :], 0)])

            for n, (t, what) in enumerate(qk_groups):
                r = ROWS[t]
                if n == 0:
                    pe.wait_ge(pj_out[0], 9)
                    pe.wait_ge(pj_out[1], 9)
                pe.wait_ge(roped, {"raw": 0, "rot": 1, "dif": 4, "kd": 5, "kc": 3}[what])
                src = {"raw": qraw[0:r, t], "rot": qrot[0:r, t], "dif": qdif[0:r, t], "kd": proj[0:r, t, P_KD:P_KD + 512]}
                if what == "kc":
                    cols = [P_SEL, P_WIN] + ([P_CMP, P_CMP + 128] if t < 2 else [])
                    tp(G_QK + n, [(proj[0:r, t, c:c + 128], r * k) for k, c in enumerate(cols)])
                else:
                    tp(G_QK + n, [(src[what][:, 128 * k:128 * k + 128], r * k) for k in range(4)])

            def scores(u):
                kind, t, g = UNITS[u]
                if u >= 2:
                    pe.wait_ge(s_read, u - 1)
                nk = unit_keys(u)
                b0 = 512 * (2 + 2 * (u % 2))
                for m in range(4):
                    out = PS[:, b0 + 256 * m:b0 + 256 * m + nk]
                    if kind == "dif":
                        h, c = 2 * g + m % 2, m // 2
                        q, k = qTd[64 * c:64 * c + 64, h], kdnT[64 * c:64 * c + 64, h, 0:nk]
                    else:
                        q = (qTraw if kind == "cmp" else qTrot)[64 * g:64 * g + 64, m]
                        k = {"sel": ksT, "win": kwT, "cmp": kcT.rearrange("p b n -> p (b n)")}[kind][64 * g:64 * g + 64, 0:nk]
                    last = nc.tensor.matmul(out, q[:, 128 * t:128 * t + 128], k, start=True, stop=True)
                last.then_inc(s_full, 1)

            def probs_t(u):
                nk, e0 = unit_keys(u), 1024 * (u % 2)
                pe.wait_ge(e_ready, u + 1)
                for j in range(unit_groups(u)):
                    w = min(128, nk)
                    tp(G_UNIT[u] + j, [(ebuf[:, e0 + m * nk + 128 * j:e0 + m * nk + 128 * j + w], 128 * m) for m in range(4)])

            def values(u):
                kind, t, g = UNITS[u]
                out_done(pe, G_UNIT[u + 1] - 1)
                if u >= 2:
                    pe.wait_ge(pv_read, u - 1)
                ng, dv = unit_groups(u), 128 if kind == "dif" else 64
                rows = NCP if kind == "cmp" else 128
                for m in range(4):
                    for j in range(ng):
                        p0 = 1024 * (u % 2) + 512 * j + 128 * m
                        if kind == "cmp":
                            v = vc[0:NCP, 0, 64 * g:64 * g + 64]
                        elif kind == "dif":
                            h = 2 * g + m % 2
                            v = proj[:, j, P_VD + 128 * h:P_VD + 128 * h + 128]
                        else:
                            base = (P_SEL if kind == "sel" else P_WIN) + 128 + 64 * g
                            v = proj[:, j, base:base + 64]
                        last = nc.tensor.matmul(bank(6 + u % 2)[:, dv * m:dv * m + dv], ptb[0:rows, p0:p0 + 128], v,
                                                start=(j == 0), stop=(j == ng - 1))
                last.then_inc(pv_full, 1)

            def hidden(c):
                for l in range(CB // 2):
                    for k, rows in enumerate((pcT[:, c, 0, l:l + CS // 2 * (NCP - 1) + 1:CS // 2],
                                              pcT[:, c, 1, l:l + CS // 2 * (NCP - 1) + 1:CS // 2],
                                              peT[:, c * (CB // 2) + l:c * (CB // 2) + l + 1])):
                        last = nc.tensor.matmul(bank(7)[32 * k:32 * k + rows.free_size(), 128 * c:128 * c + 128], rows, w1[:, c, l, :],
                                                start=(l == 0), stop=(l == CB // 2 - 1))
                last.then_inc(ph_full, 1)

            def hidden_t():
                pe.wait_ge(ph_out, 1)
                for c in range(2):
                    for k, n in ((0, NCP), (1, NCP), (2, 1)):
                        col = 256 + 48 * c + 16 * k
                        last = nc.tensor.transpose(bank(7)[:, col:col + n], hrows[0:n, k, 128 * c:128 * c + 128],
                                                   ident[0:n, 0:n])
                last.then_inc(ph_full, 1)

            def compressed():
                pe.wait_ge(ph_out, 2)
                for g in range(2):
                    nc.tensor.matmul(bank(7)[64 * g:64 * g + 64, 352:352 + NCP], w2[:, 0, :], hid[:, 0, g, 0:NCP], start=True, stop=True)
                for g in range(2):
                    last = nc.tensor.matmul(bank(7)[0:NCP, 368 + 64 * g:432 + 64 * g], hid[:, 1, g, 0:NCP], w2[:, 1, :], start=True, stop=True)
                last.then_inc(pkv_full, 1)

            out_done(pe, G_QK + 14)
            n = len(UNITS)
            for s in range(n + 2):
                if s < n:
                    scores(s)
                if s == 0:
                    arrived(pe, "w1")
                    hidden(0)
                if s == 3:
                    compressed()
                if 1 <= s <= n:
                    probs_t(s - 1)
                if s == 1:
                    hidden(1)
                if s == 3:
                    pe.wait_ge(pkv_out, 1)
                if s >= 2:
                    values(s - 2)
                if s == 2:
                    hidden_t()
            pe.wait_ge(od_ready, 1)
            for t in range(2):
                tp(G_OUT + 2 * t, [(ons[:, t, 128 * k:128 * k + 128], 128 * k) for k in range(4)])
                tp(G_OUT + 2 * t + 1, [(ods[:, t, k, :], 128 * k) for k in range(4)])
            pe_attention(pe)

        def projection_out(eng, st, q, which, copy):
            for s in range(2):
                j = PAIRS[q][s]
                eng.wait_ge(pj_full, 5 * (q % 3) + 2 * s + which + 1)
                place(copy, st, j, which, bank(proj_bank(q, 2 * s + which)), 128, which)
            eng.wait_ge(pj_full, 5 * (q % 3) + 5)
            place(copy, st, PAIRS[q][which], 2, bank(proj_bank(q, 4))[64 * which:64 * which + 64], 64, which)

        def place(copy, st, j, t, src, r, which):
            w = CHUNKS[j][1]
            src = src[:, 0:w]
            if j == 0:
                dst = qraw[0:r, t].rearrange("p (r g d) -> p r g d", r=4, g=2)
                src = src.rearrange("p (g r d) -> p r g d", r=4, g=2)
            elif j == 3:
                dst = qdif[0:r, t]
            else:
                off = {1: P_CMP, 2: P_WIN, 4: P_KD, 5: P_VD}[j]
                dst = proj[0:r, t, off:off + w]
            st(copy(dst, src), pj_out[which])

        def qk_out(st, n, which, copy):
            t, what = qk_groups[n]
            g, r = G_QK + n, ROWS[t]
            src = bank(g % 2)[:, 0:4 * r].rearrange("p (k n) -> p k n", k=4)
            if what == "kc":
                parts = [(ksT[:, 128 * t:128 * t + r], src[:, 0]), (kwT[:, 128 * t:128 * t + r], src[:, 1])]
                if t < 2:
                    for gg in range(2):
                        for odd in range(2):
                            parts.append((pcT[64 * odd:64 * odd + 64, :, gg, 64 * t:64 * t + 64],
                                          src[64 * gg:64 * gg + 64, 2:4, odd:r:2]))
            elif what == "kd":
                parts = [(kdnT[:, :, 128 * t:128 * t + r], src)]
            elif t < 2:
                parts = [({"raw": qTraw, "rot": qTrot, "dif": qTd}[what][:, :, 128 * t:128 * t + r], src)]
            elif what == "dif":
                parts = []
                for c in range(2):
                    d = bd_dif[64 * c:64 * c + 64].rearrange("p b (h x) -> p h b x", h=4)[:, :, :, 8 * c:8 * c + 8]
                    parts.append((d, src[64 * c:64 * c + 64].rearrange("p h (b t) -> p h b t", b=NB)))
            else:
                parts = []
                for gg in range(2):
                    d = (bd_raw if what == "raw" else bd_rot)[64 * gg:64 * gg + 64, :, 32 * gg:32 * gg + 32]
                    parts.append((d.rearrange("p b (r t) -> p r b t", r=4),
                                  src[64 * gg:64 * gg + 64].rearrange("p r (b t) -> p r b t", b=NB)))
            for k, (d, s) in enumerate(parts):
                st(copy(d, s), tp_out[which] if k == len(parts) - 1 else None)

        def prompt_evac(eng, st, u, which, copy):
            if u >= 2:
                eng.wait_ge(pv_full, u - 1)
            for j in range(unit_groups(u)):
                g = G_UNIT[u] + j
                if g % 2 == which:
                    eng.wait_ge(tp_full, g + 1)
                    rows = min(128, unit_keys(u))
                    p0 = 1024 * (u % 2) + 512 * j
                    st(copy(ptb[0:rows, p0:p0 + 512], bank(g % 2)[0:rows, :]), tp_out[which])

        def prompt_out(st, g, t, k, which):
            src = bank(g % 2).rearrange("p (k n) -> p k n", k=4)
            dst = (onT if k == 0 else odT)[:, :, 128 * t:128 * t + 128]
            if k == 0:
                ins = nc.scalar.activation(dst, src, ACT.Copy) if which == 0 else nc.vector.tensor_copy(dst, src)
            else:
                ins = (nc.scalar.activation(dst, src, ACT.Copy, scale=sg) if which == 0
                       else nc.vector.tensor_scalar(dst, src, sg, None, ALU.mult))
            st(ins, tp_out[which])

        @block.scalar
        def _(act):
            st = Steps(act, act_own)
            copy = lambda d, s: nc.scalar.activation(d, s, ACT.Copy)
            def root(v):
                n = st.n.get("root_ready", 0) + 1
                act.wait_ge(var_ready, n)
                st(nc.scalar.activation(v, v, ACT.Sqrt), root_ready)

            for t in range(3):
                arrived(act, f"x{t}")
                st(nc.scalar.activation(at(31232 + 1024 * t, 1024)[0:ROWS[t]], xin[0:ROWS[t], t, :], ACT.Square,
                                        accum_out=ssq[0:ROWS[t], t:t + 1]), squares)
            arrived(act, "const")
            for n in (0, 2, 4):
                t, r = n // 2, ROWS[n // 2]
                root(ssq[0:r, 3 + t:4 + t])
                act.wait_ge(tp_full, n + 1)
                for k in range(4):
                    st(nc.scalar.activation(xnT[:, k, 128 * t:128 * t + r], bank(0)[:, r * k:r * k + r], ACT.Copy,
                                            scale=gmix[:, k:k + 1]), tp_out[0] if k == 3 else None)
            act.wait_ge(pool_own, 7)
            for q in range(3):
                projection_out(act, st, q, 0, copy)
                if q == 1:
                    act.wait_ge(pj_out[0], 6)
                    act.wait_ge(pj_out[1], 6)
                    nc.scalar.activation(gates, proj[:, :, P_GN:P_GN + 24], ACT.Sigmoid).then_inc(gates_ready, 1)
            act.wait_ge(tp_full, G_PE + 1)
            st(copy(peT, bank(0)[:, 0:CB]), tp_out[0])
            for n in range(15):
                if (G_QK + n) % 2 == 0:
                    act.wait_ge(tp_full, G_QK + n + 1)
                    qk_out(st, n, 0, copy)
            act.wait_ge(lam_sums, 1)
            nc.scalar.activation(lam[:, 2:4], lam[:, 0:2], ACT.Exp).then_inc(lam_exp, 1)
            def compress():
                act.wait_ge(ph_full, 3)
                hT = bank(7)[:, 256:352].rearrange("p (c k n) -> p c k n", c=2, n=16)
                st(copy(hb, hT[:, :, 2, 0]))
                st.own()
                for c in range(2):
                    last = nc.scalar.activation(hid[:, c, :, 0:NCP], hT[:, c, 0:2, 0:NCP], ACT.Gelu_apprx_tanh, bias=hb[:, c:c + 1])
                st(last, ph_out)
                act.wait_ge(pkv_full, 1)
                st(copy(kcT.rearrange("p b n -> p (b n)")[:, 0:NCP], bank(7)[:, 352:352 + NCP]))
                st(copy(vc[0:NCP, 0, :], bank(7)[0:NCP, 368:496]), pkv_out)

            n = len(UNITS)
            for s in range(n + 1):
                if s == 2:
                    act.wait_ge(ph_full, 2)
                    for k, rows in ((0, NCP), (1, NCP), (2, 1)):
                        st(copy(hrows[0:rows, k], bank(7)[32 * k:32 * k + rows, 0:256]), ph_out if k == 2 else None)
                if s == 3:
                    compress()
                if s >= 1:
                    prompt_evac(act, st, s - 1, 0, copy)
                if s < n:
                    nk, e0 = unit_keys(s), 1024 * (s % 2)
                    act.wait_ge(nmx_ready, s + 1)
                    if s >= 4:
                        act.wait_ge(pv_read, s - 3)
                    for m in range(4):
                        e = ebuf[:, e0 + m * nk:e0 + (m + 1) * nk]
                        st(nc.scalar.activation(e, e, ACT.Exp, bias=nmx[:, s % 2, m:m + 1], scale=SCALE,
                                                accum_out=sm[:, s % 4, m:m + 1]), e_ready if m == 3 else None)
            root(ssq)
            for t in range(2):
                for k in range(2):
                    g = G_OUT + 2 * t + k
                    if g % 2 == 0:
                        act.wait_ge(tp_full, g + 1)
                        prompt_out(st, g, t, k, 0)
            act_attention(act, st)

        @block.vector
        def _(dve):
            st = Steps(dve, dve_own)
            V = nc.vector

            def rstd(dst, src, n):
                st(V.tensor_scalar(dst, src, 1.0 / n, EPS, ALU.mult, ALU.add), var_ready)
                dve.wait_ge(root_ready, st.n["var_ready"])
                st(V.reciprocal(dst, dst))
                st.own()

            for t in range(3):
                r = ROWS[t]
                dve.wait_ge(squares, t + 1)
                rstd(ssq[0:r, 3 + t:4 + t], ssq[0:r, t:t + 1], D)
                for half in range(2):
                    v = xin[0:r, t, 512 * half:512 * half + 512]
                    st(V.tensor_scalar(v, v, ssq[0:r, 3 + t:4 + t], None, ALU.mult), xn_ready)
                n = 2 * t + 1
                if t == 0:
                    arrived(dve, "const")
                dve.wait_ge(tp_full, n + 1)
                st(V.tensor_tensor(xnT[:, 4:8, 128 * t:128 * t + r], bank(1)[:, 0:4 * r].rearrange("p (k n) -> p k n", k=4),
                                   gmix[:, 4:8].unsqueeze(2).to_broadcast([128, 4, r]), ALU.mult), tp_out[1])
            arrived(dve, "small")
            l4 = dl.rearrange("p (a b d) -> p a b d", a=2, b=2)
            st(V.tensor_tensor(l4[:, :, 0], l4[:, :, 0], l4[:, :, 1], ALU.mult))
            st.own()
            st(V.reduce_sum(lam[:, 0:2], l4[:, :, 0], AX), lam_sums)
            arrived(dve, "small")
            st(V.tensor_scalar(sg, sg, 1.0 - LAMBDA0, None, ALU.mult))
            dve.wait_ge(pool_own, 7)
            copy = V.tensor_copy

            def rope(src, dst, nh):
                x1, x2 = src[:, :, :, 0:8], src[:, :, :, 8:16]
                cos = const("cos", 3, 8).unsqueeze(2).to_broadcast([128, 3, nh, 8])
                sin = const("sin", 3, 8).unsqueeze(2).to_broadcast([128, 3, nh, 8])
                tmp = [v[:, 0:24 * nh].rearrange("p (t h d) -> p t h d", t=3, h=nh) for v in ropet]
                for d, a, b in ((tmp[0], x1, cos), (tmp[1], x2, sin), (tmp[2], x1, sin), (tmp[3], x2, cos)):
                    st(V.tensor_tensor(d, a, b, ALU.mult))
                st.own()
                st(V.tensor_tensor(dst[:, :, :, 0:8], tmp[0], tmp[1], ALU.subtract))
                st(V.tensor_tensor(dst[:, :, :, 8:16], tmp[2], tmp[3], ALU.add), roped)
                st.own()

            heads = lambda v: v.rearrange("p t (h d) -> p t h d", d=HD)
            projection_out(dve, st, 0, 1, copy)
            dve.wait_ge(pj_out[0], 3)
            st.own()
            st(copy(qrot, qraw))
            st.own()
            rope(heads(qraw), heads(qrot), 8)
            rope(heads(proj[:, :, P_SEL:P_SEL + 128]), heads(proj[:, :, P_SEL:P_SEL + 128]), 2)
            projection_out(dve, st, 1, 1, copy)
            dve.wait_ge(pj_out[0], 6)
            st.own()
            rope(heads(proj[:, :, P_WIN:P_WIN + 128]), heads(proj[:, :, P_WIN:P_WIN + 128]), 2)
            rope(heads(qdif), heads(qdif), 8)
            projection_out(dve, st, 2, 1, copy)
            dve.wait_ge(pj_out[0], 9)
            st.own()
            rope(heads(proj[:, :, P_KD:P_KD + 512]), heads(proj[:, :, P_KD:P_KD + 512]), 8)
            for n in range(15):
                if (G_QK + n) % 2 == 1:
                    dve.wait_ge(tp_full, G_QK + n + 1)
                    qk_out(st, n, 1, copy)
            dve.wait_ge(lam_exp, 1)
            st(V.tensor_tensor(lam[:, 4:5], lam[:, 3:4], lam[:, 2:3], ALU.subtract))
            st.own()
            st(V.tensor_scalar(lam[:, 4:5], lam[:, 4:5], LAMBDA0, None, ALU.subtract))
            st(V.memset(lv[:, 0:2], 1.0))
            st.own()
            st(V.tensor_copy(lv[:, 2:4], lam[:, 4:5].to_broadcast([128, 2])))
            st(V.scalar_tensor_tensor(cmat, const("c1"), lam[:, 4:5], const("c0"), ALU.mult, ALU.add), lam_done)

            def masked(u):
                kind, t, g = UNITS[u]
                nk, e0, b0 = unit_keys(u), 1024 * (u % 2), 512 * (2 + 2 * (u % 2))
                dve.wait_ge(s_full, u + 1)
                if u >= 2:
                    dve.wait_ge(tp_full, G_UNIT[u - 1])
                m = (const("cmpm", 2, NCP) if kind == "cmp" else const("causal", 2, SEQ))[:, t, 0:nk]
                e = ebuf[:, e0:e0 + 4 * nk].rearrange("p (m k) -> p m k", m=4)
                s = PS[:, b0:b0 + 1024].rearrange("p (m k) -> p m k", m=4)[:, :, 0:nk]
                st(V.tensor_tensor(e, s, m.unsqueeze(1).to_broadcast([128, 4, nk]), ALU.add), s_read)
                st.own()
                st(V.reduce_max(mx[:, u % 2], e, AX))
                st.own()
                if u >= 2:
                    dve.wait_ge(e_ready, u - 1)
                st(V.tensor_scalar(nmx[:, u % 2], mx[:, u % 2], -SCALE, None, ALU.mult), nmx_ready)

            def combine(u):
                kind, t, g = UNITS[u]
                c = cf[:, u % 2]
                dve.wait_ge(pv_full, u + 1)
                st(V.reciprocal(c, sm[:, u % 4]))
                st.own()
                if kind == "dif":
                    st(V.tensor_tensor(c, c, lv, ALU.mult))
                else:
                    br = {"cmp": 0, "sel": 1, "win": 2}[kind]
                    st(V.tensor_tensor(c, c, gates[:, t, 12 * g:12 * g + 12].rearrange("p (r b) -> p r b", b=3)[:, :, br], ALU.mult))
                    if kind == "cmp":
                        st.own()
                        st(V.tensor_scalar(c, c, const("cmpv")[:, t:t + 1], None, ALU.mult))
                st.own()
                if kind == "dif":
                    pv = bank(6 + u % 2).rearrange("p (m e) -> p m e", m=4)
                    tm = pvt.rearrange("p (m e) -> p m e", m=4)
                    st(V.tensor_tensor(tm, pv, c.unsqueeze(2).to_broadcast([128, 4, 128]), ALU.mult), pv_read)
                    st.own()
                    st(V.tensor_tensor(ods[:, t, 2 * g:2 * g + 2, :], tm[:, 0:2], tm[:, 2:4], ALU.add))
                else:
                    pv = bank(6 + u % 2)[:, 0:256].rearrange("p (m e) -> p m e", m=4)
                    dst = ons[:, t, 256 * g:256 * g + 256].rearrange("p (m e) -> p m e", m=4)
                    out = dst if kind == "sel" else pvt[:, 0:256].rearrange("p (m e) -> p m e", m=4)
                    st(V.tensor_tensor(out, pv, c.unsqueeze(2).to_broadcast([128, 4, 64]), ALU.mult), pv_read)
                    if kind != "sel":
                        st.own()
                        st(V.tensor_tensor(dst, dst, out, ALU.add))
                st.own()

            dve.wait_ge(gates_ready, 1)
            dve.wait_ge(xn_stored, 16)
            n = len(UNITS)
            for s in range(n + 2):
                if s < n:
                    masked(s)
                if 1 <= s <= n:
                    prompt_evac(dve, st, s - 1, 1, copy)
                if s >= 2:
                    combine(s - 2)
            sq = at(24576, 1024)
            st(V.tensor_tensor(sq, ods.rearrange("p t h e -> p (t h e)"), ods.rearrange("p t h e -> p (t h e)"), ALU.mult))
            st.own()
            st(V.reduce_sum(ssq, sq.rearrange("p (a e) -> p a e", e=128), AX))
            st.own()
            rstd(ssq, ssq, 128)
            o8 = ods.rearrange("p t h e -> p (t h) e")
            st(V.tensor_tensor(o8, o8, ssq.unsqueeze(2).to_broadcast([128, 8, 128]), ALU.mult), od_ready)
            for t in range(2):
                for k in range(2):
                    g = G_OUT + 2 * t + k
                    if g % 2 == 1:
                        dve.wait_ge(tp_full, g + 1)
                        prompt_out(st, g, t, k, 1)
            dve_attention(dve, st)


_INS = ['x_prompt', 'x_sample', 'cache_cmp_kv', 'cache_sel_kv', 'state_win_kv', 'cache_diff_k', 'cache_diff_v',
        'page_table', 'norm_mix', 'w_in', 'cmp_pe', 'w_cmp1', 'w_cmp2', 'diff_lambda', 'diff_subln', 'w_br_nsa',
        'w_br_diff', 'w_out', 'norm_ffn', 'w_router', 'b_router', 'w_gate_up', 'b_gate_up', 'w_down', 'b_down',
        'norm_final']
_OUTS = [('y_prompt', (1, SEQ, D)), ('y_sample', (NB, NT, D)),
         ('new_cmp_kv_prompt', (1, 1, SEQ, 2, 2, HD)), ('new_cmp_kv_sample', (1, NB, NT, 2, 2, HD)),
         ('new_sel_kv_prompt', (1, 1, SEQ, 2, 2, HD)), ('new_sel_kv_sample', (1, NB, NT, 2, 2, HD)),
         ('new_win_kv_prompt', (1, 1, WIN, 2, 2, HD)), ('new_win_kv_sample', (1, NB, WIN, 2, 2, HD)),
         ('new_diff_k_prompt', (1, 1, SEQ, 4, 2, HD)), ('new_diff_k_sample', (1, NB, NT, 4, 2, HD)),
         ('new_diff_v_prompt', (1, 1, SEQ, 4, 128)), ('new_diff_v_sample', (1, NB, NT, 4, 128))]


def kernel(**inputs):
    import numpy as _np
    import concourse.bacc as _bacc
    from concourse import mybir as _mybir
    from concourse.bass_utils import run_bass_kernel_spmd as _run

    nc = _bacc.Bacc("TRN2", target_bir_lowering=False, num_devices=1)
    const_a, at_a, const_b, at_b = shape_constants()
    arrays, io = {}, {}
    for name in _INS:
        a = _np.ascontiguousarray(inputs[name])
        arrays["in_" + name] = a
        io[name] = nc.dram_tensor("in_" + name, a.shape, _mybir.dt.from_np(a.dtype), kind="ExternalInput").ap()
    for name, a in (("const_a", const_a), ("const_b", const_b)):
        arrays["in_" + name] = a
        io[name] = nc.dram_tensor("in_" + name, a.shape, _mybir.dt.from_np(a.dtype), kind="ExternalInput").ap()
    for name, shape in _OUTS:
        io[name] = nc.dram_tensor("out_" + name, shape, F32, kind="ExternalOutput").ap()
    build(nc, io, const_a, at_a, const_b, at_b)
    r = _run(nc, [arrays], core_ids=[0])
    return tuple(r.results[0]["out_" + name] for name, _ in _OUTS)
```
